# Optimizing a Trainium2 kernel written in Bass

```python
import jax, jax.numpy as jnp
from jax import lax
import numpy as np

D_MODEL = 1024
BATCH = 1
SEQ = 256
DEPTH = 2

CONV_WIDTH = 512
CONV_K = 3
MLA_HEADS = 8
MLA_NOPE = 64
MLA_ROPE = 32
MLA_V = 64
MLA_Q_RANK = 256
MLA_KV_RANK = 128
ROPE_THETA = 10000.0
SB_HEADS = 8
SB_HEAD_DIM = 64
SB_WIDTH = SB_HEADS * SB_HEAD_DIM
Q_BLOCK = 128
N_BRANCHES = 3
OFF_CONV = 0
OFF_CQ = OFF_CONV + 3 * CONV_WIDTH
OFF_CKV = OFF_CQ + MLA_Q_RANK
OFF_KR = OFF_CKV + MLA_KV_RANK
OFF_SB = OFF_KR + MLA_ROPE
OFF_GATE = OFF_SB + 3 * SB_WIDTH
IN_COLS = OFF_GATE + N_BRANCHES * D_MODEL
N_GROUPS = 4
EXPERTS_PER_GROUP = 8
N_EXPERTS = N_GROUPS * EXPERTS_PER_GROUP
TOP_K_IN_GROUP = 2
D_EXPERT = 256
EPS = 1e-6

kernel_name = "hybrid_conv_mla_stickbreak_hiermoe"

def rms_norm(x, g):
    xf = x.astype(jnp.float32)
    y = xf * lax.rsqrt(jnp.mean(xf * xf, axis=-1, keepdims=True) + EPS)
    return (y * g.astype(jnp.float32)).astype(x.dtype)

def apply_rope(x, positions):
    half = x.shape[-1] // 2
    freqs = ROPE_THETA ** (-jnp.arange(half, dtype=jnp.float32) / half)
    ang = positions.astype(jnp.float32)[..., None] * freqs
    ang = ang.reshape(ang.shape[:2] + (1,) * (x.ndim - 3) + (half,))
    cos, sin = jnp.cos(ang), jnp.sin(ang)
    xf = x.astype(jnp.float32)
    x1, x2 = xf[..., :half], xf[..., half:]
    out = jnp.concatenate([x1 * cos - x2 * sin, x2 * cos + x1 * sin], axis=-1)
    return out.astype(x.dtype)

def short_conv_mixer(h_c, b_g, c_g, conv_w, w_out):
    u = c_g * h_c
    y = lax.conv_general_dilated(
        u, conv_w[:, None, :].astype(u.dtype), window_strides=(1,),
        padding=[(CONV_K - 1, 0)], dimension_numbers=("NWC", "WIO", "NWC"),
        feature_group_count=CONV_WIDTH)
    return (b_g * y) @ w_out

def mla_mixer(c_q, c_kv, k_rope, positions, q_norm, kv_norm, w_uq, w_ukv, w_out):
    B, S, _ = c_q.shape
    q = (rms_norm(c_q, q_norm) @ w_uq).reshape(B, S, MLA_HEADS, MLA_NOPE + MLA_ROPE)
    q_nope = q[..., :MLA_NOPE]
    q_rope = apply_rope(q[..., MLA_NOPE:], positions)
    kv = (rms_norm(c_kv, kv_norm) @ w_ukv).reshape(B, S, MLA_HEADS, MLA_NOPE + MLA_V)
    k_nope, v = kv[..., :MLA_NOPE], kv[..., MLA_NOPE:]
    k_rope = apply_rope(k_rope, positions)
    scale = (MLA_NOPE + MLA_ROPE) ** -0.5
    outs = []
    for i in range(S // Q_BLOCK):
        t0, kend = i * Q_BLOCK, (i + 1) * Q_BLOCK
        s = jnp.einsum("bqhd,bkhd->bhqk", q_nope[:, t0:kend], k_nope[:, :kend],
                       preferred_element_type=jnp.float32)
        s = s + jnp.einsum("bqhr,bkr->bhqk", q_rope[:, t0:kend], k_rope[:, :kend],
                           preferred_element_type=jnp.float32)
        mask = (t0 + jnp.arange(Q_BLOCK))[:, None] >= jnp.arange(kend)[None, :]
        s = jnp.where(mask, s * scale, -jnp.inf)
        p = jax.nn.softmax(s, axis=-1).astype(v.dtype)
        outs.append(jnp.einsum("bhqk,bkhd->bqhd", p, v[:, :kend]))
    o = jnp.concatenate(outs, axis=1).reshape(B, S, MLA_HEADS * MLA_V)
    return o @ w_out

def stick_breaking_mixer(q, k, v, w_out):
    B, S, _ = q.shape
    q = q.reshape(B, S, SB_HEADS, SB_HEAD_DIM)
    k = k.reshape(B, S, SB_HEADS, SB_HEAD_DIM)
    v = v.reshape(B, S, SB_HEADS, SB_HEAD_DIM)
    scale = SB_HEAD_DIM ** -0.5
    outs = []
    for i in range(S // Q_BLOCK):
        t0, kend = i * Q_BLOCK, (i + 1) * Q_BLOCK
        z = jnp.einsum("bqhd,bkhd->bhqk", q[:, t0:kend], k[:, :kend],
                       preferred_element_type=jnp.float32) * scale
        mask = (t0 + jnp.arange(Q_BLOCK))[:, None] > jnp.arange(kend)[None, :]
        log_1m = jnp.where(mask, jax.nn.log_sigmoid(-z), 0.0)
        suffix = lax.cumsum(log_1m, axis=3, reverse=True) - log_1m
        a = jnp.where(mask, jnp.exp(jax.nn.log_sigmoid(z) + suffix), 0.0)
        outs.append(jnp.einsum("bhqk,bkhd->bqhd", a.astype(v.dtype), v[:, :kend]))
    o = jnp.concatenate(outs, axis=1).reshape(B, S, SB_WIDTH)
    return o @ w_out

def hierarchical_moe(h, w_rg, b_rg, w_re, b_re, w_g, w_u, w_d):
    B, S, D = h.shape
    hf = h.reshape(B * S, D)
    g_prob = jax.nn.softmax((hf @ w_rg).astype(jnp.float32) + b_rg.astype(jnp.float32), axis=-1)
    g_w, g_idx = lax.top_k(g_prob, 1)
    e_logits = ((hf @ w_re).astype(jnp.float32) + b_re.astype(jnp.float32)).reshape(
        B * S, N_GROUPS, EXPERTS_PER_GROUP)
    e_sel = jnp.einsum("nge,ng->ne", e_logits,
                       jax.nn.one_hot(g_idx[:, 0], N_GROUPS, dtype=jnp.float32))
    e_w, e_idx = lax.top_k(jax.nn.softmax(e_sel, axis=-1), TOP_K_IN_GROUP)
    e_w = e_w / jnp.sum(e_w, axis=-1, keepdims=True)
    weights = g_w * e_w
    expert_id = g_idx * EXPERTS_PER_GROUP + e_idx
    combine = jnp.sum(jax.nn.one_hot(expert_id, N_EXPERTS, dtype=jnp.float32)
                      * weights[..., None], axis=1).astype(hf.dtype)
    out = jnp.zeros_like(hf)
    for e in range(N_EXPERTS):
        act = jax.nn.silu(hf @ w_g[e]) * (hf @ w_u[e])
        out = out + combine[:, e:e + 1] * (act @ w_d[e])
    return out.reshape(B, S, D)

def hybrid_layer(x, positions, attn_norm, w_in, b_gate, conv_w, w_out_conv, q_norm, kv_norm,
                 w_uq, w_ukv, w_out_mla, w_out_sb, w_o, ffn_norm, w_router_group,
                 b_router_group, w_router_expert, b_router_expert, w_exp_gate, w_exp_up,
                 w_exp_down):
    B, S, D = x.shape
    h = rms_norm(x, attn_norm)
    proj = h @ w_in
    h_c = proj[..., OFF_CONV:OFF_CONV + CONV_WIDTH]
    b_g = proj[..., OFF_CONV + CONV_WIDTH:OFF_CONV + 2 * CONV_WIDTH]
    c_g = proj[..., OFF_CONV + 2 * CONV_WIDTH:OFF_CQ]
    c_q = proj[..., OFF_CQ:OFF_CKV]
    c_kv = proj[..., OFF_CKV:OFF_KR]
    k_r = proj[..., OFF_KR:OFF_SB]
    q_sb = proj[..., OFF_SB:OFF_SB + SB_WIDTH]
    k_sb = proj[..., OFF_SB + SB_WIDTH:OFF_SB + 2 * SB_WIDTH]
    v_sb = proj[..., OFF_SB + 2 * SB_WIDTH:OFF_GATE]
    gates = jax.nn.sigmoid((proj[..., OFF_GATE:] + b_gate).astype(jnp.float32))
    gates = gates.astype(x.dtype).reshape(B, S, N_BRANCHES, D)

    y_a = short_conv_mixer(h_c, b_g, c_g, conv_w, w_out_conv)
    y_b = mla_mixer(c_q, c_kv, k_r, positions, q_norm, kv_norm, w_uq, w_ukv, w_out_mla)
    y_c = stick_breaking_mixer(q_sb, k_sb, v_sb, w_out_sb)
    merged = gates[:, :, 0] * y_a + gates[:, :, 1] * y_b + gates[:, :, 2] * y_c
    x = x + merged @ w_o

    h2 = rms_norm(x, ffn_norm)
    x = x + hierarchical_moe(h2, w_router_group, b_router_group, w_router_expert,
                             b_router_expert, w_exp_gate, w_exp_up, w_exp_down)
    return x

def setup_inputs(seed: int = 0) -> dict:
    key = jax.random.key(seed)
    ks = jax.random.split(key, 24)
    f32 = jnp.float32

    def nrm(k, shape, fan_in):
        return jax.random.normal(k, shape, f32) * (fan_in ** -0.5)

    def gain(k, shape):
        return 1.0 + 0.02 * jax.random.normal(k, shape, f32)

    x = jax.random.normal(ks[0], (BATCH, SEQ, D_MODEL), f32)
    offsets = jax.random.randint(ks[1], (BATCH, 1), 0, 4096, dtype=jnp.int32)
    positions = offsets + jnp.arange(SEQ, dtype=jnp.int32)[None, :]
    return {
        "x": x,
        "positions": positions,
        "attn_norm": gain(ks[2], (DEPTH, D_MODEL)),
        "w_in": nrm(ks[3], (DEPTH, D_MODEL, IN_COLS), D_MODEL),
        "b_gate": 0.02 * jax.random.normal(ks[4], (DEPTH, N_BRANCHES * D_MODEL), f32),
        "conv_w": nrm(ks[5], (DEPTH, CONV_K, CONV_WIDTH), CONV_K),
        "w_out_conv": nrm(ks[6], (DEPTH, CONV_WIDTH, D_MODEL), CONV_WIDTH),
        "q_norm": gain(ks[7], (DEPTH, MLA_Q_RANK)),
        "kv_norm": gain(ks[8], (DEPTH, MLA_KV_RANK)),
        "w_uq": nrm(ks[9], (DEPTH, MLA_Q_RANK, MLA_HEADS * (MLA_NOPE + MLA_ROPE)), MLA_Q_RANK),
        "w_ukv": nrm(ks[10], (DEPTH, MLA_KV_RANK, MLA_HEADS * (MLA_NOPE + MLA_V)), MLA_KV_RANK),
        "w_out_mla": nrm(ks[11], (DEPTH, MLA_HEADS * MLA_V, D_MODEL), MLA_HEADS * MLA_V),
        "w_out_sb": nrm(ks[12], (DEPTH, SB_WIDTH, D_MODEL), SB_WIDTH),
        "w_o": nrm(ks[13], (DEPTH, D_MODEL, D_MODEL), D_MODEL),
        "ffn_norm": gain(ks[14], (DEPTH, D_MODEL)),
        "w_router_group": nrm(ks[15], (DEPTH, D_MODEL, N_GROUPS), D_MODEL),
        "b_router_group": 0.01 * jax.random.normal(ks[16], (DEPTH, N_GROUPS), f32),
        "w_router_expert": nrm(ks[17], (DEPTH, D_MODEL, N_EXPERTS), D_MODEL),
        "b_router_expert": 0.01 * jax.random.normal(ks[18], (DEPTH, N_EXPERTS), f32),
        "w_exp_gate": nrm(ks[19], (DEPTH, N_EXPERTS, D_MODEL, D_EXPERT), D_MODEL),
        "w_exp_up": nrm(ks[20], (DEPTH, N_EXPERTS, D_MODEL, D_EXPERT), D_MODEL),
        "w_exp_down": nrm(ks[21], (DEPTH, N_EXPERTS, D_EXPERT, D_MODEL), D_EXPERT),
        "final_norm": gain(ks[22], (D_MODEL,)),
    }

def reference(x, positions, attn_norm, w_in, b_gate, conv_w, w_out_conv, q_norm, kv_norm,
              w_uq, w_ukv, w_out_mla, w_out_sb, w_o, ffn_norm, w_router_group,
              b_router_group, w_router_expert, b_router_expert, w_exp_gate, w_exp_up,
              w_exp_down, final_norm):
    for l in range(DEPTH):
        x = hybrid_layer(x, positions, attn_norm[l], w_in[l], b_gate[l], conv_w[l],
                         w_out_conv[l], q_norm[l], kv_norm[l], w_uq[l], w_ukv[l],
                         w_out_mla[l], w_out_sb[l], w_o[l], ffn_norm[l], w_router_group[l],
                         b_router_group[l], w_router_expert[l], b_router_expert[l],
                         w_exp_gate[l], w_exp_up[l], w_exp_down[l])
    return rms_norm(x, final_norm)


_drawn_inputs = setup_inputs


def setup_inputs(seed=0):
    import zlib

    import numpy as np

    out = dict(_drawn_inputs(seed))
    spreads = {}
    factors = {'b_gate': 3.22,
     'q_norm': 4.971,
     'kv_norm': 4.221,
     'b_router_group': 14.88,
     'b_router_expert': 2.678,
     'final_norm': 7.974}
    for name, (base, spread) in spreads.items():
        noise = np.random.default_rng([zlib.crc32(name.encode()), seed]).standard_normal(out[name].shape)
        drawn = base * np.exp(spread * noise) if base else spread * noise
        out[name] = __import__('jax').numpy.asarray(drawn.astype(out[name].dtype))
    for name, factor in factors.items():
        out[name] = (out[name] * factor).astype(out[name].dtype)
    return out
```

```python
from contextlib import ExitStack

import numpy as np

import concourse.bass as bass
from concourse import mybir

F32 = mybir.dt.float32
I32 = mybir.dt.int32
ALU = mybir.AluOpType
ACT = mybir.ActivationFunctionType
AX = mybir.AxisListType

P = 128
D = 1024
T = 256
TT = T // P
DC = D // P
DEPTH = 2
CW = 512
CB = CW // P
H = 8
NOPE, ROPE, VD = 64, 32, 64
QK = NOPE + ROPE
HALF = ROPE // 2
QR, KVR = 256, 128
SBD = 64
LAT = QR + KVR + ROPE
OFF_HC, OFF_BG, OFF_CG = 0, CW, 2 * CW
OFF_LAT = 3 * CW
OFF_SB = OFF_LAT + LAT
OFF_GATE = OFF_SB + 3 * CW
IN_COLS = OFF_GATE + 3 * D
NG, EPG = 4, 8
E = NG * EPG
FE = 256
FC = FE // P
SLOTS = 64
PAIRS = E // 2
OCTS = E // 8
EPS = 1e-6
NEG = -1e30
AREA = 21700
RING = 5
MAGIC = 1.5 * 2.0 ** 23
TWO_PI = 2.0 * np.pi
C1 = 6.28125
C2 = float(np.float32(np.floor((TWO_PI - C1) * 2 ** 22) / 2 ** 22))
C3 = float(np.float32(TWO_PI - C1 - C2))
PI_LOW = 3.1415925

INS = ["x", "positions", "attn_norm", "w_in", "b_gate", "conv_w", "w_out_conv", "q_norm", "kv_norm",
       "w_uq", "w_ukv", "w_out_mla", "w_out_sb", "w_o", "ffn_norm", "w_router_group",
       "b_router_group", "w_router_expert", "b_router_expert", "w_exp_gate", "w_exp_up",
       "w_exp_down", "final_norm"]


class Plan:

    def __init__(self):
        self.jobs = {}
        self.n = 0
        self.freed = {"dve": 0, "act": 0}
        self.last = [None] * 8
        self.at = 0

    def add(self, key, by, banks=8):
        bank = self.at % banks
        self.at += 1
        self.place(key, by, bank)

    def place(self, key, by, bank, before=None):
        self.n += 1
        self.freed[by] += 1
        self.jobs[key] = (self.n, bank, by, self.freed[by], before if before else self.last[bank])
        self.last[bank] = key


def place_of(h):
    return (h % 2) * (H // 2) + h // 2


def head_at(place):
    return 2 * (place % (H // 2)) + place // (H // 2)


def make_plan():
    p = Plan()
    for l in range(DEPTH):
        for j in range(4):
            p.add(("tr", l, j), "dve" if j % 2 == 0 else "act")
        for name, by in (("qs", "act"), ("ks", "act"), ("vs", "dve"), ("lat", "act")):
            for j in range(2):
                p.add((name, l, j), by)
        for j in range(6):
            p.add(("z", l, j), "act")
        for name, by in (("hc", "act"), ("bg", "act"), ("cg", "dve")):
            for j in range(2):
                p.add((name, l, j), by)
        for j in range(2):
            p.add(("latT", l, j), "dve")
        for j in range(6):
            p.add(("cum", l, j), "dve")
        for name in ("q", "kv"):
            for j in range(4):
                p.add((name, l, j), "act")
        for j in range(4):
            p.add(("gate", l, 0, j), "act")
            p.add(("y", l, 0, j), "dve")
        for j in range(4):
            p.add(("qT", l, j), "act")
        for j in range(4):
            p.add(("kT", l, j), "dve")
        for j in range(2):
            p.add(("pvs", l, j), "act")
        for j in range(6):
            p.add(("s", l, j), "dve")
        for j in range(4):
            p.add(("gate", l, 2, j), "act")
            p.add(("y", l, 2, j), "dve")
        for j in range(6):
            p.add(("pT", l, j), "dve" if j % 2 == 0 else "act")
        for j in range(2):
            p.add(("pvm", l, j), "act")
        for j in range(4):
            p.add(("gate", l, 1, j), "act")
            p.add(("y", l, 1, j), "dve")
        for j in range(4):
            p.add(("wo", l, j), "dve")
        for j in range(4):
            p.add(("tr2", l, j), "dve" if j % 2 == 0 else "act")
        p.add(("route", l), "dve")
        p.add(("rank", l), "dve")
        before = [p.last[4 + j] for j in range(4)]
        for o in range(OCTS):
            for c in range(DC):
                p.add(("gather", l, o, c), "dve" if c % 2 == 0 else "act", 4)
            for pr in range(4 * o, 4 * o + 4):
                p.add(("sT", l, pr), "act", 4)
                p.add(("gu", l, pr), "act", 4)
                p.add(("guT", l, pr), "dve", 4)
                p.add(("down", l, pr, 0), "act", 4)
                p.add(("down", l, pr, 1), "dve", 4)
        for j in range(4):
            p.place(("moe", l, j), "dve", 4 + j, before[j])
    return p


def unit_list():
    units = []
    for l in range(DEPTH):
        for name in ("qs", "ks", "vs", "lat", "hc", "bg", "cg"):
            units.append((name, l, 0))
        for b in (0, 2, 1):
            for i in range(2):
                units.append(("gate", l, 2 * b + i))
            units.append(("wy", l, b))
        units += [("wo", l, 0), ("wo", l, 1)]
        for pr in range(PAIRS):
            units += [("gu", l, 2 * pr), ("gu", l, 2 * pr + 1), ("dn", l, pr)]
    return units


def unit_end(name, l, i):
    if name in ("qs", "ks", "vs", "lat", "hc", "bg", "cg"):
        return (name, l, 1)
    if name == "gate":
        return ("gate", l, i // 2, 2 * (i % 2) + 1)
    if name == "wy":
        return ("y", l, i, 3)
    if name == "wo":
        return ("wo", l, 3)
    if name == "gu":
        return ("gu", l, i // 2)
    return ("down", l, i, 1)


def build(nc, A, freqs_d, out_d):
    plan = make_plan()
    jobs = plan.jobs
    units = unit_list()
    unit_of = {u: n for n, u in enumerate(units)}

    with ExitStack() as ctx:
        def sb(name, shape, dt=F32):
            return ctx.enter_context(nc.sbuf_tensor(name, shape, dt))

        def sem(name):
            return ctx.enter_context(nc.semaphore(name))

        bank = [ctx.enter_context(nc.psum_tensor(f"bank{i}", [P, 512], F32)) for i in range(8)]

        ring = sb("ring", [P, RING, 4096])
        xs = sb("xs", [P, TT, D])
        xn = sb("xn", [P, TT, D])
        hT = sb("hT", [P, DC, T])
        wuq = sb("wuq", [P, 2, H * QK])
        wukv = sb("wukv", [P, H * (NOPE + VD)])
        wr = sb("wr", [P, DC, NG + E])
        rbias = sb("rbias", [P, NG + E])
        gains = sb("gains", [P, 2, DC])
        lgain = sb("lgain", [P, 3])
        nbg = sb("nbg", [P, 24])
        cw = sb("cw", [P, 3, CB])
        fgain = xn[:, 1, :]
        ident = sb("ident", [P, P])
        low = sb("low", [P, P])
        upx = sb("upx", [P, P])
        ones = sb("ones", [P, P])
        mneg = sb("mneg", [P, P])
        tneg = sb("tneg", [P, P])
        tkeep = sb("tkeep", [P, P])
        iot_i = sb("iot_i", [P, SLOTS], I32)
        iot = sb("iot", [P, SLOTS])
        epst = sb("epst", [P, 1])
        pos_i = sb("pos_i", [P, TT], I32)
        posf = sb("posf", [P, TT])
        frq = sb("frq", [P, HALF])
        cosn = sb("cosn", [P, TT, HALF])
        sinn = sb("sinn", [P, TT, HALF])
        ang = sb("ang", [P, 2, TT, HALF])
        ang2 = sb("ang2", [P, 2, TT, HALF])
        nst = sb("nst", [P, 8, 8])
        rope_t = sb("rope_t", [P, 4, H, HALF])

        area = sb("area", [P, AREA])
        at = [0]

        def cut(*shape, back=None):
            if back is not None:
                at[0] = back
            n = int(np.prod(shape))
            a = area[:, at[0]:at[0] + n]
            at[0] += n
            assert at[0] <= AREA, at[0]
            if len(shape) == 2:
                a = a.rearrange("p (a b) -> p a b", b=shape[1])
            elif len(shape) == 3:
                a = a.rearrange("p (a b c) -> p a b c", b=shape[1], c=shape[2])
            elif len(shape) == 4:
                a = a.rearrange("p (a b c d) -> p a b c d", b=shape[1], c=shape[2], d=shape[3])
            return a

        qsT = cut(CB, T)
        ksT = cut(CB, T)
        vs = cut(TT, CW)
        z0 = cut(H, T)
        z1 = cut(H, P)
        l0 = cut(H, T)
        l1 = cut(H, P)
        lat = cut(TT, LAT)
        qn = cut(TT, H, QK)
        kn = cut(TT, H, QK)
        vn = cut(TT, CW)
        qT = cut(H, T)
        kT = cut(H, T)
        hc = cut(CB, T)
        bg = cut(CB, T)
        yc = cut(CB, T)
        sig = hc.rearrange("p a b -> p (a b)").rearrange("p (a b) -> p a b", a=2)
        latT = bg[:, 0:3, :]
        osT = qsT
        omT = ksT
        s0, s1 = z0[:, :, 0:P], z0
        pt0, pt1 = l0, l1
        kr = ang2[:, 0, :, :]

        Ps = cut(2, E, SLOTS, back=0)
        PW = [cut(2, 8, SLOTS), cut(2, 8, SLOTS)]
        xe = [cut(DC, 512), cut(DC, 512)]
        gus = cut(2, 512)
        aT = cut(2, 2, 4, P)
        yS = cut(2, D)
        sS = cut(2, T)
        lg = cut(2, NG + E)
        lge = cut(2, E)
        r4 = cut(8, 2, NG)
        r8 = cut(10, 2, EPG)
        r1 = cut(12, 2)
        member = cut(2, E)
        comb = cut(2, E)
        rk = cut(2, E)
        over = cut(2, E)
        ocol = cut(2, 2)
        og = [xe[0].rearrange("p c n -> p (c n)"), xe[1].rearrange("p c n -> p (c n)")]
        o_gu = og[0].rearrange("p (g c n) -> p g c n", g=2, c=DC)
        o_dn = og[1][:, 0:FC * D].rearrange("p (c n) -> p c n", c=FC)
        o_e = gus
        o_a = yS[:, 0, 0:TT * FE].rearrange("p (t n) -> p t n", t=TT)
        o_aT = yS[:, 1, 0:FC * T].rearrange("p (c n) -> p c n", c=FC)
        flag_i = sb("flag_i", [P, DEPTH], I32)

        pe_done = sem("pe_done")
        dve_freed = sem("dve_freed")
        act_freed = sem("act_freed")
        dve_step = sem("dve_step")
        act_step = sem("act_step")
        freed = {"dve": dve_freed, "act": act_freed}
        landed = [sem(f"unit_landed{i}") for i in range(RING)]
        consts_made = sem("consts_made")
        iota_made = sem("iota_made")
        x_landed = sem("x_landed")
        once_landed = sem("once_landed")
        small_landed = [sem(f"small_landed{l}") for l in range(DEPTH)]
        final_landed = sem("final_landed")
        angles_ready = sem("angles_ready")
        rope_ready = sem("rope_ready")
        const_ready = sem("const_ready")
        x_ready = sem("x_ready")
        ss_ready = sem("ss_ready")
        xn_ready = sem("xn_ready")
        z_abs = sem("z_abs")
        z_sp = sem("z_sp")
        l_ready = sem("l_ready")
        arg_ready = sem("arg_ready")
        a_ready = sem("a_ready")
        lat_ss = sem("lat_ss")
        lat_ready = sem("lat_ready")
        conv_ready = sem("conv_ready")
        rope_q = sem("rope_q")
        rope_k = sem("rope_k")
        ssub_ready = sem("ssub_ready")
        exp_ready = sem("exp_ready")
        pn_ready = sem("pn_ready")
        sig_ready = sem("sig_ready")
        sig_used = sem("sig_used")
        merged_ready = sem("merged_ready")
        rt_a = sem("rt_a")
        rt_b = sem("rt_b")
        member_ready = sem("member_ready")
        p_ready = sem("p_ready")
        pw_ready = sem("pw_ready")
        eg_ready = sem("eg_ready")
        out_stored = sem("out_stored")
        flag_ready = sem("flag_ready")
        o_landed, o_gu_done, o_exp, o_act, o_turned, o_copied, o_y, o_used, o_step = (
            [sem(f"{n}{l}") for l in range(DEPTH)] for n in
            ("o_landed", "o_gu_done", "o_exp", "o_act", "o_turned", "o_copied", "o_y", "o_used", "o_step"))

        w_in, w_o = A["w_in"], A["w_o"]
        w_y = {0: A["w_out_conv"], 1: A["w_out_mla"], 2: A["w_out_sb"]}
        col0 = {"qs": OFF_SB, "ks": OFF_SB + CW, "vs": OFF_SB + 2 * CW, "lat": OFF_LAT,
                "hc": OFF_HC, "bg": OFF_BG, "cg": OFF_CG}

        def slot(name, l, i=0):
            return unit_of[(name, l, i)] % RING

        def cols_unit(name, l, i=0):
            w = LAT if name == "lat" else 512
            return ring[:, slot(name, l, i), 0:DC * w].rearrange("p (c n) -> p c n", c=DC)

        def rows_unit(name, l, i):
            return ring[:, slot(name, l, i), :].rearrange("p (c n) -> p c n", c=4)

        def gu_unit(l, e):
            return ring[:, slot("gu", l, e), :].rearrange("p (g c n) -> p g c n", g=2, c=DC)

        def dn_unit(l, pr):
            return ring[:, slot("dn", l, pr), :].rearrange("p (e c n) -> p e c n", e=2, c=FC)

        def wait_unit(eng, name, l, i=0):
            n = unit_of[(name, l, i)]
            eng.wait_ge(landed[n % RING], 32 * (n // RING + 1))

        def wait_pe(eng, *key):
            eng.wait_ge(pe_done, jobs[key][0])

        def wait_read(eng, *key):
            _, _, by, value, _ = jobs[key]
            eng.wait_ge(freed[by], value)

        def B(*key):
            return bank[jobs[key][1]]

        block = ctx.enter_context(nc.Block())

        @block.sync
        def _(sp):
            sp.dma_start(xs[:], A["x"].rearrange("b (t p) d -> p (b t) d", p=P)).then_inc(x_landed, 16)
            with nc.allow_non_contiguous_dma("small transposed vectors"):
                sp.dma_start(pos_i[:], A["positions"].rearrange("b (t p) -> p (b t)", p=P)).then_inc(once_landed, 16)
            sp.dma_start(frq[:], freqs_d.partition_broadcast(P)).then_inc(once_landed, 16)
            for n, (name, l, i) in enumerate(units):
                first_of_layer = name == "qs"
                if first_of_layer:
                    if l:
                        wait_pe(sp, "kv", l - 1, 3)
                        wait_pe(sp, "route", l - 1)
                        wait_read(sp, "route", l - 1)
                        wait_read(sp, "gate", l - 1, 1, 3)
                        wait_read(sp, "gather", l - 1, OCTS - 1, 6)
                        wait_read(sp, "gather", l - 1, OCTS - 1, 7)
                    s = small_landed[l]
                    with nc.allow_non_contiguous_dma("small transposed vectors"):
                        sp.dma_start(gains[:, 0, :], A["attn_norm"][l].rearrange("(p c) -> p c", c=DC)).then_inc(s, 16)
                        sp.dma_start(gains[:, 1, :], A["ffn_norm"][l].rearrange("(p c) -> p c", c=DC)).then_inc(s, 16)
                        sp.dma_start(lgain[:, 0:2], A["q_norm"][l].rearrange("(c p) -> p c", p=P)).then_inc(s, 16)
                        sp.dma_start(lgain[:, 2:3], A["kv_norm"][l].rearrange("(c p) -> p c", p=P)).then_inc(s, 16)
                        sp.dma_start(nbg[:], A["b_gate"][l].rearrange("(c p) -> p c", p=P)).then_inc(s, 16)
                        for k in range(3):
                            sp.dma_start(cw[:, k, :], A["conv_w"][l, k].rearrange("(c p) -> p c", p=P)).then_inc(s, 16)
                    sp.dma_start(rbias[:, 0:NG], A["b_router_group"][l].partition_broadcast(P)).then_inc(s, 16)
                    sp.dma_start(rbias[:, NG:], A["b_router_expert"][l].partition_broadcast(P)).then_inc(s, 16)
                    sp.dma_start(wr[:, :, 0:NG], A["w_router_group"][l].rearrange("(p c) n -> p c n", c=DC)).then_inc(s, 16)
                    sp.dma_start(wr[:, :, NG:], A["w_router_expert"][l].rearrange("(p c) n -> p c n", c=DC)).then_inc(s, 16)
                    sp.dma_start(wuq[:], A["w_uq"][l].rearrange("(c p) n -> p c n", p=P)).then_inc(s, 16)
                    sp.dma_start(wukv[:], A["w_ukv"][l]).then_inc(s, 16)
                if n >= RING:
                    wait_pe(sp, *unit_end(*units[n - RING]))
                s = landed[n % RING]
                if name in col0 or name == "gate":
                    c0 = OFF_GATE + 512 * i if name == "gate" else col0[name]
                    dst = cols_unit(name, l, i)
                    src = w_in[l].rearrange("(p c) n -> p c n", c=DC)[:, :, c0:c0 + dst.shape[2]]
                    for hh in range(2):
                        sp.dma_start(dst[:, 4 * hh:4 * hh + 4, :], src[:, 4 * hh:4 * hh + 4, :]).then_inc(s, 16)
                elif name in ("wy", "wo"):
                    src = w_o[l, CW * i:CW * (i + 1), :] if name == "wo" else w_y[i][l]
                    src = src.rearrange("(c p) n -> p c n", p=P)
                    dst = rows_unit(name, l, i)
                    for hh in range(2):
                        sp.dma_start(dst[:, 2 * hh:2 * hh + 2, :], src[:, 2 * hh:2 * hh + 2, :]).then_inc(s, 16)
                elif name == "gu":
                    dst = gu_unit(l, i)
                    for g, w in enumerate(("w_exp_gate", "w_exp_up")):
                        sp.dma_start(dst[:, g, :, :], A[w][l, i].rearrange("(p c) n -> p c n", c=DC)).then_inc(s, 16)
                else:
                    dst = dn_unit(l, i)
                    for j in range(2):
                        sp.dma_start(dst[:, j, :, :], A["w_exp_down"][l, 2 * i + j].rearrange("(p c) n -> p c n", c=FC)).then_inc(s, 16)
            wait_pe(sp, "gather", DEPTH - 1, OCTS - 1, DC - 1)
            sp.dma_start(fgain, A["final_norm"].partition_broadcast(P)).then_inc(final_landed, 16)
            sp.wait_ge(xn_ready, 2 * DEPTH * TT + 2)
            sp.dma_start(out_d.rearrange("b (t p) d -> p (b t) d", p=P), xs[:]).then_inc(out_stored, 16)
            sp.wait_ge(out_stored, 16)

        @block.gpsimd
        def _(pool):
            n = [0]

            def step(ins):
                n[0] += 1
                ins.then_inc(consts_made, 1)
                pool.wait_ge(consts_made, n[0])

            for t, v in ((ident, 0.0), (low, 1.0), (upx, 1.0), (ones, 1.0), (mneg, 0.0), (tneg, 0.0), (tkeep, -1.0)):
                step(nc.gpsimd.memset(t[:], v))

            def fill(t, op, mult, stepv, value):
                step(nc.gpsimd.affine_select(out=t[:], in_=t[:], compare_op=op, fill=value, base=0,
                                             pattern=[[stepv, P]], channel_multiplier=mult))

            fill(ident, ALU.not_equal, 1, -1, 1.0)
            fill(low, ALU.is_ge, 1, -1, 0.0)
            fill(upx, ALU.is_gt, -1, 1, 0.0)
            fill(mneg, ALU.is_ge, 1, -1, NEG)
            fill(tneg, ALU.is_gt, -1, 1, NEG)
            fill(tkeep, ALU.is_gt, -1, 1, 0.0)
            nc.gpsimd.iota(iot_i[:], [[1, SLOTS]], base=0, channel_multiplier=0).then_inc(iota_made, 1)
            CONSTS[0] = n[0]
            for l in range(DEPTH):
                pool.wait_ge(p_ready, 2 * l + 2)
                for o in range(OCTS):
                    if o >= 2:
                        wait_pe(pool, "sT", l, 4 * o - 5)
                    for t in range(TT):
                        nc.gpsimd.tensor_tensor(PW[o % 2][:, t, :, :], Ps[:, t, 8 * o:8 * o + 8, :],
                                                comb[:, t, 8 * o:8 * o + 8].unsqueeze(2).to_broadcast([P, 8, SLOTS]),
                                                ALU.mult).then_inc(pw_ready, 1)
                pool.wait_ge(flag_ready, l + 1)
                with pool.If(pool.value_load(flag_i[0:1, l:l + 1], min_val=0, max_val=1) != 0):
                    wait_pe(pool, "moe", l, 3)
                    with pool.Fori(0, E, 1) as e:
                        pool.wait_ge(o_used[l], e + 1)
                        for g, w in enumerate(("w_exp_gate", "w_exp_up")):
                            pool.dma_start(o_gu[:, g, :, :], A[w][l, bass.ds(e, 1)].rearrange("e (p c) n -> p (e c) n", c=DC)).then_inc(o_landed[l], 16)
                        pool.dma_start(o_dn, A["w_exp_down"][l, bass.ds(e, 1)].rearrange("e (p c) n -> p (e c) n", c=FC)).then_inc(o_landed[l], 16)

        @block.tensor
        def _(pe):
            def begin(*key):
                before = jobs[key][4]
                if before:
                    wait_read(pe, *before)
                return B(*key)

            def blocks(name, l, unit, i, key, j):
                ps = begin(*key)
                w = cols_unit(unit, l, i)
                for b in range(2):
                    c0 = (2 * j + b) * P % 512
                    for c in range(DC):
                        mm = pe.matmul(ps[:, b * T:(b + 1) * T], w[:, c, c0:c0 + P], hT[:, c, :],
                                       start=c == 0, stop=c == DC - 1)
                mm.then_inc(pe_done, 1)

            def natural(name, l, t):
                ps = begin(name, l, t)
                w = cols_unit(name, l)
                for c in range(DC):
                    mm = pe.matmul(ps[:, 0:w.shape[2]], hT[:, c, t * P:(t + 1) * P], w[:, c, :],
                                   start=c == 0, stop=c == DC - 1)
                mm.then_inc(pe_done, 1)

            def turn_x(name, l, n):
                pe.wait_ge(xn_ready, TT * n + TT)
                for j in range(4):
                    ps = begin(name, l, j)
                    for cc in range(2):
                        for t in range(TT):
                            c = 2 * j + cc
                            mm = pe.transpose(ps[:, (2 * cc + t) * P:(2 * cc + t + 1) * P],
                                              xn[:, t, c * P:(c + 1) * P], ident[:])
                    mm.then_inc(pe_done, 1)

            def gate_and_y(l, b, src):
                for j in range(4):
                    if j % 2 == 0:
                        wait_unit(pe, "gate", l, 2 * b + j // 2)
                    blocks("gate", l, "gate", 2 * b + j // 2, ("gate", l, b, j), j)
                    if j == 0:
                        wait_unit(pe, "wy", l, b)
                    ps = begin("y", l, b, j)
                    w = rows_unit("wy", l, b)
                    for bb in range(2):
                        m = 2 * j + bb
                        for c in range(CB):
                            mm = pe.matmul(ps[:, bb * T:(bb + 1) * T], w[:, c, m * P:(m + 1) * P], src[:, c, :],
                                           start=c == 0, stop=c == CB - 1)
                    mm.then_inc(pe_done, 1)

            pe.wait_ge(consts_made, CONSTS_N)
            for l in range(DEPTH):
                turn_x("tr", l, 2 * l)
                wait_read(pe, "tr", l, 2)
                wait_read(pe, "tr", l, 3)
                for name in ("qs", "ks"):
                    wait_unit(pe, name, l)
                    for j in range(2):
                        blocks(name, l, name, 0, (name, l, j), j)
                for name in ("vs", "lat"):
                    wait_unit(pe, name, l)
                    for t in range(TT):
                        natural(name, l, t)
                wait_read(pe, "qs", l, 1)
                wait_read(pe, "ks", l, 1)
                for j in range(6):
                    ps = begin("z", l, j)
                    per = 2 if j < 4 else 4
                    h0 = 2 * j if j < 4 else 4 * (j - 4)
                    q0, k0 = (0, 0) if j < 4 else (P, P)
                    nq = T - q0
                    for i in range(per):
                        h = head_at(h0 + i)
                        r0 = SBD * (h % 2)
                        mm = pe.matmul(ps[:, i * nq:(i + 1) * nq], ksT[r0:r0 + SBD, h // 2, k0:k0 + P],
                                       qsT[r0:r0 + SBD, h // 2, q0:T], start=True, stop=True)
                    mm.then_inc(pe_done, 1)
                for name in ("hc", "bg", "cg"):
                    wait_unit(pe, name, l)
                    for j in range(2):
                        blocks(name, l, name, 0, (name, l, j), j)
                pe.wait_ge(lat_ready, l + 1)
                for j in range(2):
                    ps = begin("latT", l, j)
                    for i, c in enumerate((0, 1) if j == 0 else (2,)):
                        for t in range(TT):
                            mm = pe.transpose(ps[:, (TT * i + t) * P:(TT * i + t + 1) * P],
                                              lat[:, t, c * P:(c + 1) * P], ident[:])
                    mm.then_inc(pe_done, 1)
                pe.wait_ge(l_ready, l + 1)
                for j in range(6):
                    ps = begin("cum", l, j)
                    if j < 4:
                        pe.matmul(ps[:, :], low[:], l0[:, 2 * j:2 * j + 2, :], start=True, stop=False)
                        mm = pe.matmul(ps[:, :].rearrange("p (h q) -> p h q", h=2)[:, :, P:T], ones[:],
                                       l1[:, 2 * j:2 * j + 2, :], start=False, stop=True)
                    else:
                        mm = pe.matmul(ps[:, :], low[:], l1[:, 4 * (j - 4):4 * (j - 3), :], start=True, stop=True)
                    mm.then_inc(pe_done, 1)
                if True:
                    pe.wait_ge(small_landed[l], 16 * SMALL)
                wait_read(pe, "latT", l, 1)
                for j in range(4):
                    ps = begin("q", l, j)
                    t, hh = j // 2, j % 2
                    for c in range(2):
                        mm = pe.matmul(ps[:, 0:4 * QK], latT[:, c, t * P:(t + 1) * P],
                                       wuq[:, c, hh * 4 * QK:(hh + 1) * 4 * QK], start=c == 0, stop=c == 1)
                    mm.then_inc(pe_done, 1)
                for j in range(4):
                    ps = begin("kv", l, j)
                    t, hh = j // 2, j % 2
                    pe.matmul(ps[:, :], latT[:, 2, t * P:(t + 1) * P], wukv[:, hh * 512:(hh + 1) * 512],
                              start=True, stop=True).then_inc(pe_done, 1)
                pe.wait_ge(conv_ready, l + 1)
                gate_and_y(l, 0, yc)
                for name, src, rdy in (("qT", qn, rope_q), ("kT", kn, rope_k)):
                    pe.wait_ge(rdy, l + 1)
                    for j in range(4):
                        ps = begin(name, l, j)
                        for i in range(2):
                            for t in range(TT):
                                mm = pe.transpose(ps[0:QK, (TT * i + t) * P:(TT * i + t + 1) * P],
                                                  src[:, t, 2 * j + i, :], ident[:])
                        mm.then_inc(pe_done, 1)
                for j in range(2):
                    ps = begin("pvs", l, j)
                    for i in range(4):
                        h = 4 * j + i
                        if i % 2 == 0:
                            pe.wait_ge(a_ready, 2 * l + 2)
                        o = ps[SBD * (h % 2):SBD * (h % 2) + SBD, (i // 2) * T:(i // 2 + 1) * T]
                        pe.matmul(o, vs[:, 0, h * SBD:(h + 1) * SBD], l0[:, place_of(h), :], start=True, stop=False)
                        mm = pe.matmul(o[:, P:T], vs[:, 1, h * SBD:(h + 1) * SBD], l1[:, place_of(h), :], start=False, stop=True)
                    mm.then_inc(pe_done, 1)
                wait_read(pe, "qT", l, 3)
                wait_read(pe, "kT", l, 3)
                for j in range(6):
                    ps = begin("s", l, j)
                    per = 4 if j < 2 else 2
                    h0 = 4 * j if j < 2 else 2 * (j - 2)
                    t, nk = (0, P) if j < 2 else (1, T)
                    for i in range(per):
                        mm = pe.matmul(ps[:, i * nk:(i + 1) * nk], qT[0:QK, h0 + i, t * P:(t + 1) * P],
                                       kT[0:QK, h0 + i, 0:nk], start=True, stop=True)
                    mm.then_inc(pe_done, 1)
                wait_read(pe, "pvs", l, 1)
                gate_and_y(l, 2, osT)
                pe.wait_ge(pn_ready, l + 1)
                for j in range(6):
                    ps = begin("pT", l, j)
                    for i in range(4):
                        h = 4 * (j % 2) + i
                        src = (z1[:, h, :], z0[:, h, 0:P], z0[:, h, P:T])[j // 2]
                        mm = pe.transpose(ps[:, i * P:(i + 1) * P], src, ident[:])
                    mm.then_inc(pe_done, 1)
                wait_read(pe, "pT", l, 4)
                wait_read(pe, "pT", l, 5)
                for j in range(2):
                    ps = begin("pvm", l, j)
                    for i in range(4):
                        h = 4 * j + i
                        o = ps[VD * (h % 2):VD * (h % 2) + VD, (i // 2) * T:(i // 2 + 1) * T]
                        pe.matmul(o, vn[:, 0, h * VD:(h + 1) * VD], pt0[:, h, :], start=True, stop=False)
                        mm = pe.matmul(o[:, P:T], vn[:, 1, h * VD:(h + 1) * VD], pt1[:, h, :], start=False, stop=True)
                    mm.then_inc(pe_done, 1)
                wait_read(pe, "pvm", l, 1)
                gate_and_y(l, 1, omT)
                pe.wait_ge(merged_ready, l + 1)
                wait_unit(pe, "wo", l, 0)
                wait_unit(pe, "wo", l, 1)
                mT = xn[:, :, :].rearrange("p t (c n) -> p (t c) n", n=T)
                for j in range(4):
                    ps = begin("wo", l, j)
                    t, hh = j // 2, j % 2
                    for c in range(DC):
                        w = rows_unit("wo", l, c // 4)
                        mm = pe.matmul(ps[:, :], mT[:, c, t * P:(t + 1) * P], w[:, c % 4, hh * 512:(hh + 1) * 512],
                                       start=c == 0, stop=c == DC - 1)
                    mm.then_inc(pe_done, 1)

                turn_x("tr2", l, 2 * l + 1)
                wait_read(pe, "tr2", l, 2)
                wait_read(pe, "tr2", l, 3)
                ps = begin("route", l)
                for t in range(TT):
                    for c in range(DC):
                        mm = pe.matmul(ps[:, t * 64:t * 64 + NG + E], hT[:, c, t * P:(t + 1) * P], wr[:, c, :],
                                       start=c == 0, stop=c == DC - 1)
                mm.then_inc(pe_done, 1)
                pe.wait_ge(member_ready, l + 1)
                ps = begin("rank", l)
                pe.matmul(ps[:, 0:E], upx[:], member[:, 0, :], start=True, stop=True)
                pe.matmul(ps[:, E:2 * E], ones[:], member[:, 0, :], start=True, stop=False)
                pe.matmul(ps[:, E:2 * E], upx[:], member[:, 1, :], start=False, stop=True)
                pe.matmul(ps[:, 2 * E:3 * E], ones[:], member[:, 0, :], start=True, stop=False)
                pe.matmul(ps[:, 2 * E:3 * E], ones[:], member[:, 1, :], start=False, stop=True).then_inc(pe_done, 1)
                pe.wait_ge(p_ready, 2 * l + 2)

                def gather(o):
                    for c in range(DC):
                        ps = begin("gather", l, o, c)
                        for t in range(TT):
                            mm = pe.matmul(ps[:, :], xn[:, t, c * P:(c + 1) * P],
                                           Ps[:, t, 8 * o:8 * o + 8, :], start=t == 0, stop=t == TT - 1)
                        mm.then_inc(pe_done, 1)

                for o in range(OCTS):
                    gather(o)
                    wait_read(pe, "gather", l, o, DC - 2)
                    wait_read(pe, "gather", l, o, DC - 1)
                    for pr in range(4 * o, 4 * o + 4):
                        x_e = xe[o % 2]
                        pe.wait_ge(pw_ready, 2 * (OCTS * l + o) + 2)
                        ps = begin("sT", l, pr)
                        for t in range(TT):
                            mm = pe.transpose(ps[:, t * P:(t + 1) * P], PW[o % 2][:, t, 2 * pr - 8 * o:2 * pr - 8 * o + 2, :], ident[:])
                        mm.then_inc(pe_done, 1)
                        wait_unit(pe, "gu", l, 2 * pr)
                        wait_unit(pe, "gu", l, 2 * pr + 1)
                        ps = begin("gu", l, pr)
                        for c in range(DC):
                            for g in range(2):
                                for e in range(2):
                                    s = (2 * pr + e) % 8 * SLOTS
                                    mm = pe.matmul(ps[e * SLOTS:(e + 1) * SLOTS, g * FE:(g + 1) * FE],
                                                   x_e[:, c, s:s + SLOTS], gu_unit(l, 2 * pr + e)[:, g, c, :],
                                                   start=c == 0 and g == 0, stop=c == DC - 1,
                                                   skip_group_check=True)
                        mm.then_inc(pe_done, 1)
                        wait_read(pe, "gu", l, pr)
                        ps = begin("guT", l, pr)
                        for g in range(2):
                            for c in range(FC):
                                mm = pe.transpose(ps[:, (FC * g + c) * P:(FC * g + c + 1) * P],
                                                  gus[:, pr % 2, g * FE + c:(g + 1) * FE:FC], ident[:])
                        mm.then_inc(pe_done, 1)
                        wait_read(pe, "guT", l, pr)
                        wait_unit(pe, "dn", l, pr)
                        for hh in range(2):
                            ps = begin("down", l, pr, hh)
                            for c in range(FC):
                                for e in range(2):
                                    mm = pe.matmul(ps[e * SLOTS:(e + 1) * SLOTS, :],
                                                   aT[:, pr % 2, c, 3, e * SLOTS:(e + 1) * SLOTS],
                                                   dn_unit(l, pr)[:, e, c, hh * 512:(hh + 1) * 512],
                                                   start=c == 0, stop=c == FC - 1, skip_group_check=True)
                            mm.then_inc(pe_done, 1)
                        wait_read(pe, "down", l, pr, 0)
                        wait_read(pe, "down", l, pr, 1)
                        wait_read(pe, "sT", l, pr)
                        for j in range(4):
                            if pr == 0:
                                begin("moe", l, j)
                            t, hh = j // 2, j % 2
                            mm = pe.matmul(B("moe", l, j)[:, :], sS[:, pr % 2, t * P:(t + 1) * P],
                                           yS[:, pr % 2, hh * 512:(hh + 1) * 512],
                                           start=pr == 0, stop=pr == PAIRS - 1, skip_group_check=True)
                            if pr == PAIRS - 1:
                                mm.then_inc(pe_done, 1)

                pe.wait_ge(flag_ready, l + 1)
                with pe.If(pe.value_load(flag_i[0:1, l:l + 1], min_val=0, max_val=1) != 0):
                    for key in (("moe", l, 3), ("down", l, PAIRS - 1, 0)):
                        wait_read(pe, *key)
                    with pe.Fori(0, E, 1) as e:
                        pe.wait_ge(o_landed[l], 48 * e + 48)
                        pe.wait_ge(o_used[l], e + 1)
                        for t in range(TT):
                            for c in range(DC):
                                mm = pe.matmul(bank[t][:, :], hT[:, c, t * P:(t + 1) * P], o_gu[:, :, c, :],
                                               start=c == 0, stop=c == DC - 1)
                            mm.then_inc(o_gu_done[l], 1)
                        pe.wait_ge(o_act[l], 2 * e + 2)
                        for c in range(FC):
                            for t in range(TT):
                                mm = pe.transpose(bank[2][:, (TT * c + t) * P:(TT * c + t + 1) * P],
                                                  o_a[:, t, c:FE:FC], ident[:])
                        mm.then_inc(o_turned[l], 1)
                        pe.wait_ge(o_copied[l], e + 1)
                        for t in range(TT):
                            for hh in range(2):
                                for c in range(FC):
                                    mm = pe.matmul(bank[4 + 2 * t + hh][:, :], o_aT[:, c, t * P:(t + 1) * P],
                                                   o_dn[:, c, hh * 512:(hh + 1) * 512], start=c == 0, stop=c == FC - 1)
                        mm.then_inc(o_y[l], 1)

        @block.scalar
        def _(act):
            steps = [0]
            reads = [0]

            def link(ins):
                steps[0] += 1
                ins.then_inc(act_step, 1)
                act.wait_ge(act_step, steps[0])

            def done(ins, *key):
                reads[0] += 1
                assert jobs[key][2:4] == ("act", reads[0]), key
                ins.then_inc(act_freed, 1)

            def rms(n, parts, width, signal):
                for src, junk, k in parts:
                    last = act.activation(junk, src, ACT.Square, accum_out=nst[:, n, k:k + 1])
                link(last)
                for a, b, w in width:
                    last = act.activation(nst[:, n + 1, a:b], nst[:, n, a:b], ACT.Ln, scale=1.0 / w, bias=epst[:, 0:1])
                link(last)
                k = width[-1][1]
                act.activation(nst[:, n + 2, 0:k], nst[:, n + 1, 0:k], ACT.Exp, scale=-0.5).then_inc(signal, 1)

            def norm_x():
                rms(0, [(xs[:, t, :], xn[:, t, :], t) for t in range(TT)], [(0, TT, D)], ss_ready)

            def copy_pair(name, l, dst, scale=1.0):
                for j in range(2):
                    wait_pe(act, name, l, j)
                    done(act.activation(dst[:, 2 * j:2 * j + 2, :], B(name, l, j)[:, :], ACT.Copy, scale=scale), name, l, j)

            def turned(name, l, g):
                for j in (1, 3):
                    wait_pe(act, name, l, j)
                    for cc in range(2):
                        c = 2 * j + cc
                        ins = act.activation(hT[:, c, :], B(name, l, j)[:, cc * T:(cc + 1) * T], ACT.Copy,
                                             scale=gains[:, g, c:c + 1])
                    done(ins, name, l, j)

            def gates(l, b):
                for j in range(4):
                    n = 12 * l + 4 * (0, 2, 1)[b] + j
                    wait_pe(act, "gate", l, b, j)
                    if n >= 2:
                        act.wait_ge(sig_used, n - 1)
                    for bb in range(2):
                        c = 8 * b + 2 * j + bb
                        ins = act.activation(sig[:, n % 2, bb * T:(bb + 1) * T], B("gate", l, b, j)[:, bb * T:(bb + 1) * T],
                                             ACT.Exp, scale=-1.0, bias=nbg[:, c:c + 1])
                    done(ins, "gate", l, b, j)

            act.wait_ge(angles_ready, 1)
            act.activation(sinn[:], ang[:, 0, :, :], ACT.Sin)
            act.activation(cosn[:], ang[:, 1, :, :], ACT.Sin).then_inc(rope_ready, 1)
            act.wait_ge(const_ready, 1)
            act.wait_ge(x_landed, 16)
            for l in range(DEPTH):
                if l:
                    act.wait_ge(x_ready, 2 * l)
                norm_x()
                act.wait_ge(const_ready, 2 + l)
                turned("tr", l, 0)
                copy_pair("qs", l, qsT, SBD ** -0.5)
                copy_pair("ks", l, ksT)
                for t in range(TT):
                    wait_pe(act, "lat", l, t)
                    done(act.activation(lat[:, t, :], B("lat", l, t)[:, 0:LAT], ACT.Copy), "lat", l, t)
                for j in range(6):
                    wait_pe(act, "z", l, j)
                    dst = z0[:, 2 * j:2 * j + 2, :] if j < 4 else z1[:, 4 * (j - 4):4 * (j - 3), :]
                    done(act.activation(dst, B("z", l, j)[:, :], ACT.Copy), "z", l, j)
                act.wait_ge(act_freed, jobs[("lat", l, 1)][3])
                rms(3, [(lat[:, t, c0:c1], latT.rearrange("p c n -> p (c n)")[:, TT * c0 + t * (c1 - c0):TT * c0 + (t + 1) * (c1 - c0)], 2 * i + t)
                        for i, (c0, c1) in enumerate(((0, QR), (QR, QR + KVR))) for t in range(TT)],
                    [(0, 2, QR), (2, 4, KVR)], lat_ss)
                act.wait_ge(z_abs, l + 1)
                act.activation(l0[:, :, :], l0[:, :, :], ACT.Exp)
                link(act.activation(l1[:, :, :], l1[:, :, :], ACT.Exp))
                act.activation(l0[:, :, :], l0[:, :, :], ACT.Ln, bias=1.0)
                act.activation(l1[:, :, :], l1[:, :, :], ACT.Ln, bias=1.0).then_inc(z_sp, 1)
                copy_pair("hc", l, hc)
                copy_pair("bg", l, bg)
                act.wait_ge(arg_ready, l + 1)
                act.activation(l0[:, :, :], z0[:, :, :], ACT.Exp).then_inc(a_ready, 1)
                act.activation(l1[:, :, :], z1[:, :, :], ACT.Exp).then_inc(a_ready, 1)
                for j in range(4):
                    t, hh = j // 2, j % 2
                    wait_pe(act, "q", l, j)
                    done(act.activation(qn[:, t, 4 * hh:4 * hh + 4, :], B("q", l, j)[:, 0:4 * QK], ACT.Copy), "q", l, j)
                for j in range(4):
                    t, hh = j // 2, j % 2
                    wait_pe(act, "kv", l, j)
                    ps = B("kv", l, j)[:, :].rearrange("p (h d) -> p h d", h=4)
                    act.activation(kn[:, t, 4 * hh:4 * hh + 4, 0:NOPE], ps[:, :, 0:NOPE], ACT.Copy)
                    dst = vn[:, t, hh * 256:(hh + 1) * 256].rearrange("p (h d) -> p h d", h=4)
                    done(act.activation(dst, ps[:, :, NOPE:], ACT.Copy), "kv", l, j)
                gates(l, 0)
                for j in range(4):
                    wait_pe(act, "qT", l, j)
                    done(act.activation(qT[0:QK, 2 * j:2 * j + 2, :], B("qT", l, j)[0:QK, :], ACT.Copy), "qT", l, j)
                copy_pair("pvs", l, osT)
                act.wait_ge(ssub_ready, l + 1)
                act.activation(z1[:, :, :], z1[:, :, :], ACT.Exp)
                act.activation(z0[:, :, :], z0[:, :, :], ACT.Exp).then_inc(exp_ready, 1)
                gates(l, 2)
                for j in (1, 3, 5):
                    turned_probs(act, l, j, done, wait_pe, B, pt0, pt1, "act")
                copy_pair("pvm", l, omT)
                gates(l, 1)

                act.wait_ge(x_ready, 2 * l + 1)
                norm_x()
                turned("tr2", l, 1)
                act.wait_ge(rt_a, l + 1)
                act.activation(r4[:, 1, :, :], r4[:, 0, :, :], ACT.Exp)
                act.activation(r1[:, 4, :], r1[:, 3, :], ACT.Exp).then_inc(rt_b, 1)
                for o in range(OCTS):
                    for c in range(1, DC, 2):
                        wait_pe(act, "gather", l, o, c)
                        done(act.activation(xe[o % 2][:, c, :], B("gather", l, o, c)[:, :], ACT.Copy,
                                            scale=gains[:, 1, c:c + 1]), "gather", l, o, c)
                    for pr in range(4 * o, 4 * o + 4):
                        wait_pe(act, "sT", l, pr)
                        done(act.activation(sS[:, pr % 2, :], B("sT", l, pr)[:, 0:T], ACT.Copy), "sT", l, pr)
                        wait_pe(act, "gu", l, pr)
                        done(act.activation(gus[:, pr % 2, :], B("gu", l, pr)[:, :], ACT.Copy), "gu", l, pr)
                        wait_pe(act, "guT", l, pr)
                        act.activation(aT[:, pr % 2, :, 0, :], B("guT", l, pr)[:, 0:FC * P], ACT.Exp,
                                       scale=-1.0).then_inc(eg_ready, 1)
                        wait_pe(act, "down", l, pr, 0)
                        done(act.activation(yS[:, pr % 2, 0:512], B("down", l, pr, 0)[:, :], ACT.Copy), "down", l, pr, 0)
                act.wait_ge(flag_ready, l + 1)
                with act.If(act.value_load(flag_i[0:1, l:l + 1], min_val=0, max_val=1) != 0):
                    with act.Fori(0, E, 1) as e:
                        for t in range(TT):
                            act.wait_ge(o_gu_done[l], 2 * e + t + 1)
                            act.activation(o_e[:, 0, t * FE:(t + 1) * FE], bank[t][:, 0:FE], ACT.Exp, scale=-1.0).then_inc(o_exp[l], 1)
                        act.wait_ge(o_turned[l], e + 1)
                        act.activation(o_aT[:, :, :], bank[2][:, :], ACT.Copy).then_inc(o_copied[l], 1)
            act.wait_ge(x_ready, 2 * DEPTH)
            rms(0, [(xs[:, t, :], hT[:, 4 * t:4 * t + 4, :], t) for t in range(TT)], [(0, TT, D)], ss_ready)

        @block.vector
        def _(dve):
            steps = [0]
            reads = [0]

            def link(ins):
                steps[0] += 1
                ins.then_inc(dve_step, 1)
                dve.wait_ge(dve_step, steps[0])

            def done(ins, *key):
                reads[0] += 1
                assert jobs[key][2:4] == ("dve", reads[0]), key
                ins.then_inc(dve_freed, 1)

            def newton(n, width):
                k = width[-1][1]
                for a, b, w in width:
                    last = dve.tensor_scalar(nst[:, n + 1, a:b], nst[:, n, a:b], 1.0 / w, EPS, ALU.mult, ALU.add)
                link(last)
                link(dve.tensor_tensor(nst[:, n + 1, 0:k], nst[:, n + 1, 0:k], nst[:, n + 2, 0:k], ALU.mult))
                link(dve.tensor_tensor(nst[:, n + 1, 0:k], nst[:, n + 1, 0:k], nst[:, n + 2, 0:k], ALU.mult))
                link(dve.tensor_scalar(nst[:, n + 1, 0:k], nst[:, n + 1, 0:k], -0.5, 1.5, ALU.mult, ALU.add))
                link(dve.tensor_tensor(nst[:, n + 2, 0:k], nst[:, n + 1, 0:k], nst[:, n + 2, 0:k], ALU.mult))

            def norm_x(n):
                dve.wait_ge(ss_ready, n + 1)
                newton(0, [(0, TT, D)])
                for t in range(TT):
                    dve.tensor_scalar(xn[:, t, :].rearrange("q (c p) -> q p c", c=DC), xs[:, t, :].rearrange("q (p c) -> q p c", c=DC),
                                      nst[:, 2, t:t + 1], None, ALU.mult).then_inc(xn_ready, 1)

            def turned(name, l, g):
                for j in (0, 2):
                    wait_pe(dve, name, l, j)
                    for cc in range(2):
                        c = 2 * j + cc
                        ins = dve.tensor_scalar(hT[:, c, :], B(name, l, j)[:, cc * T:(cc + 1) * T],
                                                gains[:, g, c:c + 1], None, ALU.mult)
                    done(ins, name, l, j)

            def rotate(x1, x2, t, n):
                c = cosn[:, t, :].unsqueeze(1).to_broadcast([P, n, HALF])
                s = sinn[:, t, :].unsqueeze(1).to_broadcast([P, n, HALF])
                r = [rope_t[:, i, 0:n, :] for i in range(4)]
                dve.tensor_tensor(r[0], x1, c, ALU.mult)
                dve.tensor_tensor(r[1], x2, s, ALU.mult)
                dve.tensor_tensor(r[2], x2, c, ALU.mult)
                link(dve.tensor_tensor(r[3], x1, s, ALU.mult))
                dve.tensor_tensor(x1, r[0], r[1], ALU.subtract)
                last = dve.tensor_tensor(x2, r[2], r[3], ALU.add)
                return last

            def gated(l, b):
                mT = xn[:, :, :].rearrange("p t (c n) -> p (t c) n", n=T)
                for j in range(4):
                    n = 12 * l + 4 * (0, 2, 1)[b] + j
                    s = sig[:, n % 2, :]
                    wait_read(dve, "gate", l, b, j)
                    link(dve.tensor_scalar(s, s, 1.0, None, ALU.add))
                    link(dve.reciprocal(s, s))
                    wait_pe(dve, "y", l, b, j)
                    m = mT[:, 2 * j:2 * j + 2, :]
                    y = B("y", l, b, j)[:, :]
                    sv = s.rearrange("p (a n) -> p a n", a=2)
                    yv = y.rearrange("p (a n) -> p a n", a=2)
                    if b == 0:
                        ins = dve.tensor_tensor(m, sv, yv, ALU.mult)
                        done(ins, "y", l, b, j)
                        steps[0] += 1
                        nop = dve.tensor_copy(nst[:, 7, 0:1], nst[:, 7, 1:2])
                        nop.then_inc(dve_step, 1)
                        dve.wait_ge(dve_freed, reads[0])
                        dve.wait_ge(dve_step, steps[0])
                        dve.tensor_copy(nst[:, 7, 2:3], nst[:, 7, 3:4]).then_inc(sig_used, 1)
                    else:
                        ins = dve.tensor_tensor(sv, sv, yv, ALU.mult)
                        done(ins, "y", l, b, j)
                        dve.wait_ge(dve_freed, reads[0])
                        dve.tensor_tensor(m, m, sv, ALU.add).then_inc(sig_used, 1)

            dve.memset(epst[:], EPS)
            link(dve.memset(nst[:], 0.0))
            dve.wait_ge(iota_made, 1)
            link(dve.tensor_copy(iot[:], iot_i[:]))
            dve.wait_ge(once_landed, 32)
            link(dve.tensor_copy(posf[:], pos_i[:]))
            for t in range(TT):
                last = dve.tensor_scalar(ang[:, 0, t, :], frq[:], posf[:, t:t + 1], None, ALU.mult)
            link(last)
            for i, shift in ((1, 0.25), (0, 0.0)):
                k, a = ang2[:, i, :, :], ang[:, i, :, :]
                link(dve.tensor_scalar(k, ang[:, 0, :, :], float(np.float32(1 / TWO_PI)), shift, ALU.mult, ALU.add))
                link(dve.tensor_scalar(k, k, MAGIC, None, ALU.add))
                link(dve.tensor_scalar(k, k, -MAGIC, None, ALU.add))
                link(dve.scalar_tensor_tensor(out=a, in0=k, scalar=-C1, in1=ang[:, 0, :, :], op0=ALU.mult, op1=ALU.add))
                link(dve.scalar_tensor_tensor(out=a, in0=k, scalar=-C2, in1=a, op0=ALU.mult, op1=ALU.add))
                link(dve.scalar_tensor_tensor(out=a, in0=k, scalar=-C3, in1=a, op0=ALU.mult, op1=ALU.add))
                link(dve.tensor_scalar(a, a, float(np.float32(np.pi / 2)) if i else 0.0, PI_LOW, ALU.add, ALU.min))
                last = dve.tensor_scalar(a, a, -PI_LOW, None, ALU.max)
                link(last)
            dve.tensor_copy(nst[:, 6, 0:1], nst[:, 6, 1:2]).then_inc(angles_ready, 1)
            dve.tensor_copy(nst[:, 6, 2:3], nst[:, 6, 3:4]).then_inc(const_ready, 1)
            dve.wait_ge(rope_ready, 1)
            dve.wait_ge(consts_made, CONSTS_N)

            for l in range(DEPTH):
                dve.wait_ge(small_landed[l], 16 * SMALL)
                dve.tensor_scalar(nbg[:], nbg[:], -1.0, None, ALU.mult).then_inc(const_ready, 1)
                norm_x(2 * l)
                turned("tr", l, 0)
                for t in range(TT):
                    wait_pe(dve, "vs", l, t)
                    done(dve.tensor_copy(vs[:, t, :], B("vs", l, t)[:, :]), "vs", l, t)
                wait_read(dve, "z", l, 5)
                dve.scalar_tensor_tensor(out=l0[:, :, :], in0=z0[:, :, :], scalar=-1.0, in1=z0[:, :, :], op0=ALU.mult, op1=ALU.min)
                dve.scalar_tensor_tensor(out=l1[:, :, :], in0=z1[:, :, :], scalar=-1.0, in1=z1[:, :, :], op0=ALU.mult, op1=ALU.min).then_inc(z_abs, 1)
                dve.wait_ge(lat_ss, l + 1)
                newton(3, [(0, 2, QR), (2, 4, KVR)])
                for t in range(TT):
                    dve.tensor_scalar(lat[:, t, 0:QR], lat[:, t, 0:QR], nst[:, 5, t:t + 1], None, ALU.mult)
                    last = dve.tensor_scalar(lat[:, t, QR:QR + KVR], lat[:, t, QR:QR + KVR], nst[:, 5, 2 + t:3 + t], None, ALU.mult)
                last.then_inc(lat_ready, 1)
                for t in range(TT):
                    kr0 = lat[:, t, QR + KVR:LAT].rearrange("p (a n) -> p a n", a=2)
                    link(rotate(kr0[:, 0:1, :], kr0[:, 1:2, :], t, 1))
                dve.wait_ge(z_sp, l + 1)
                dve.scalar_tensor_tensor(out=l0[:, :, :], in0=z0[:, :, :], scalar=0.0, in1=l0[:, :, :], op0=ALU.max, op1=ALU.add)
                link(dve.scalar_tensor_tensor(out=l1[:, :, :], in0=z1[:, :, :], scalar=0.0, in1=l1[:, :, :], op0=ALU.max, op1=ALU.add))
                keep = tkeep[:, :].unsqueeze(1).to_broadcast([P, H, P])
                dve.tensor_tensor(l0[:, :, 0:P], l0[:, :, 0:P], keep, ALU.mult)
                dve.tensor_scalar(l0[:, :, P:T], l0[:, :, P:T], -1.0, None, ALU.mult)
                dve.tensor_tensor(l1[:, :, :], l1[:, :, :], keep, ALU.mult).then_inc(l_ready, 1)
                hide = tneg[:, :].unsqueeze(1).to_broadcast([P, H, P])
                dve.tensor_tensor(z0[:, :, 0:P], z0[:, :, 0:P], hide, ALU.add)
                link(dve.tensor_tensor(z1[:, :, :], z1[:, :, :], hide, ALU.add))
                for j in range(2):
                    wait_read(dve, "hc", l, j)
                    wait_pe(dve, "cg", l, j)
                    m = hc[:, 2 * j:2 * j + 2, :]
                    ins = dve.tensor_tensor(m, m, B("cg", l, j)[:, :].rearrange("p (a n) -> p a n", a=2), ALU.mult)
                    done(ins, "cg", l, j)
                dve.wait_ge(dve_freed, reads[0])
                for c in range(CB):
                    last = dve.tensor_scalar(yc[:, c, :], hc[:, c, :], cw[:, 2, c:c + 1], None, ALU.mult)
                link(last)
                for k in (1, 0):
                    s = 2 - k
                    for c in range(CB):
                        last = dve.scalar_tensor_tensor(out=yc[:, c, s:T], in0=hc[:, c, 0:T - s], scalar=cw[:, k, c:c + 1],
                                                        in1=yc[:, c, s:T], op0=ALU.mult, op1=ALU.add)
                    link(last)
                wait_read(dve, "bg", l, 1)
                dve.tensor_tensor(yc[:, :, :], yc[:, :, :], bg[:, :, :], ALU.mult).then_inc(conv_ready, 1)
                dve.wait_ge(conv_ready, l + 1)
                for j in range(2):
                    wait_pe(dve, "latT", l, j)
                    for i, c in enumerate((0, 1) if j == 0 else (2,)):
                        ins = dve.tensor_scalar(latT[:, c, :], B("latT", l, j)[:, i * T:(i + 1) * T], lgain[:, c:c + 1], None, ALU.mult)
                    done(ins, "latT", l, j)
                for j in range(6):
                    wait_pe(dve, "cum", l, j)
                    m = z0[:, 2 * j:2 * j + 2, :] if j < 4 else z1[:, 4 * (j - 4):4 * (j - 3), :]
                    ins = dve.tensor_tensor(m, m, B("cum", l, j)[:, :].rearrange("p (a n) -> p a n", a=2 if j < 4 else 4), ALU.add)
                    done(ins, "cum", l, j)
                dve.wait_ge(dve_freed, reads[0])
                dve.tensor_copy(nst[:, 6, 0:1], nst[:, 6, 1:2]).then_inc(arg_ready, 1)
                wait_read(dve, "q", l, 3)
                for t in range(TT):
                    link(rotate(qn[:, t, :, NOPE:NOPE + HALF], qn[:, t, :, NOPE + HALF:QK], t, H))
                dve.tensor_copy(nst[:, 6, 0:1], nst[:, 6, 1:2]).then_inc(rope_q, 1)
                wait_read(dve, "kv", l, 3)
                for t in range(TT):
                    last = dve.tensor_copy(kn[:, t, :, NOPE:QK], lat[:, t, QR + KVR:LAT].unsqueeze(1).to_broadcast([P, H, ROPE]))
                last.then_inc(rope_k, 1)
                gated(l, 0)
                for j in range(4):
                    wait_pe(dve, "kT", l, j)
                    done(dve.tensor_copy(kT[0:QK, 2 * j:2 * j + 2, :], B("kT", l, j)[0:QK, :].rearrange("p (a n) -> p a n", a=2)), "kT", l, j)
                scale = QK ** -0.5
                for j in range(6):
                    wait_pe(dve, "s", l, j)
                    per, nk = (4, P) if j < 2 else (2, T)
                    ps = B("s", l, j)[:, :].rearrange("p (h k) -> p h k", h=per)
                    dst = z1[:, 4 * j:4 * j + 4, :] if j < 2 else z0[:, 2 * (j - 2):2 * (j - 1), :]
                    if j >= 2:
                        dve.tensor_scalar(dst[:, :, 0:P], ps[:, :, 0:P], scale, None, ALU.mult)
                    done(dve.scalar_tensor_tensor(out=dst[:, :, nk - P:nk], in0=ps[:, :, nk - P:nk], scalar=scale,
                                                  in1=mneg[:, :].unsqueeze(1).to_broadcast([P, per, P]),
                                                  op0=ALU.mult, op1=ALU.add), "s", l, j)
                dve.wait_ge(dve_freed, reads[0])
                mx = rope_t[:, 0, :, 0:2]
                dve.tensor_reduce(mx[:, :, 0:1], z1[:, :, :], AX.X, ALU.max)
                link(dve.tensor_reduce(mx[:, :, 1:2], z0[:, :, :], AX.X, ALU.max))
                dve.tensor_tensor(z1[:, :, :], z1[:, :, :], mx[:, :, 0:1].to_broadcast([P, H, P]), ALU.subtract)
                dve.tensor_tensor(z0[:, :, :], z0[:, :, :], mx[:, :, 1:2].to_broadcast([P, H, T]), ALU.subtract).then_inc(ssub_ready, 1)
                gated_first = 2
                dve.wait_ge(exp_ready, l + 1)
                dve.tensor_reduce(mx[:, :, 0:1], z1[:, :, :], AX.X, ALU.add)
                link(dve.tensor_reduce(mx[:, :, 1:2], z0[:, :, :], AX.X, ALU.add))
                link(dve.reciprocal(rope_t[:, 1, :, 0:2], mx))
                rc = rope_t[:, 1, :, :]
                dve.tensor_tensor(z1[:, :, :], z1[:, :, :], rc[:, :, 0:1].to_broadcast([P, H, P]), ALU.mult)
                dve.tensor_tensor(z0[:, :, :], z0[:, :, :], rc[:, :, 1:2].to_broadcast([P, H, T]), ALU.mult).then_inc(pn_ready, 1)
                gated(l, gated_first)
                for j in (0, 2, 4):
                    turned_probs(dve, l, j, done, wait_pe, B, pt0, pt1, "dve")
                gated(l, 1)
                dve.wait_ge(sig_used, 12 * l + 12)
                dve.tensor_copy(nst[:, 6, 0:1], nst[:, 6, 1:2]).then_inc(merged_ready, 1)
                for j in range(4):
                    t, hh = j // 2, j % 2
                    wait_pe(dve, "wo", l, j)
                    m = xs[:, t, hh * 512:(hh + 1) * 512]
                    done(dve.tensor_tensor(m, m, B("wo", l, j)[:, :], ALU.add), "wo", l, j)
                dve.wait_ge(dve_freed, reads[0])
                dve.tensor_copy(nst[:, 6, 0:1], nst[:, 6, 1:2]).then_inc(x_ready, 1)

                norm_x(2 * l + 1)
                turned("tr2", l, 1)
                wait_pe(dve, "route", l)
                done(dve.tensor_tensor(lg[:, :, :], B("route", l)[:, 0:TT * 64].rearrange("p (t n) -> p t n", t=TT)[:, :, 0:NG + E],
                                       rbias[:, :].unsqueeze(1).to_broadcast([P, TT, NG + E]), ALU.add), "route", l)
                dve.wait_ge(dve_freed, reads[0])

                def bc(a, n):
                    return a.unsqueeze(2).to_broadcast([P, TT, n])

                def first_of(dst, at, top, n, tmp):
                    link(dve.tensor_tensor(tmp, at, bc(top, n), ALU.is_equal))
                    link(dve.tensor_tensor(tmp, tmp, countdown[n], ALU.mult))
                    link(dve.tensor_reduce(r1[:, 11, :], tmp, AX.X, ALU.max))
                    link(dve.tensor_tensor(dst, tmp, bc(r1[:, 11, :], n), ALU.is_equal))

                link(dve.tensor_scalar(r8[:, 9, 0, :], iot[:, 0:EPG], -1.0, float(EPG), ALU.mult, ALU.add))
                link(dve.tensor_scalar(r4[:, 7, 0, :], iot[:, 0:NG], -1.0, float(NG), ALU.mult, ALU.add))
                countdown = {EPG: r8[:, 9, 0:1, :].to_broadcast([P, TT, EPG]), NG: r4[:, 7, 0:1, :].to_broadcast([P, TT, NG])}
                link(dve.tensor_reduce(r1[:, 0, :], lg[:, :, 0:NG], AX.X, ALU.max))
                link(dve.tensor_tensor(r4[:, 0, :, :], lg[:, :, 0:NG], bc(r1[:, 0, :], NG), ALU.subtract))
                first_of(r4[:, 2, :, :], lg[:, :, 0:NG], r1[:, 0, :], NG, r4[:, 3, :, :])
                for g in range(NG):
                    ge = lg[:, :, NG + EPG * g:NG + EPG * (g + 1)]
                    link(dve.tensor_tensor(r8[:, 0 if g == 0 else 1, :, :], ge, bc(r4[:, 2, :, g], EPG), ALU.mult))
                    if g:
                        link(dve.tensor_tensor(r8[:, 0, :, :], r8[:, 0, :, :], r8[:, 1, :, :], ALU.add))
                link(dve.tensor_reduce(r1[:, 1, :], r8[:, 0, :, :], AX.X, ALU.max))
                first_of(r8[:, 2, :, :], r8[:, 0, :, :], r1[:, 1, :], EPG, r8[:, 3, :, :])
                link(dve.scalar_tensor_tensor(out=r8[:, 4, :, :], in0=r8[:, 2, :, :], scalar=NEG, in1=r8[:, 0, :, :],
                                              op0=ALU.mult, op1=ALU.add))
                link(dve.tensor_reduce(r1[:, 2, :], r8[:, 4, :, :], AX.X, ALU.max))
                first_of(r8[:, 5, :, :], r8[:, 4, :, :], r1[:, 2, :], EPG, r8[:, 3, :, :])
                dve.tensor_tensor(r1[:, 3, :], r1[:, 2, :], r1[:, 1, :], ALU.subtract).then_inc(rt_a, 1)
                link(dve.tensor_tensor(r8[:, 6, :, :], r8[:, 2, :, :], r8[:, 5, :, :], ALU.add))
                for g in range(NG):
                    last = dve.tensor_tensor(member[:, :, EPG * g:EPG * (g + 1)], r8[:, 6, :, :], bc(r4[:, 2, :, g], EPG), ALU.mult)
                last.then_inc(member_ready, 1)
                dve.wait_ge(rt_b, l + 1)
                link(dve.tensor_reduce(r1[:, 5, :], r4[:, 1, :, :], AX.X, ALU.add))
                link(dve.tensor_scalar(r1[:, 6, :], r1[:, 4, :], 1.0, None, ALU.add))
                link(dve.tensor_tensor(r1[:, 7, :], r1[:, 5, :], r1[:, 6, :], ALU.mult))
                link(dve.reciprocal(r1[:, 8, :], r1[:, 7, :]))
                link(dve.tensor_tensor(r8[:, 7, :, :], r8[:, 5, :, :], bc(r1[:, 4, :], EPG), ALU.mult))
                link(dve.tensor_tensor(r8[:, 7, :, :], r8[:, 7, :, :], r8[:, 2, :, :], ALU.add))
                link(dve.tensor_tensor(r8[:, 8, :, :], r8[:, 7, :, :], bc(r1[:, 8, :], EPG), ALU.mult))
                for g in range(NG):
                    last = dve.tensor_tensor(comb[:, :, EPG * g:EPG * (g + 1)], r8[:, 8, :, :], bc(r4[:, 2, :, g], EPG), ALU.mult)
                link(last)
                wait_pe(dve, "rank", l)
                link(dve.tensor_reduce(nst[:, 6, 4:5], B("rank", l)[:, TT * E:TT * E + E], AX.X, ALU.max))
                link(dve.tensor_scalar(nst[:, 6, 5:6], nst[:, 6, 4:5], float(SLOTS), None, ALU.is_gt))
                dve.tensor_copy(flag_i[:, l:l + 1], nst[:, 6, 5:6]).then_inc(flag_ready, 1)
                done(dve.scalar_tensor_tensor(out=rk[:, :, :], in0=B("rank", l)[:, 0:TT * E].rearrange("p (t n) -> p t n", t=TT),
                                              scalar=1.0, in1=member[:, :, :], op0=ALU.add, op1=ALU.mult), "rank", l)
                dve.wait_ge(dve_freed, reads[0])
                link(dve.tensor_scalar(rk[:, :, :], rk[:, :, :], -1.0, None, ALU.add))
                dve.scalar_tensor_tensor(out=over[:, :, :], in0=rk[:, :, :], scalar=float(SLOTS), in1=comb[:, :, :],
                                         op0=ALU.is_ge, op1=ALU.mult)
                for t in range(TT):
                    dve.tensor_tensor(Ps[:, t, :, :], iot[:, :].unsqueeze(1).to_broadcast([P, E, SLOTS]),
                                      rk[:, t, :].unsqueeze(2).to_broadcast([P, E, SLOTS]), ALU.is_equal).then_inc(p_ready, 1)
                for o in range(OCTS):
                    for c in range(0, DC, 2):
                        wait_pe(dve, "gather", l, o, c)
                        done(dve.tensor_scalar(xe[o % 2][:, c, :], B("gather", l, o, c)[:, :], gains[:, 1, c:c + 1], None, ALU.mult),
                             "gather", l, o, c)
                    for pr in range(4 * o, 4 * o + 4):
                        a = aT[:, pr % 2, :, :, :]
                        ps = B("guT", l, pr)[:, :].rearrange("p (g c s) -> p g c s", g=2, c=FC)
                        dve.wait_ge(eg_ready, PAIRS * l + pr + 1)
                        link(dve.tensor_scalar(a[:, :, 0, :], a[:, :, 0, :], 1.0, None, ALU.add))
                        link(dve.reciprocal(a[:, :, 1, :], a[:, :, 0, :]))
                        link(dve.tensor_tensor(a[:, :, 2, :], a[:, :, 1, :], ps[:, 0, :, :], ALU.mult))
                        done(dve.tensor_tensor(a[:, :, 3, :], a[:, :, 2, :], ps[:, 1, :, :], ALU.mult), "guT", l, pr)
                        wait_pe(dve, "down", l, pr, 1)
                        done(dve.tensor_copy(yS[:, pr % 2, 512:D], B("down", l, pr, 1)[:, :]), "down", l, pr, 1)
                for j in range(4):
                    t, hh = j // 2, j % 2
                    wait_pe(dve, "moe", l, j)
                    m = xs[:, t, hh * 512:(hh + 1) * 512]
                    done(dve.tensor_tensor(m, m, B("moe", l, j)[:, :], ALU.add), "moe", l, j)
                dve.wait_ge(dve_freed, reads[0])
                with dve.If(dve.value_load(flag_i[0:1, l:l + 1], min_val=0, max_val=1) != 0):
                    dve.tensor_copy(nst[:, 6, 0:1], nst[:, 6, 1:2]).then_inc(o_used[l], 1)
                    with dve.Fori(0, E, 1) as e:
                        for t in range(TT):
                            a = o_e[:, 0, t * FE:(t + 1) * FE]
                            b = o_e[:, 1, t * FE:(t + 1) * FE]
                            dve.wait_ge(o_exp[l], 2 * e + t + 1)
                            dve.tensor_scalar(a, a, 1.0, None, ALU.add).then_inc(o_step[l], 1)
                            dve.wait_ge(o_step[l], 7 * e + 3 * t + 1)
                            dve.reciprocal(b, a).then_inc(o_step[l], 1)
                            dve.wait_ge(o_step[l], 7 * e + 3 * t + 2)
                            dve.tensor_tensor(a, b, bank[t][:, 0:FE], ALU.mult).then_inc(o_step[l], 1)
                            dve.wait_ge(o_step[l], 7 * e + 3 * t + 3)
                            dve.tensor_tensor(o_a[:, t, :], a, bank[t][:, FE:2 * FE], ALU.mult).then_inc(o_act[l], 1)
                        dve.tensor_copy(ocol[:, 0, :], over[:, :, bass.ds(e, 1)].rearrange("p t e -> p (t e)")).then_inc(o_step[l], 1)
                        dve.wait_ge(o_step[l], 7 * e + 7)
                        dve.wait_ge(o_y[l], e + 1)
                        for t in range(TT):
                            for hh in range(2):
                                m = xs[:, t, hh * 512:(hh + 1) * 512]
                                ins = dve.scalar_tensor_tensor(out=m, in0=bank[4 + 2 * t + hh][:, :], scalar=ocol[:, 0, t:t + 1],
                                                               in1=m, op0=ALU.mult, op1=ALU.add)
                        ins.then_inc(o_used[l], 1)
                    dve.wait_ge(o_used[l], E + 1)
                dve.tensor_copy(nst[:, 6, 0:1], nst[:, 6, 1:2]).then_inc(x_ready, 1)

            dve.wait_ge(ss_ready, 2 * DEPTH + 1)
            newton(0, [(0, TT, D)])
            dve.wait_ge(final_landed, 16)
            for t in range(TT):
                dve.scalar_tensor_tensor(out=xs[:, t, :], in0=xs[:, t, :], scalar=nst[:, 2, t:t + 1], in1=fgain,
                                         op0=ALU.mult, op1=ALU.mult).then_inc(xn_ready, 1)


SMALL = 14
CONSTS_N = 13
CONSTS = [0]


def turned_probs(eng, l, j, done, wait_pe, B, pt0, pt1, by):
    wait_pe(eng, "pT", l, j)
    h0 = 4 * (j % 2)
    dst = (pt0[:, h0:h0 + 4, 0:P], pt0[:, h0:h0 + 4, P:T], pt1[:, h0:h0 + 4, :])[j // 2]
    src = B("pT", l, j)[:, :].rearrange("p (h q) -> p h q", h=4)
    if by == "act":
        done(eng.activation(dst, src, ACT.Copy), "pT", l, j)
    else:
        done(eng.tensor_copy(dst, src), "pT", l, j)


def kernel(**inputs):
    import concourse.bacc as bacc
    from concourse.bass_utils import run_bass_kernel_spmd

    nc = bacc.Bacc("TRN2", target_bir_lowering=False, num_devices=1)
    arrays, aps = {}, {}
    for name in INS:
        a = np.ascontiguousarray(inputs[name])
        arrays[f"in_{name}"] = a
        aps[name] = nc.dram_tensor(f"in_{name}", a.shape, mybir.dt.from_np(a.dtype), kind="ExternalInput").ap()
    freqs = (np.float32(10000.0) ** (-np.arange(HALF, dtype=np.float32) / np.float32(HALF))).astype(np.float32)
    arrays["in_freqs"] = freqs
    freqs_d = nc.dram_tensor("in_freqs", freqs.shape, F32, kind="ExternalInput").ap()
    out_d = nc.dram_tensor("out_x", (1, T, D), F32, kind="ExternalOutput").ap()
    build(nc, aps, freqs_d, out_d)
    r = run_bass_kernel_spmd(nc, [arrays], core_ids=[0])
    return r.results[0]["out_x"]
```

```python
from contextlib import ExitStack

import numpy as np

import concourse.bass as bass
from concourse import mybir

F32 = mybir.dt.float32
I32 = mybir.dt.int32
ALU = mybir.AluOpType
ACT = mybir.ActivationFunctionType
AX = mybir.AxisListType

P = 128
D = 1024
T = 256
TT = T // P
DC = D // P
DEPTH = 2
CW = 512
CB = CW // P
H = 8
NOPE, ROPE, VD = 64, 32, 64
QK = NOPE + ROPE
HALF = ROPE // 2
QR, KVR = 256, 128
SBD = 64
LAT = QR + KVR + ROPE
OFF_HC, OFF_BG, OFF_CG = 0, CW, 2 * CW
OFF_LAT = 3 * CW
OFF_SB = OFF_LAT + LAT
OFF_GATE = OFF_SB + 3 * CW
IN_COLS = OFF_GATE + 3 * D
NG, EPG = 4, 8
E = NG * EPG
FE = 256
FC = FE // P
SLOTS = 32
QE = P // SLOTS
QUADS = E // QE
GD = 4
MIDDLE = QUADS // 2
MORE = T // SLOTS - 1
EPS = 1e-6
NEG = -1e30
AREA = 15936
RING = 7
MAGIC = 1.5 * 2.0 ** 23
TWO_PI = 2.0 * np.pi
C1 = 6.28125
C2 = float(np.float32(np.floor((TWO_PI - C1) * 2 ** 22) / 2 ** 22))
C3 = float(np.float32(TWO_PI - C1 - C2))
PI_LOW = 3.1415925

INS = ["x", "positions", "attn_norm", "w_in", "b_gate", "conv_w", "w_out_conv", "q_norm", "kv_norm",
       "w_uq", "w_ukv", "w_out_mla", "w_out_sb", "w_o", "ffn_norm", "w_router_group",
       "b_router_group", "w_router_expert", "b_router_expert", "w_exp_gate", "w_exp_up",
       "w_exp_down", "final_norm"]


class Plan:

    def __init__(self):
        self.jobs = {}
        self.n = 0
        self.freed = {"dve": 0, "act": 0}
        self.last = [None] * 8
        self.at = 0

    def add(self, key, by, banks=8):
        bank = self.at % banks
        self.at += 1
        self.place(key, by, bank)

    def place(self, key, by, bank, before=None):
        self.n += 1
        self.freed[by] += 1
        self.jobs[key] = (self.n, bank, by, self.freed[by], before if before else self.last[bank])
        self.last[bank] = key


def place_of(h):
    return (h % 2) * (H // 2) + h // 2


def head_at(place):
    return 2 * (place % (H // 2)) + place // (H // 2)


def make_plan():
    p = Plan()
    for l in range(DEPTH):
        for j in range(4):
            p.add(("tr", l, j), "dve" if j % 2 == 0 else "act")
        for name, by in (("qs", "act"), ("ks", "act"), ("vs", "dve")):
            for j in range(2):
                p.add((name, l, j), by)
        for j in range(6):
            p.add(("z", l, j), "act")
        for name, by in (("hc", "act"), ("bg", "act"), ("cg", "dve"), ("lat", "act"), ("latT", "dve")):
            for j in range(2):
                p.add((name, l, j), by)
        for j in range(6):
            p.add(("cum", l, j), "dve")
        for j in range(4):
            p.add(("gate", l, 0, j), "act")
            p.add(("y", l, 0, j), "dve")
        for name in ("q", "kv"):
            for j in range(4):
                p.add((name, l, j), "act")
        for j in range(4):
            p.add(("qT", l, j), "act")
        for j in range(2):
            p.add(("pvs", l, j), "act")
        for j in range(4):
            p.add(("kT", l, j), "dve")
        for j in range(6):
            p.add(("s", l, j), "dve")
        for j in range(4):
            p.add(("gate", l, 2, j), "act")
            p.add(("y", l, 2, j), "dve")
        for j in range(6):
            p.add(("pT", l, j), "dve" if j % 2 == 0 else "act")
        for j in range(2):
            p.add(("pvm", l, j), "act")
        for j in range(4):
            p.add(("gate", l, 1, j), "act")
            p.add(("y", l, 1, j), "dve")
        for j in range(4):
            p.add(("wo", l, j), "dve")
        for j in range(4):
            p.add(("tr2", l, j), "dve" if j % 2 == 0 else "act")
        p.add(("route", l), "dve")
        p.add(("rank", l), "dve")
        before = [p.last[4 + j] for j in range(4)]
        for q in range(QUADS):
            p.add(("gather", l, q, 0), "dve", 4)
            p.add(("gather", l, q, 1), "act", 4)
            p.add(("sT", l, q), "act", 4)
            p.add(("gu", l, q), "act", 4)
            p.add(("guT", l, q), "dve", 4)
            p.add(("down", l, q, 0), "act", 4)
            p.add(("down", l, q, 1), "dve", 4)
        for j in range(4):
            p.place(("moe", l, j), "dve", 4 + j, before[j])
    return p


def unit_list():
    units = []
    for l in range(DEPTH):
        for name in ("qs", "ks", "vs", "hc", "bg", "cg", "lat"):
            units.append((name, l, 0))
        for b in (0, 2, 1):
            units += [("gate", l, 2 * b), ("wy", l, b), ("gate", l, 2 * b + 1)]
            if b == 0:
                units.append(("wu", l, 0))
        units += [("wo", l, 0), ("wo", l, 1)]
        for q in range(QUADS):
            units += [("gu", l, QE * q + i) for i in range(QE)] + [("dn", l, 2 * q), ("dn", l, 2 * q + 1)]
            if q == MIDDLE - 1:
                units += [("more_gu", l, 0), ("more_dn", l, 0)]
    return units


def unit_end(name, l, i):
    if name in ("qs", "ks", "vs", "lat", "hc", "bg", "cg"):
        return (name, l, 1)
    if name == "gate":
        return ("gate", l, i // 2, 2 * (i % 2) + 1)
    if name == "wy":
        return ("y", l, i, 3)
    if name == "wo":
        return ("wo", l, 3)
    if name == "wu":
        return ("kv", l, 3)
    if name in ("more_gu", "more_dn"):
        return ("gather", l, MIDDLE, 0)
    if name == "gu":
        return ("gu", l, i // QE)
    return ("down", l, i // 2, 1)


def build(nc, A, freqs_d, out_d):
    plan = make_plan()
    jobs = plan.jobs
    units = unit_list()
    unit_of = {u: n for n, u in enumerate(units)}

    with ExitStack() as ctx:
        def sb(name, shape, dt=F32):
            return ctx.enter_context(nc.sbuf_tensor(name, shape, dt))

        def sem(name):
            return ctx.enter_context(nc.semaphore(name))

        bank = [ctx.enter_context(nc.psum_tensor(f"bank{i}", [P, 512], F32)) for i in range(8)]

        ring = sb("ring", [P, RING, 4096])
        xs = sb("xs", [P, TT, D])
        xn = sb("xn", [P, TT, D])
        hT = sb("hT", [P, DC, T])
        wr = [sb(f"wr{l}", [P, DC, NG + E]) for l in range(DEPTH)]
        rbias = [sb(f"rbias{l}", [P, NG + E]) for l in range(DEPTH)]
        gains = [sb(f"gains{l}", [P, 2, DC]) for l in range(DEPTH)]
        lgain = [sb(f"lgain{l}", [P, 3]) for l in range(DEPTH)]
        nbg = [sb(f"nbg{l}", [P, 24]) for l in range(DEPTH)]
        cw = [sb(f"cw{l}", [P, 3, CB]) for l in range(DEPTH)]
        fgain = hT[:, 0:4, :].rearrange("p c n -> p (c n)")
        ident = sb("ident", [P, P])
        low = sb("low", [P, P])
        ones = sb("ones", [P, P])
        fold = sb("fold", [P, SLOTS])
        mneg = sb("mneg", [P, P])
        tneg = sb("tneg", [P, P])
        before = sb("before", [P, P])
        iot_i = sb("iot_i", [P, SLOTS], I32)
        iot = sb("iot", [P, SLOTS])
        epst = sb("epst", [P, 1])
        pos_i = sb("pos_i", [P, TT], I32)
        posf = sb("posf", [P, TT])
        frq = sb("frq", [P, HALF])
        cosn = sb("cosn", [P, TT, HALF])
        sinn = sb("sinn", [P, TT, HALF])
        nst = sb("nst", [P, 8, 8])
        flag_i = sb("flag_i", [P, DEPTH], I32)
        e_i = sb("e_i", [P, 1], I32)
        rope_t = sb("rope_t", [P, 4, H, HALF])

        area = sb("area", [P, AREA])
        at = [0]

        def cut(*shape, back=None):
            if back is not None:
                at[0] = back
            n = int(np.prod(shape))
            a = area[:, at[0]:at[0] + n]
            at[0] += n
            assert at[0] <= AREA, at[0]
            if len(shape) == 2:
                a = a.rearrange("p (a b) -> p a b", b=shape[1])
            elif len(shape) == 3:
                a = a.rearrange("p (a b c) -> p a b c", b=shape[1], c=shape[2])
            elif len(shape) == 4:
                a = a.rearrange("p (a b c d) -> p a b c d", b=shape[1], c=shape[2], d=shape[3])
            return a

        qsT = cut(CB, T)
        ksT = cut(CB, T)
        vs = cut(TT, CW)
        z0 = cut(H, T)
        z1 = cut(H, P)
        l0 = cut(H, T)
        l1 = cut(H, P)
        lat_at = at[0]
        lat = cut(TT, LAT)
        latT = cut(3, T)
        vn = cut(TT, CW)
        ang, ang2 = (vn[:, i, 0:64].rearrange("p (s t n) -> p s t n", s=2, t=TT) for i in range(2))
        sig = cut(2, 512)
        mark = at[0]
        hc = cut(CB, T)
        bg = cut(CB, T)
        yc = cut(CB, T)
        qn = cut(TT, H, QK, back=mark)
        kn = cut(TT, H, QK)
        qT = area[:, 0:H * T].rearrange("p (a b) -> p a b", b=T)
        kT = l0
        omT = cut(CB, T, back=mark)
        osT = cut(CB, T, back=lat_at)
        at[0] = mark + 3 * CB * T
        pt0, pt1 = l0, l1

        Ps = cut(TT, E, SLOTS, back=0)
        PW = [cut(TT, QE, SLOTS) for _ in range(2)]
        xe = [cut(DC, P), cut(DC, P)]
        gus = cut(2, 512)
        aT = cut(2, FC, 4, P)
        yS = cut(2, D)
        sS = cut(2, T)
        lg = cut(TT, NG + E)
        r4 = cut(8, TT, NG)
        r8 = cut(10, TT, EPG)
        r1 = cut(12, TT)
        member = cut(TT, E)
        comb = cut(TT, E)
        rk = cut(TT, E)
        count = cut(1, E)[:, 0, :]
        blk = cut(MORE, E)
        blk_one = cut(MORE, E)
        o_eq = cut(MORE, E)
        o_first = cut(MORE, E)
        o_sel = cut(1, E)[:, 0, :]
        o_tmp = cut(TT, E)
        o_num = cut(1, 8)[:, 0, :]
        o_rk = cut(1, 4)[:, 0, :]
        o_P = cut(TT, SLOTS)
        o_PW = cut(TT, SLOTS)
        o_x = cut(DC, SLOTS)
        turn = cut(1, 1)[:, 0, :]
        ones_row = ones[:, 0:1].to_broadcast([P, MORE * E])

        pe_done = sem("pe_done")
        dve_freed = sem("dve_freed")
        act_freed = sem("act_freed")
        dve_step = sem("dve_step")
        act_step = sem("act_step")
        freed = {"dve": dve_freed, "act": act_freed}
        landed = [sem(f"unit_landed{i}") for i in range(RING)]
        consts_made = sem("consts_made")
        iota_made = sem("iota_made")
        x_landed = sem("x_landed")
        once_landed = sem("once_landed")
        small_landed = [sem(f"small_landed{l}") for l in range(DEPTH)]
        final_landed = sem("final_landed")
        angles_ready = sem("angles_ready")
        rope_ready = sem("rope_ready")
        const_ready = sem("const_ready")
        x_ready = sem("x_ready")
        ss_ready = sem("ss_ready")
        xn_ready = sem("xn_ready")
        z_abs = sem("z_abs")
        z_sp = sem("z_sp")
        l_ready = sem("l_ready")
        arg_ready = sem("arg_ready")
        a_ready = sem("a_ready")
        lat_ss = sem("lat_ss")
        lat_ready = sem("lat_ready")
        conv_ready = sem("conv_ready")
        rope_q = sem("rope_q")
        rope_k = sem("rope_k")
        ssub_ready = sem("ssub_ready")
        exp_ready = sem("exp_ready")
        pn_ready = sem("pn_ready")
        sig_ready = sem("sig_ready")
        sig_used = sem("sig_used")
        merged_ready = sem("merged_ready")
        rt_a = sem("rt_a")
        rt_b = sem("rt_b")
        member_ready = sem("member_ready")
        p_ready = sem("p_ready")
        pw_ready = sem("pw_ready")
        eg_ready = sem("eg_ready")
        out_stored = sem("out_stored")
        flag_ready = sem("flag_ready")
        fold_ready = sem("fold_ready")
        (o_chosen, o_taken, o_landed, o_slots, o_gathered, o_x_ready, o_gu_done, o_gu_read, o_turned, o_exp, o_act,
         o_down, o_y_ready, o_out, o_used, o_step) = (
            [sem(f"{n}{l}") for l in range(DEPTH)] for n in
            ("o_chosen", "o_taken", "o_landed", "o_slots", "o_gathered", "o_x_ready", "o_gu_done", "o_gu_read", "o_turned",
             "o_exp", "o_act", "o_down", "o_y_ready", "o_out", "o_used", "o_step"))

        w_in, w_o = A["w_in"], A["w_o"]
        w_y = {0: A["w_out_conv"], 1: A["w_out_mla"], 2: A["w_out_sb"]}
        col0 = {"qs": OFF_SB, "ks": OFF_SB + CW, "vs": OFF_SB + 2 * CW, "lat": OFF_LAT,
                "hc": OFF_HC, "bg": OFF_BG, "cg": OFF_CG}

        def slot(name, l, i=0):
            return unit_of[(name, l, i)] % RING

        def cols_unit(name, l, i=0):
            w = LAT if name == "lat" else 512
            return ring[:, slot(name, l, i), 0:DC * w].rearrange("p (c n) -> p c n", c=DC)

        def rows_unit(name, l, i):
            return ring[:, slot(name, l, i), :].rearrange("p (c n) -> p c n", c=4)

        def gu_unit(l, e):
            return ring[:, slot("gu", l, e), :].rearrange("p (g c n) -> p g c n", g=2, c=DC)

        def dn_unit(l, pr):
            return ring[:, slot("dn", l, pr), :].rearrange("p (e c n) -> p e c n", e=2, c=FC)

        def wuq(l):
            return ring[:, slot("wu", l), 0:2 * H * QK].rearrange("p (c n) -> p c n", c=2)

        def wukv(l):
            return ring[:, slot("wu", l), 2 * H * QK:2 * H * QK + H * (NOPE + VD)]

        def o_gu(l):
            return ring[:, slot("more_gu", l), :].rearrange("p (g c n) -> p g c n", g=2, c=DC)

        def o_dn(l):
            return ring[:, slot("more_dn", l), 0:FC * D].rearrange("p (c n) -> p c n", c=FC)

        def wait_unit(eng, name, l, i=0):
            n = unit_of[(name, l, i)]
            seen = sum(units[m][0] not in ("more_gu", "more_dn") for m in range(n % RING, n + 1, RING))
            eng.wait_ge(landed[n % RING], 32 * seen)

        def wait_pe(eng, *key):
            eng.wait_ge(pe_done, jobs[key][0])

        def wait_read(eng, *key):
            _, _, by, value, _ = jobs[key]
            eng.wait_ge(freed[by], value)

        def B(*key):
            return bank[jobs[key][1]]

        block = ctx.enter_context(nc.Block())

        @block.sync
        def _(sp):
            sp.dma_start(xs[:], A["x"].rearrange("b (t p) d -> p (b t) d", p=P)).then_inc(x_landed, 16)
            with nc.allow_non_contiguous_dma("small transposed vectors"):
                sp.dma_start(pos_i[:], A["positions"].rearrange("b (t p) -> p (b t)", p=P)).then_inc(once_landed, 16)
            sp.dma_start(frq[:], freqs_d.partition_broadcast(P)).then_inc(once_landed, 16)
            for n, (name, l, i) in enumerate(units):
                first_of_layer = name == "qs"
                if first_of_layer:
                    s = small_landed[l]
                    with nc.allow_non_contiguous_dma("small transposed vectors"):
                        sp.dma_start(gains[l][:, 0, :], A["attn_norm"][l].rearrange("(p c) -> p c", c=DC)).then_inc(s, 16)
                        sp.dma_start(gains[l][:, 1, :], A["ffn_norm"][l].rearrange("(p c) -> p c", c=DC)).then_inc(s, 16)
                        sp.dma_start(lgain[l][:, 0:2], A["q_norm"][l].rearrange("(c p) -> p c", p=P)).then_inc(s, 16)
                        sp.dma_start(lgain[l][:, 2:3], A["kv_norm"][l].rearrange("(c p) -> p c", p=P)).then_inc(s, 16)
                        sp.dma_start(nbg[l][:], A["b_gate"][l].rearrange("(c p) -> p c", p=P)).then_inc(s, 16)
                        for k in range(3):
                            sp.dma_start(cw[l][:, k, :], A["conv_w"][l, k].rearrange("(c p) -> p c", p=P)).then_inc(s, 16)
                    sp.dma_start(rbias[l][:, 0:NG], A["b_router_group"][l].partition_broadcast(P)).then_inc(s, 16)
                    sp.dma_start(rbias[l][:, NG:], A["b_router_expert"][l].partition_broadcast(P)).then_inc(s, 16)
                    sp.dma_start(wr[l][:, :, 0:NG], A["w_router_group"][l].rearrange("(p c) n -> p c n", c=DC)).then_inc(s, 16)
                    sp.dma_start(wr[l][:, :, NG:], A["w_router_expert"][l].rearrange("(p c) n -> p c n", c=DC)).then_inc(s, 16)
                if n >= RING:
                    wait_pe(sp, *unit_end(*units[n - RING]))
                s = landed[n % RING]
                if name == "more_gu":
                    continue
                if name == "more_dn":
                    sp.wait_ge(flag_ready, l + 1)
                    n_more = sp.value_load(flag_i[0:1, l:l + 1], min_val=0, max_val=E * MORE)
                    with sp.If(n_more != 0):
                        with sp.Fori(0, n_more, 1) as i:
                            sp.wait_ge(o_chosen[l], i + 1)
                            sp.sem_inc(o_taken[l], 1)
                            e = sp.value_load(e_i[0:1, 0:1], min_val=0, max_val=E - 1)
                            for g, w in enumerate(("w_exp_gate", "w_exp_up")):
                                sp.dma_start(o_gu(l)[:, g, :, :], A[w][l, bass.ds(e, 1)].rearrange("e (p c) n -> p (e c) n", c=DC)).then_inc(o_landed[l], 16)
                            sp.dma_start(o_dn(l), A["w_exp_down"][l, bass.ds(e, 1)].rearrange("e (p c) n -> p (e c) n", c=FC)).then_inc(o_landed[l], 16)
                    continue
                if name in col0 or name == "gate":
                    c0 = OFF_GATE + 512 * i if name == "gate" else col0[name]
                    dst = cols_unit(name, l, i)
                    src = w_in[l].rearrange("(p c) n -> p c n", c=DC)[:, :, c0:c0 + dst.shape[2]]
                    for hh in range(2):
                        sp.dma_start(dst[:, 4 * hh:4 * hh + 4, :], src[:, 4 * hh:4 * hh + 4, :]).then_inc(s, 16)
                elif name in ("wy", "wo"):
                    src = w_o[l, CW * i:CW * (i + 1), :] if name == "wo" else w_y[i][l]
                    src = src.rearrange("(c p) n -> p c n", p=P)
                    dst = rows_unit(name, l, i)
                    for hh in range(2):
                        sp.dma_start(dst[:, 2 * hh:2 * hh + 2, :], src[:, 2 * hh:2 * hh + 2, :]).then_inc(s, 16)
                elif name == "wu":
                    sp.dma_start(wuq(l), A["w_uq"][l].rearrange("(c p) n -> p c n", p=P)).then_inc(s, 16)
                    sp.dma_start(wukv(l), A["w_ukv"][l]).then_inc(s, 16)
                elif name == "gu":
                    dst = gu_unit(l, i)
                    for g, w in enumerate(("w_exp_gate", "w_exp_up")):
                        sp.dma_start(dst[:, g, :, :], A[w][l, i].rearrange("(p c) n -> p c n", c=DC)).then_inc(s, 16)
                else:
                    dst = dn_unit(l, i)
                    for j in range(2):
                        sp.dma_start(dst[:, j, :, :], A["w_exp_down"][l, 2 * i + j].rearrange("(p c) n -> p c n", c=FC)).then_inc(s, 16)
            wait_pe(sp, "route", DEPTH - 1)
            sp.dma_start(fgain, A["final_norm"].partition_broadcast(P)).then_inc(final_landed, 16)
            sp.wait_ge(xn_ready, 2 * DEPTH * TT + 2)
            sp.dma_start(out_d.rearrange("b (t p) d -> p (b t) d", p=P), xs[:]).then_inc(out_stored, 16)
            sp.wait_ge(out_stored, 16)

        @block.gpsimd
        def _(pool):
            n = [0]

            def step(ins):
                n[0] += 1
                ins.then_inc(consts_made, 1)
                pool.wait_ge(consts_made, n[0])

            for t, v in ((ident, 0.0), (low, 1.0), (before, 1.0), (ones, 1.0), (mneg, 0.0), (tneg, 0.0)):
                step(nc.gpsimd.memset(t[:], v))

            def fill(t, op, mult, stepv, value):
                step(nc.gpsimd.affine_select(out=t[:], in_=t[:], compare_op=op, fill=value, base=0,
                                             pattern=[[stepv, P]], channel_multiplier=mult))

            fill(ident, ALU.not_equal, 1, -1, 1.0)
            fill(low, ALU.is_ge, 1, -1, 0.0)
            fill(before, ALU.is_gt, -1, 1, 0.0)
            fill(mneg, ALU.is_ge, 1, -1, NEG)
            fill(tneg, ALU.is_gt, -1, 1, NEG)
            nc.gpsimd.iota(iot_i[:], [[1, SLOTS]], base=0, channel_multiplier=0).then_inc(iota_made, 1)
            CONSTS[0] = n[0]
            for l in range(DEPTH):
                pool.wait_ge(p_ready, 2 * l + 2)
                for q in range(QUADS):
                    if q >= 2:
                        wait_pe(pool, "sT", l, q - 2)
                    for t in range(TT):
                        nc.gpsimd.tensor_tensor(PW[q % 2][:, t, :, :], Ps[:, t, QE * q:QE * q + QE, :],
                                                comb[:, t, QE * q:QE * q + QE].unsqueeze(2).to_broadcast([P, QE, SLOTS]),
                                                ALU.mult).then_inc(pw_ready, 1)

        @block.tensor
        def _(pe):
            def begin(*key):
                before = jobs[key][4]
                if before:
                    wait_read(pe, *before)
                return B(*key)

            def blocks(name, l, unit, i, key, j):
                ps = begin(*key)
                w = cols_unit(unit, l, i)
                for b in range(2):
                    c0 = (2 * j + b) * P % 512
                    for c in range(DC):
                        mm = pe.matmul(ps[:, b * T:(b + 1) * T], w[:, c, c0:c0 + P], hT[:, c, :],
                                       start=c == 0, stop=c == DC - 1)
                mm.then_inc(pe_done, 1)

            def natural(name, l, t):
                ps = begin(name, l, t)
                w = cols_unit(name, l)
                for c in range(DC):
                    mm = pe.matmul(ps[:, 0:w.shape[2]], hT[:, c, t * P:(t + 1) * P], w[:, c, :],
                                   start=c == 0, stop=c == DC - 1)
                mm.then_inc(pe_done, 1)

            def turn_x(name, l, n):
                pe.wait_ge(xn_ready, TT * n + TT)
                for j in range(4):
                    ps = begin(name, l, j)
                    for cc in range(2):
                        for t in range(TT):
                            c = 2 * j + cc
                            mm = pe.transpose(ps[:, (2 * cc + t) * P:(2 * cc + t + 1) * P],
                                              xn[:, t, c * P:(c + 1) * P], ident[:])
                    mm.then_inc(pe_done, 1)

            def turn_heads(name, l, src):
                for j in range(4):
                    ps = begin(name, l, j)
                    for i in range(2):
                        for t in range(TT):
                            mm = pe.transpose(ps[0:QK, (TT * i + t) * P:(TT * i + t + 1) * P],
                                              src[:, t, 2 * j + i, :], ident[:])
                    mm.then_inc(pe_done, 1)

            def gate_and_y(l, b, src):
                for j in range(4):
                    if j % 2 == 0:
                        wait_unit(pe, "gate", l, 2 * b + j // 2)
                    blocks("gate", l, "gate", 2 * b + j // 2, ("gate", l, b, j), j)
                    if j == 0:
                        wait_unit(pe, "wy", l, b)
                    ps = begin("y", l, b, j)
                    w = rows_unit("wy", l, b)
                    for bb in range(2):
                        m = 2 * j + bb
                        for c in range(CB):
                            mm = pe.matmul(ps[:, bb * T:(bb + 1) * T], w[:, c, m * P:(m + 1) * P], src[:, c, :],
                                           start=c == 0, stop=c == CB - 1)
                    mm.then_inc(pe_done, 1)

            def further_blocks(l):
                pe.wait_ge(flag_ready, l + 1)
                n_more = pe.value_load(flag_i[0:1, l:l + 1], min_val=0, max_val=E * MORE)
                with pe.If(n_more != 0):
                    for j in range(2):
                        wait_read(pe, "down", l, MIDDLE - 1, j)
                    with pe.Fori(0, n_more, 1) as i:
                        pe.wait_ge(o_slots[l], i + 1)
                        for c in range(DC):
                            for t in range(TT):
                                pe.matmul(bank[0][:, c * SLOTS:(c + 1) * SLOTS], xn[:, t, c * P:(c + 1) * P],
                                          o_P[:, t, :], start=t == 0, stop=t == TT - 1)
                        for t in range(TT):
                            mm = pe.transpose(bank[1][0:SLOTS, t * P:(t + 1) * P], o_PW[:, t, :], ident[:])
                        mm.then_inc(o_gathered[l], 1)
                        pe.wait_ge(o_landed[l], 48 * i + 48)
                        pe.wait_ge(o_x_ready[l], i + 1)
                        for cc in range(2):
                            for g in range(2):
                                for j in range(QE):
                                    c = 2 * j + cc
                                    mm = pe.matmul(bank[2][j * SLOTS:(j + 1) * SLOTS, g * FE:(g + 1) * FE], o_x[:, c, :],
                                                   o_gu(l)[:, g, c, :], start=cc == 0 and g == 0, stop=cc == 1,
                                                   skip_group_check=True)
                        mm.then_inc(o_gu_done[l], 1)
                        pe.wait_ge(o_gu_read[l], i + 1)
                        for g in range(2):
                            for c in range(FC):
                                mm = pe.matmul(bank[3][:, (FC * g + c) * SLOTS:(FC * g + c + 1) * SLOTS],
                                               gus[:, 0, g * FE + c:(g + 1) * FE:FC], fold[:], start=True, stop=True)
                        mm.then_inc(o_turned[l], 1)
                        pe.wait_ge(o_act[l], i + 1)
                        for hh in range(2):
                            for c in range(FC):
                                mm = pe.matmul(bank[hh][0:SLOTS, :], aT[:, 0, c, 3, 0:SLOTS],
                                               o_dn(l)[:, c, hh * 512:(hh + 1) * 512], start=c == 0, stop=c == FC - 1)
                        mm.then_inc(o_down[l], 1)
                        pe.wait_ge(o_y_ready[l], i + 1)
                        for t in range(TT):
                            for hh in range(2):
                                mm = pe.matmul(bank[4 + 2 * t + hh][:, :], sS[0:SLOTS, 0, t * P:(t + 1) * P],
                                               yS[0:SLOTS, 0, hh * 512:(hh + 1) * 512], start=False, stop=False,
                                               skip_group_check=True)
                        mm.then_inc(o_out[l], 1)

            pe.wait_ge(consts_made, CONSTS_N)
            pe.wait_ge(fold_ready, 1)
            for l in range(DEPTH):
                turn_x("tr", l, 2 * l)
                wait_read(pe, "tr", l, 2)
                wait_read(pe, "tr", l, 3)
                for name in ("qs", "ks"):
                    wait_unit(pe, name, l)
                    for j in range(2):
                        blocks(name, l, name, 0, (name, l, j), j)
                wait_unit(pe, "vs", l)
                for t in range(TT):
                    natural("vs", l, t)
                wait_read(pe, "qs", l, 1)
                wait_read(pe, "ks", l, 1)
                for j in range(6):
                    ps = begin("z", l, j)
                    per = 2 if j < 4 else 4
                    h0 = 2 * j if j < 4 else 4 * (j - 4)
                    q0, k0 = (0, 0) if j < 4 else (P, P)
                    nq = T - q0
                    for i in range(per):
                        h = head_at(h0 + i)
                        r0 = SBD * (h % 2)
                        mm = pe.matmul(ps[:, i * nq:(i + 1) * nq], ksT[r0:r0 + SBD, h // 2, k0:k0 + P],
                                       qsT[r0:r0 + SBD, h // 2, q0:T], start=True, stop=True)
                    mm.then_inc(pe_done, 1)
                for name in ("hc", "bg", "cg"):
                    wait_unit(pe, name, l)
                    for j in range(2):
                        blocks(name, l, name, 0, (name, l, j), j)
                wait_unit(pe, "lat", l)
                for t in range(TT):
                    natural("lat", l, t)
                pe.wait_ge(lat_ready, l + 1)
                for j in range(2):
                    ps = begin("latT", l, j)
                    for i, c in enumerate((0, 1) if j == 0 else (2,)):
                        for t in range(TT):
                            mm = pe.transpose(ps[:, (TT * i + t) * P:(TT * i + t + 1) * P],
                                              lat[:, t, c * P:(c + 1) * P], ident[:])
                    mm.then_inc(pe_done, 1)
                pe.wait_ge(l_ready, l + 1)
                for j in range(6):
                    ps = begin("cum", l, j)
                    if j < 4:
                        pe.matmul(ps[:, :], low[:], l0[:, 2 * j:2 * j + 2, :], start=True, stop=False)
                        mm = pe.matmul(ps[:, :].rearrange("p (h q) -> p h q", h=2)[:, :, P:T], ones[:],
                                       l1[:, 2 * j:2 * j + 2, :], start=False, stop=True)
                    else:
                        mm = pe.matmul(ps[:, :], low[:], l1[:, 4 * (j - 4):4 * (j - 3), :], start=True, stop=True)
                    mm.then_inc(pe_done, 1)
                pe.wait_ge(conv_ready, l + 1)
                gate_and_y(l, 0, yc)
                wait_unit(pe, "wu", l)
                for j in range(4):
                    ps = begin("q", l, j)
                    t, hh = j // 2, j % 2
                    for c in range(2):
                        mm = pe.matmul(ps[:, 0:4 * QK], latT[:, c, t * P:(t + 1) * P],
                                       wuq(l)[:, c, hh * 4 * QK:(hh + 1) * 4 * QK], start=c == 0, stop=c == 1)
                    mm.then_inc(pe_done, 1)
                for j in range(4):
                    ps = begin("kv", l, j)
                    t, hh = j // 2, j % 2
                    pe.matmul(ps[:, :], latT[:, 2, t * P:(t + 1) * P], wukv(l)[:, hh * 512:(hh + 1) * 512],
                              start=True, stop=True).then_inc(pe_done, 1)
                pe.wait_ge(rope_q, l + 1)
                turn_heads("qT", l, qn)
                pe.wait_ge(rope_k, l + 1)
                for j in range(2):
                    ps = begin("pvs", l, j)
                    for i in range(4):
                        h = 4 * j + i
                        if i % 2 == 0:
                            pe.wait_ge(a_ready, 2 * l + 2)
                        o = ps[SBD * (h % 2):SBD * (h % 2) + SBD, (i // 2) * T:(i // 2 + 1) * T]
                        pe.matmul(o, vs[:, 0, h * SBD:(h + 1) * SBD], l0[:, place_of(h), :], start=True, stop=False)
                        mm = pe.matmul(o[:, P:T], vs[:, 1, h * SBD:(h + 1) * SBD], l1[:, place_of(h), :], start=False, stop=True)
                    mm.then_inc(pe_done, 1)
                turn_heads("kT", l, kn)
                wait_read(pe, "qT", l, 3)
                wait_read(pe, "kT", l, 3)
                for j in range(6):
                    ps = begin("s", l, j)
                    per = 4 if j < 2 else 2
                    h0 = 4 * j if j < 2 else 2 * (j - 2)
                    t, nk = (0, P) if j < 2 else (1, T)
                    for i in range(per):
                        mm = pe.matmul(ps[:, i * nk:(i + 1) * nk], qT[0:QK, h0 + i, t * P:(t + 1) * P],
                                       kT[0:QK, h0 + i, 0:nk], start=True, stop=True)
                    mm.then_inc(pe_done, 1)
                wait_read(pe, "pvs", l, 1)
                gate_and_y(l, 2, osT)
                pe.wait_ge(pn_ready, l + 1)
                for j in range(6):
                    ps = begin("pT", l, j)
                    for i in range(4):
                        h = 4 * (j % 2) + i
                        src = (z1[:, h, :], z0[:, h, 0:P], z0[:, h, P:T])[j // 2]
                        mm = pe.transpose(ps[:, i * P:(i + 1) * P], src, ident[:])
                    mm.then_inc(pe_done, 1)
                wait_read(pe, "pT", l, 4)
                wait_read(pe, "pT", l, 5)
                for j in range(2):
                    ps = begin("pvm", l, j)
                    for i in range(4):
                        h = 4 * j + i
                        o = ps[VD * (h % 2):VD * (h % 2) + VD, (i // 2) * T:(i // 2 + 1) * T]
                        pe.matmul(o, vn[:, 0, h * VD:(h + 1) * VD], pt0[:, h, :], start=True, stop=False)
                        mm = pe.matmul(o[:, P:T], vn[:, 1, h * VD:(h + 1) * VD], pt1[:, h, :], start=False, stop=True)
                    mm.then_inc(pe_done, 1)
                wait_read(pe, "pvm", l, 1)
                gate_and_y(l, 1, omT)
                pe.wait_ge(merged_ready, l + 1)
                wait_unit(pe, "wo", l, 0)
                wait_unit(pe, "wo", l, 1)
                mT = xn[:, :, :].rearrange("p t (c n) -> p (t c) n", n=T)
                for j in range(4):
                    ps = begin("wo", l, j)
                    t, hh = j // 2, j % 2
                    for c in range(DC):
                        w = rows_unit("wo", l, c // 4)
                        mm = pe.matmul(ps[:, :], mT[:, c, t * P:(t + 1) * P], w[:, c % 4, hh * 512:(hh + 1) * 512],
                                       start=c == 0, stop=c == DC - 1)
                    mm.then_inc(pe_done, 1)

                turn_x("tr2", l, 2 * l + 1)
                wait_read(pe, "tr2", l, 2)
                wait_read(pe, "tr2", l, 3)
                ps = begin("route", l)
                for t in range(TT):
                    for c in range(DC):
                        mm = pe.matmul(ps[:, t * 64:t * 64 + NG + E], hT[:, c, t * P:(t + 1) * P], wr[l][:, c, :],
                                       start=c == 0, stop=c == DC - 1)
                mm.then_inc(pe_done, 1)
                pe.wait_ge(member_ready, l + 1)
                ps = begin("rank", l)
                pe.matmul(ps[:, 0:E], before[:], member[:, 0, :], start=True, stop=True)
                pe.matmul(ps[:, E:2 * E], ones[:], member[:, 0, :], start=True, stop=False)
                pe.matmul(ps[:, E:2 * E], before[:], member[:, 1, :], start=False, stop=True)
                pe.matmul(ps[:, 2 * E:3 * E], ones[:], member[:, 0, :], start=True, stop=False)
                pe.matmul(ps[:, 2 * E:3 * E], ones[:], member[:, 1, :], start=False, stop=True).then_inc(pe_done, 1)
                pe.wait_ge(p_ready, 2 * l + 2)
                for pr in range(QUADS):
                    if pr == MIDDLE:
                        further_blocks(l)
                    x_e = xe[pr % 2]
                    for b in range(2):
                        ps = begin("gather", l, pr, b)
                        for cc in range(GD):
                            c = GD * b + cc
                            for t in range(TT):
                                mm = pe.matmul(ps[:, cc * P:(cc + 1) * P], xn[:, t, c * P:(c + 1) * P],
                                               Ps[:, t, QE * pr:QE * pr + QE, :], start=t == 0, stop=t == TT - 1)
                        mm.then_inc(pe_done, 1)
                    pe.wait_ge(pw_ready, 2 * (QUADS * l + pr) + 2)
                    ps = begin("sT", l, pr)
                    for t in range(TT):
                        mm = pe.transpose(ps[:, t * P:(t + 1) * P], PW[pr % 2][:, t, :, :], ident[:])
                    mm.then_inc(pe_done, 1)
                    wait_read(pe, "gather", l, pr, 0)
                    wait_read(pe, "gather", l, pr, 1)
                    for e in range(QE):
                        wait_unit(pe, "gu", l, QE * pr + e)
                    ps = begin("gu", l, pr)
                    for c in range(DC):
                        for g in range(2):
                            for e in range(QE):
                                s = e * SLOTS
                                mm = pe.matmul(ps[e * SLOTS:(e + 1) * SLOTS, g * FE:(g + 1) * FE],
                                               x_e[:, c, s:s + SLOTS], gu_unit(l, QE * pr + e)[:, g, c, :],
                                               start=c == 0 and g == 0, stop=c == DC - 1,
                                               skip_group_check=True)
                    mm.then_inc(pe_done, 1)
                    wait_read(pe, "gu", l, pr)
                    ps = begin("guT", l, pr)
                    for g in range(2):
                        for c in range(FC):
                            mm = pe.transpose(ps[:, (FC * g + c) * P:(FC * g + c + 1) * P],
                                              gus[:, pr % 2, g * FE + c:(g + 1) * FE:FC], ident[:])
                    mm.then_inc(pe_done, 1)
                    wait_read(pe, "guT", l, pr)
                    wait_unit(pe, "dn", l, 2 * pr)
                    wait_unit(pe, "dn", l, 2 * pr + 1)
                    for hh in range(2):
                        ps = begin("down", l, pr, hh)
                        for c in range(FC):
                            for e in range(QE):
                                mm = pe.matmul(ps[e * SLOTS:(e + 1) * SLOTS, :],
                                               aT[:, pr % 2, c, 3, e * SLOTS:(e + 1) * SLOTS],
                                               dn_unit(l, 2 * pr + e // 2)[:, e % 2, c, hh * 512:(hh + 1) * 512],
                                               start=c == 0, stop=c == FC - 1, skip_group_check=True)
                        mm.then_inc(pe_done, 1)
                    wait_read(pe, "down", l, pr, 0)
                    wait_read(pe, "down", l, pr, 1)
                    wait_read(pe, "sT", l, pr)
                    for j in range(4):
                        if pr == 0:
                            begin("moe", l, j)
                        t, hh = j // 2, j % 2
                        mm = pe.matmul(B("moe", l, j)[:, :], sS[:, pr % 2, t * P:(t + 1) * P],
                                       yS[:, pr % 2, hh * 512:(hh + 1) * 512],
                                       start=pr == 0, stop=pr == QUADS - 1, skip_group_check=True)
                        if pr == QUADS - 1:
                            mm.then_inc(pe_done, 1)

        @block.scalar
        def _(act):
            steps = [0]
            reads = [0]

            def link(ins):
                steps[0] += 1
                ins.then_inc(act_step, 1)
                act.wait_ge(act_step, steps[0])

            def done(ins, *key):
                reads[0] += 1
                assert jobs[key][2:4] == ("act", reads[0]), key
                ins.then_inc(act_freed, 1)

            def rms(n, parts, width, signal):
                for src, junk, k in parts:
                    last = act.activation(junk, src, ACT.Square, accum_out=nst[:, n, k:k + 1])
                link(last)
                for a, b, w in width:
                    last = act.activation(nst[:, n + 1, a:b], nst[:, n, a:b], ACT.Ln, scale=1.0 / w, bias=epst[:, 0:1])
                link(last)
                k = width[-1][1]
                act.activation(nst[:, n + 2, 0:k], nst[:, n + 1, 0:k], ACT.Exp, scale=-0.5).then_inc(signal, 1)

            def norm_x():
                rms(0, [(xs[:, t, :], xn[:, t, :], t) for t in range(TT)], [(0, TT, D)], ss_ready)

            def copy_pair(name, l, dst, scale=1.0):
                for j in range(2):
                    wait_pe(act, name, l, j)
                    done(act.activation(dst[:, 2 * j:2 * j + 2, :], B(name, l, j)[:, :], ACT.Copy, scale=scale), name, l, j)

            def turned(name, l, g):
                for j in (1, 3):
                    wait_pe(act, name, l, j)
                    for cc in range(2):
                        c = 2 * j + cc
                        ins = act.activation(hT[:, c, :], B(name, l, j)[:, cc * T:(cc + 1) * T], ACT.Copy,
                                             scale=gains[l][:, g, c:c + 1])
                    done(ins, name, l, j)

            def gates(l, b):
                for j in range(4):
                    n = 12 * l + 4 * (0, 2, 1)[b] + j
                    wait_pe(act, "gate", l, b, j)
                    if n >= 2:
                        act.wait_ge(sig_used, n - 1)
                    for bb in range(2):
                        c = 8 * b + 2 * j + bb
                        ins = act.activation(sig[:, n % 2, bb * T:(bb + 1) * T], B("gate", l, b, j)[:, bb * T:(bb + 1) * T],
                                             ACT.Exp, scale=-1.0, bias=nbg[l][:, c:c + 1])
                    done(ins, "gate", l, b, j)

            def further_blocks(l):
                act.wait_ge(flag_ready, l + 1)
                n_more = act.value_load(flag_i[0:1, l:l + 1], min_val=0, max_val=E * MORE)
                with act.If(n_more != 0):
                    with act.Fori(0, n_more, 1) as i:
                        act.wait_ge(o_gathered[l], i + 1)
                        act.activation(sS[0:SLOTS, 0, :], bank[1][0:SLOTS, 0:T], ACT.Copy)
                        act.wait_ge(o_gu_done[l], i + 1)
                        act.activation(gus[:, 0, :], bank[2][:, :], ACT.Copy).then_inc(o_gu_read[l], 1)
                        act.wait_ge(o_turned[l], i + 1)
                        act.activation(aT[:, 0, :, 0, 0:SLOTS], bank[3][:, 0:FC * SLOTS].rearrange("p (c s) -> p c s", c=FC),
                                       ACT.Exp, scale=-1.0).then_inc(o_exp[l], 1)
                        act.wait_ge(o_down[l], i + 1)
                        for hh in range(2):
                            ins = act.activation(yS[0:SLOTS, 0, hh * 512:(hh + 1) * 512], bank[hh][0:SLOTS, :], ACT.Copy)
                        ins.then_inc(o_y_ready[l], 1)

            act.wait_ge(angles_ready, 1)
            act.activation(sinn[:], ang[:, 0, :, :], ACT.Sin)
            act.activation(cosn[:], ang[:, 1, :, :], ACT.Sin).then_inc(rope_ready, 1)
            act.wait_ge(const_ready, 1)
            act.wait_ge(x_landed, 16)
            for l in range(DEPTH):
                if l:
                    act.wait_ge(x_ready, 2 * l)
                norm_x()
                act.wait_ge(const_ready, 2 + l)
                turned("tr", l, 0)
                copy_pair("qs", l, qsT, SBD ** -0.5)
                copy_pair("ks", l, ksT)
                for j in range(6):
                    wait_pe(act, "z", l, j)
                    dst = z0[:, 2 * j:2 * j + 2, :] if j < 4 else z1[:, 4 * (j - 4):4 * (j - 3), :]
                    done(act.activation(dst, B("z", l, j)[:, :], ACT.Copy), "z", l, j)
                act.wait_ge(z_abs, l + 1)
                act.activation(l0[:, :, :], l0[:, :, :], ACT.Exp)
                link(act.activation(l1[:, :, :], l1[:, :, :], ACT.Exp))
                act.activation(l0[:, :, :], l0[:, :, :], ACT.Ln, bias=1.0)
                act.activation(l1[:, :, :], l1[:, :, :], ACT.Ln, bias=1.0).then_inc(z_sp, 1)
                copy_pair("hc", l, hc)
                copy_pair("bg", l, bg)
                for t in range(TT):
                    wait_pe(act, "lat", l, t)
                    done(act.activation(lat[:, t, :], B("lat", l, t)[:, 0:LAT], ACT.Copy), "lat", l, t)
                act.wait_ge(act_freed, jobs[("lat", l, 1)][3])
                rms(3, [(lat[:, t, c0:c1], latT.rearrange("p c n -> p (c n)")[:, TT * c0 + t * (c1 - c0):TT * c0 + (t + 1) * (c1 - c0)], 2 * i + t)
                        for i, (c0, c1) in enumerate(((0, QR), (QR, QR + KVR))) for t in range(TT)],
                    [(0, 2, QR), (2, 4, KVR)], lat_ss)
                act.wait_ge(arg_ready, l + 1)
                act.activation(l0[:, :, :], z0[:, :, :], ACT.Exp).then_inc(a_ready, 1)
                act.activation(l1[:, :, :], z1[:, :, :], ACT.Exp).then_inc(a_ready, 1)
                gates(l, 0)
                for j in range(4):
                    t, hh = j // 2, j % 2
                    wait_pe(act, "q", l, j)
                    done(act.activation(qn[:, t, 4 * hh:4 * hh + 4, :], B("q", l, j)[:, 0:4 * QK], ACT.Copy), "q", l, j)
                for j in range(4):
                    t, hh = j // 2, j % 2
                    wait_pe(act, "kv", l, j)
                    ps = B("kv", l, j)[:, :].rearrange("p (h d) -> p h d", h=4)
                    act.activation(kn[:, t, 4 * hh:4 * hh + 4, 0:NOPE], ps[:, :, 0:NOPE], ACT.Copy)
                    dst = vn[:, t, hh * 256:(hh + 1) * 256].rearrange("p (h d) -> p h d", h=4)
                    done(act.activation(dst, ps[:, :, NOPE:], ACT.Copy), "kv", l, j)
                for j in range(4):
                    wait_pe(act, "qT", l, j)
                    done(act.activation(qT[0:QK, 2 * j:2 * j + 2, :], B("qT", l, j)[0:QK, :], ACT.Copy), "qT", l, j)
                copy_pair("pvs", l, osT)
                act.wait_ge(ssub_ready, l + 1)
                act.activation(z1[:, :, :], z1[:, :, :], ACT.Exp)
                act.activation(z0[:, :, :], z0[:, :, :], ACT.Exp).then_inc(exp_ready, 1)
                gates(l, 2)
                for j in (1, 3, 5):
                    turned_probs(act, l, j, done, wait_pe, B, pt0, pt1, "act")
                copy_pair("pvm", l, omT)
                gates(l, 1)

                act.wait_ge(x_ready, 2 * l + 1)
                norm_x()
                turned("tr2", l, 1)
                act.wait_ge(rt_a, l + 1)
                act.activation(r4[:, 1, :, :], r4[:, 0, :, :], ACT.Exp)
                act.activation(r1[:, 4, :], r1[:, 3, :], ACT.Exp).then_inc(rt_b, 1)
                for pr in range(QUADS):
                    if pr == MIDDLE:
                        further_blocks(l)
                    wait_pe(act, "gather", l, pr, 1)
                    for cc in range(GD):
                        c = GD + cc
                        ins = act.activation(xe[pr % 2][:, c, :], B("gather", l, pr, 1)[:, cc * P:(cc + 1) * P], ACT.Copy,
                                             scale=gains[l][:, 1, c:c + 1])
                    done(ins, "gather", l, pr, 1)
                    wait_pe(act, "sT", l, pr)
                    done(act.activation(sS[:, pr % 2, :], B("sT", l, pr)[:, 0:T], ACT.Copy), "sT", l, pr)
                    wait_pe(act, "gu", l, pr)
                    done(act.activation(gus[:, pr % 2, :], B("gu", l, pr)[:, :], ACT.Copy), "gu", l, pr)
                    wait_pe(act, "guT", l, pr)
                    act.activation(aT[:, pr % 2, :, 0, :], B("guT", l, pr)[:, 0:FC * P], ACT.Exp,
                                   scale=-1.0).then_inc(eg_ready, 1)
                    wait_pe(act, "down", l, pr, 0)
                    done(act.activation(yS[:, pr % 2, 0:512], B("down", l, pr, 0)[:, :], ACT.Copy), "down", l, pr, 0)
            act.wait_ge(x_ready, 2 * DEPTH)
            rms(0, [(xs[:, t, :], (hT[:, 4:8, :], xn[:, 0, :])[t], t) for t in range(TT)], [(0, TT, D)], ss_ready)

        @block.vector
        def _(dve):
            steps = [0]
            reads = [0]

            def link(ins):
                steps[0] += 1
                ins.then_inc(dve_step, 1)
                dve.wait_ge(dve_step, steps[0])

            def done(ins, *key):
                reads[0] += 1
                assert jobs[key][2:4] == ("dve", reads[0]), key
                ins.then_inc(dve_freed, 1)

            def newton(n, width):
                k = width[-1][1]
                for a, b, w in width:
                    last = dve.tensor_scalar(nst[:, n + 1, a:b], nst[:, n, a:b], 1.0 / w, EPS, ALU.mult, ALU.add)
                link(last)
                link(dve.tensor_tensor(nst[:, n + 1, 0:k], nst[:, n + 1, 0:k], nst[:, n + 2, 0:k], ALU.mult))
                link(dve.tensor_tensor(nst[:, n + 1, 0:k], nst[:, n + 1, 0:k], nst[:, n + 2, 0:k], ALU.mult))
                link(dve.tensor_scalar(nst[:, n + 1, 0:k], nst[:, n + 1, 0:k], -0.5, 1.5, ALU.mult, ALU.add))
                link(dve.tensor_tensor(nst[:, n + 2, 0:k], nst[:, n + 1, 0:k], nst[:, n + 2, 0:k], ALU.mult))

            def norm_x(n):
                dve.wait_ge(ss_ready, n + 1)
                newton(0, [(0, TT, D)])
                for t in range(TT):
                    dve.tensor_scalar(xn[:, t, :].rearrange("q (c p) -> q p c", c=DC), xs[:, t, :].rearrange("q (p c) -> q p c", c=DC),
                                      nst[:, 2, t:t + 1], None, ALU.mult).then_inc(xn_ready, 1)

            def turned(name, l, g):
                for j in (0, 2):
                    wait_pe(dve, name, l, j)
                    for cc in range(2):
                        c = 2 * j + cc
                        ins = dve.tensor_scalar(hT[:, c, :], B(name, l, j)[:, cc * T:(cc + 1) * T],
                                                gains[l][:, g, c:c + 1], None, ALU.mult)
                    done(ins, name, l, j)

            def rotate(x1, x2, t, n):
                c = cosn[:, t, :].unsqueeze(1).to_broadcast([P, n, HALF])
                s = sinn[:, t, :].unsqueeze(1).to_broadcast([P, n, HALF])
                r = [rope_t[:, i, 0:n, :] for i in range(4)]
                dve.tensor_tensor(r[0], x1, c, ALU.mult)
                dve.tensor_tensor(r[1], x2, s, ALU.mult)
                dve.tensor_tensor(r[2], x2, c, ALU.mult)
                link(dve.tensor_tensor(r[3], x1, s, ALU.mult))
                dve.tensor_tensor(x1, r[0], r[1], ALU.subtract)
                last = dve.tensor_tensor(x2, r[2], r[3], ALU.add)
                return last

            def gated(l, b):
                mT = xn[:, :, :].rearrange("p t (c n) -> p (t c) n", n=T)
                for j in range(4):
                    n = 12 * l + 4 * (0, 2, 1)[b] + j
                    s = sig[:, n % 2, :]
                    wait_read(dve, "gate", l, b, j)
                    link(dve.tensor_scalar(s, s, 1.0, None, ALU.add))
                    link(dve.reciprocal(s, s))
                    wait_pe(dve, "y", l, b, j)
                    m = mT[:, 2 * j:2 * j + 2, :]
                    y = B("y", l, b, j)[:, :]
                    sv = s.rearrange("p (a n) -> p a n", a=2)
                    yv = y.rearrange("p (a n) -> p a n", a=2)
                    if b == 0:
                        ins = dve.tensor_tensor(m, sv, yv, ALU.mult)
                        done(ins, "y", l, b, j)
                        steps[0] += 1
                        nop = dve.tensor_copy(nst[:, 7, 0:1], nst[:, 7, 1:2])
                        nop.then_inc(dve_step, 1)
                        dve.wait_ge(dve_freed, reads[0])
                        dve.wait_ge(dve_step, steps[0])
                        dve.tensor_copy(nst[:, 7, 2:3], nst[:, 7, 3:4]).then_inc(sig_used, 1)
                    else:
                        ins = dve.tensor_tensor(sv, sv, yv, ALU.mult)
                        done(ins, "y", l, b, j)
                        dve.wait_ge(dve_freed, reads[0])
                        dve.tensor_tensor(m, m, sv, ALU.add).then_inc(sig_used, 1)

            def choose(l, first):
                k = [0]

                def olink(ins):
                    k[0] += 1
                    ins.then_inc(o_step[l], 1)
                    dve.wait_ge(o_step[l], first + k[0] - 1)

                olink(dve.tensor_scalar(turn, turn, 1.0, None, ALU.add))
                olink(dve.tensor_scalar(o_eq[:, :, :], blk[:, :, :], turn[:, 0:1], None, ALU.is_equal))
                dve.tensor_reduce(o_sel, o_eq.rearrange("p b e -> p e b"), AX.X, ALU.add)
                olink(dve.tensor_tensor(blk_one[:, :, :], o_eq[:, :, :], o_first[:, :, :], ALU.mult))
                dve.tensor_reduce(o_num[:, 0:1], blk_one[:, :, :], AX.XY, ALU.add)
                olink(dve.tensor_tensor(o_eq[:, 0, :], o_sel, iot[:], ALU.mult))
                olink(dve.tensor_reduce(o_num[:, 1:2], o_eq[:, 0, :], AX.X, ALU.add))
                dve.tensor_copy(e_i[:], o_num[:, 1:2]).then_inc(o_chosen[l], 1)
                for q, src in enumerate((rk, comb)):
                    olink(dve.tensor_tensor(o_tmp[:, :, :], src[:, :, :], o_sel.unsqueeze(1).to_broadcast([P, TT, E]), ALU.mult))
                    olink(dve.tensor_reduce(o_rk[:, 2 * q:2 * q + 2], o_tmp[:, :, :], AX.X, ALU.add))
                olink(dve.tensor_scalar(o_rk[:, 0:2], o_rk[:, 0:2], o_num[:, 0:1], None, ALU.subtract))
                for t in range(TT):
                    ins = dve.tensor_scalar(o_P[:, t, :], iot[:], o_rk[:, t:t + 1], None, ALU.is_equal)
                olink(ins)
                for t in range(TT):
                    ins = dve.tensor_scalar(o_PW[:, t, :], o_P[:, t, :], o_rk[:, 2 + t:3 + t], None, ALU.mult)
                ins.then_inc(o_slots[l], 1)
                assert k[0] == CHOICE_STEPS

            def further_blocks(l):
                n_more = dve.value_load(flag_i[0:1, l:l + 1], min_val=0, max_val=E * MORE)
                with dve.If(n_more != 0):
                    with dve.Fori(0, n_more, 1) as i:
                        k = [0]

                        def olink(ins):
                            k[0] += 1
                            ins.then_inc(o_step[l], 1)
                            dve.wait_ge(o_step[l], CHOICE_STEPS + (CHOICE_STEPS + 3) * i + k[0])

                        dve.wait_ge(o_gathered[l], i + 1)
                        dve.tensor_tensor(o_x[:, :, :], bank[0][:, 0:DC * SLOTS].rearrange("p (c s) -> p c s", c=DC),
                                          gains[l][:, 1, :].unsqueeze(2).to_broadcast([P, DC, SLOTS]), ALU.mult).then_inc(o_x_ready[l], 1)
                        dve.wait_ge(o_exp[l], i + 1)
                        a = [aT[:, 0, :, j, 0:SLOTS] for j in range(4)]
                        ps = bank[3][:, 0:2 * FC * SLOTS].rearrange("p (g c s) -> p g c s", g=2, c=FC)
                        olink(dve.tensor_scalar(a[0], a[0], 1.0, None, ALU.add))
                        olink(dve.reciprocal(a[1], a[0]))
                        olink(dve.tensor_tensor(a[2], a[1], ps[:, 0, :, :], ALU.mult))
                        dve.tensor_tensor(a[3], a[2], ps[:, 1, :, :], ALU.mult).then_inc(o_act[l], 1)
                        dve.wait_ge(o_out[l], i + 1)
                        choose(l, CHOICE_STEPS + (CHOICE_STEPS + 3) * i + 3 + 1)

            dve.memset(epst[:], EPS)
            link(dve.memset(nst[:], 0.0))
            dve.wait_ge(consts_made, CONSTS_N)
            dve.tensor_reduce(fold[:], ident[:, :].rearrange("p (j s) -> p s j", j=QE), AX.X, ALU.add).then_inc(fold_ready, 1)
            dve.wait_ge(iota_made, 1)
            link(dve.tensor_copy(iot[:], iot_i[:]))
            dve.wait_ge(once_landed, 32)
            link(dve.tensor_copy(posf[:], pos_i[:]))
            for t in range(TT):
                last = dve.tensor_scalar(ang[:, 0, t, :], frq[:], posf[:, t:t + 1], None, ALU.mult)
            link(last)
            for i, shift in ((1, 0.25), (0, 0.0)):
                k, a = ang2[:, i, :, :], ang[:, i, :, :]
                link(dve.tensor_scalar(k, ang[:, 0, :, :], float(np.float32(1 / TWO_PI)), shift, ALU.mult, ALU.add))
                link(dve.tensor_scalar(k, k, MAGIC, None, ALU.add))
                link(dve.tensor_scalar(k, k, -MAGIC, None, ALU.add))
                link(dve.scalar_tensor_tensor(out=a, in0=k, scalar=-C1, in1=ang[:, 0, :, :], op0=ALU.mult, op1=ALU.add))
                link(dve.scalar_tensor_tensor(out=a, in0=k, scalar=-C2, in1=a, op0=ALU.mult, op1=ALU.add))
                link(dve.scalar_tensor_tensor(out=a, in0=k, scalar=-C3, in1=a, op0=ALU.mult, op1=ALU.add))
                link(dve.tensor_scalar(a, a, float(np.float32(np.pi / 2)) if i else 0.0, PI_LOW, ALU.add, ALU.min))
                last = dve.tensor_scalar(a, a, -PI_LOW, None, ALU.max)
                link(last)
            dve.tensor_copy(nst[:, 6, 0:1], nst[:, 6, 1:2]).then_inc(angles_ready, 1)
            dve.tensor_copy(nst[:, 6, 2:3], nst[:, 6, 3:4]).then_inc(const_ready, 1)
            dve.wait_ge(rope_ready, 1)
            dve.wait_ge(consts_made, CONSTS_N)

            for l in range(DEPTH):
                dve.wait_ge(small_landed[l], 16 * SMALL)
                dve.tensor_scalar(nbg[l][:], nbg[l][:], -1.0, None, ALU.mult).then_inc(const_ready, 1)
                norm_x(2 * l)
                turned("tr", l, 0)
                for t in range(TT):
                    wait_pe(dve, "vs", l, t)
                    done(dve.tensor_copy(vs[:, t, :], B("vs", l, t)[:, :]), "vs", l, t)
                wait_read(dve, "z", l, 5)
                dve.scalar_tensor_tensor(out=l0[:, :, :], in0=z0[:, :, :], scalar=-1.0, in1=z0[:, :, :], op0=ALU.mult, op1=ALU.min)
                dve.scalar_tensor_tensor(out=l1[:, :, :], in0=z1[:, :, :], scalar=-1.0, in1=z1[:, :, :], op0=ALU.mult, op1=ALU.min).then_inc(z_abs, 1)
                dve.wait_ge(z_sp, l + 1)
                dve.scalar_tensor_tensor(out=l0[:, :, :], in0=z0[:, :, :], scalar=0.0, in1=l0[:, :, :], op0=ALU.max, op1=ALU.add)
                link(dve.scalar_tensor_tensor(out=l1[:, :, :], in0=z1[:, :, :], scalar=0.0, in1=l1[:, :, :], op0=ALU.max, op1=ALU.add))
                keep = before[:, :].unsqueeze(1).to_broadcast([P, H, P])
                dve.scalar_tensor_tensor(out=l0[:, :, 0:P], in0=l0[:, :, 0:P], scalar=-1.0, in1=keep, op0=ALU.mult, op1=ALU.mult)
                dve.tensor_scalar(l0[:, :, P:T], l0[:, :, P:T], -1.0, None, ALU.mult)
                dve.scalar_tensor_tensor(out=l1[:, :, :], in0=l1[:, :, :], scalar=-1.0, in1=keep, op0=ALU.mult, op1=ALU.mult).then_inc(l_ready, 1)
                hide = tneg[:, :].unsqueeze(1).to_broadcast([P, H, P])
                dve.tensor_tensor(z0[:, :, 0:P], z0[:, :, 0:P], hide, ALU.add)
                link(dve.tensor_tensor(z1[:, :, :], z1[:, :, :], hide, ALU.add))
                for j in range(2):
                    wait_read(dve, "hc", l, j)
                    wait_pe(dve, "cg", l, j)
                    m = hc[:, 2 * j:2 * j + 2, :]
                    ins = dve.tensor_tensor(m, m, B("cg", l, j)[:, :].rearrange("p (a n) -> p a n", a=2), ALU.mult)
                    done(ins, "cg", l, j)
                dve.wait_ge(dve_freed, reads[0])
                for c in range(CB):
                    last = dve.tensor_scalar(yc[:, c, :], hc[:, c, :], cw[l][:, 2, c:c + 1], None, ALU.mult)
                link(last)
                for k in (1, 0):
                    s = 2 - k
                    for c in range(CB):
                        last = dve.scalar_tensor_tensor(out=yc[:, c, s:T], in0=hc[:, c, 0:T - s], scalar=cw[l][:, k, c:c + 1],
                                                        in1=yc[:, c, s:T], op0=ALU.mult, op1=ALU.add)
                    link(last)
                wait_read(dve, "bg", l, 1)
                dve.tensor_tensor(yc[:, :, :], yc[:, :, :], bg[:, :, :], ALU.mult).then_inc(conv_ready, 1)
                dve.wait_ge(lat_ss, l + 1)
                newton(3, [(0, 2, QR), (2, 4, KVR)])
                for t in range(TT):
                    dve.tensor_scalar(lat[:, t, 0:QR], lat[:, t, 0:QR], nst[:, 5, t:t + 1], None, ALU.mult)
                    last = dve.tensor_scalar(lat[:, t, QR:QR + KVR], lat[:, t, QR:QR + KVR], nst[:, 5, 2 + t:3 + t], None, ALU.mult)
                last.then_inc(lat_ready, 1)
                for t in range(TT):
                    kr0 = lat[:, t, QR + KVR:LAT].rearrange("p (a n) -> p a n", a=2)
                    link(rotate(kr0[:, 0:1, :], kr0[:, 1:2, :], t, 1))
                for j in range(2):
                    wait_pe(dve, "latT", l, j)
                    for i, c in enumerate((0, 1) if j == 0 else (2,)):
                        ins = dve.tensor_scalar(latT[:, c, :], B("latT", l, j)[:, i * T:(i + 1) * T], lgain[l][:, c:c + 1], None, ALU.mult)
                    done(ins, "latT", l, j)
                for j in range(6):
                    wait_pe(dve, "cum", l, j)
                    m = z0[:, 2 * j:2 * j + 2, :] if j < 4 else z1[:, 4 * (j - 4):4 * (j - 3), :]
                    ins = dve.tensor_tensor(m, m, B("cum", l, j)[:, :].rearrange("p (a n) -> p a n", a=2 if j < 4 else 4), ALU.add)
                    done(ins, "cum", l, j)
                dve.wait_ge(dve_freed, reads[0])
                dve.tensor_copy(nst[:, 6, 0:1], nst[:, 6, 1:2]).then_inc(arg_ready, 1)
                gated(l, 0)
                wait_read(dve, "q", l, 3)
                for t in range(TT):
                    link(rotate(qn[:, t, :, NOPE:NOPE + HALF], qn[:, t, :, NOPE + HALF:QK], t, H))
                dve.tensor_copy(nst[:, 6, 0:1], nst[:, 6, 1:2]).then_inc(rope_q, 1)
                wait_read(dve, "kv", l, 3)
                for t in range(TT):
                    last = dve.tensor_copy(kn[:, t, :, NOPE:QK], lat[:, t, QR + KVR:LAT].unsqueeze(1).to_broadcast([P, H, ROPE]))
                last.then_inc(rope_k, 1)
                for j in range(4):
                    wait_pe(dve, "kT", l, j)
                    done(dve.tensor_copy(kT[0:QK, 2 * j:2 * j + 2, :], B("kT", l, j)[0:QK, :].rearrange("p (a n) -> p a n", a=2)), "kT", l, j)
                scale = QK ** -0.5
                for j in range(6):
                    wait_pe(dve, "s", l, j)
                    per, nk = (4, P) if j < 2 else (2, T)
                    ps = B("s", l, j)[:, :].rearrange("p (h k) -> p h k", h=per)
                    dst = z1[:, 4 * j:4 * j + 4, :] if j < 2 else z0[:, 2 * (j - 2):2 * (j - 1), :]
                    if j >= 2:
                        dve.tensor_scalar(dst[:, :, 0:P], ps[:, :, 0:P], scale, None, ALU.mult)
                    done(dve.scalar_tensor_tensor(out=dst[:, :, nk - P:nk], in0=ps[:, :, nk - P:nk], scalar=scale,
                                                  in1=mneg[:, :].unsqueeze(1).to_broadcast([P, per, P]),
                                                  op0=ALU.mult, op1=ALU.add), "s", l, j)
                dve.wait_ge(dve_freed, reads[0])
                mx = rope_t[:, 0, :, 0:2]
                dve.tensor_reduce(mx[:, :, 0:1], z1[:, :, :], AX.X, ALU.max)
                link(dve.tensor_reduce(mx[:, :, 1:2], z0[:, :, :], AX.X, ALU.max))
                dve.tensor_tensor(z1[:, :, :], z1[:, :, :], mx[:, :, 0:1].to_broadcast([P, H, P]), ALU.subtract)
                dve.tensor_tensor(z0[:, :, :], z0[:, :, :], mx[:, :, 1:2].to_broadcast([P, H, T]), ALU.subtract).then_inc(ssub_ready, 1)
                gated_first = 2
                dve.wait_ge(exp_ready, l + 1)
                dve.tensor_reduce(mx[:, :, 0:1], z1[:, :, :], AX.X, ALU.add)
                link(dve.tensor_reduce(mx[:, :, 1:2], z0[:, :, :], AX.X, ALU.add))
                link(dve.reciprocal(rope_t[:, 1, :, 0:2], mx))
                rc = rope_t[:, 1, :, :]
                dve.tensor_tensor(z1[:, :, :], z1[:, :, :], rc[:, :, 0:1].to_broadcast([P, H, P]), ALU.mult)
                dve.tensor_tensor(z0[:, :, :], z0[:, :, :], rc[:, :, 1:2].to_broadcast([P, H, T]), ALU.mult).then_inc(pn_ready, 1)
                gated(l, gated_first)
                for j in (0, 2, 4):
                    turned_probs(dve, l, j, done, wait_pe, B, pt0, pt1, "dve")
                gated(l, 1)
                dve.wait_ge(sig_used, 12 * l + 12)
                dve.tensor_copy(nst[:, 6, 0:1], nst[:, 6, 1:2]).then_inc(merged_ready, 1)
                for j in range(4):
                    t, hh = j // 2, j % 2
                    wait_pe(dve, "wo", l, j)
                    m = xs[:, t, hh * 512:(hh + 1) * 512]
                    done(dve.tensor_tensor(m, m, B("wo", l, j)[:, :], ALU.add), "wo", l, j)
                dve.wait_ge(dve_freed, reads[0])
                dve.tensor_copy(nst[:, 6, 0:1], nst[:, 6, 1:2]).then_inc(x_ready, 1)

                norm_x(2 * l + 1)
                turned("tr2", l, 1)
                wait_pe(dve, "route", l)
                done(dve.tensor_tensor(lg[:, :, :], B("route", l)[:, 0:TT * 64].rearrange("p (t n) -> p t n", t=TT)[:, :, 0:NG + E],
                                       rbias[l][:, :].unsqueeze(1).to_broadcast([P, TT, NG + E]), ALU.add), "route", l)
                dve.wait_ge(dve_freed, reads[0])

                def bc(a, n):
                    return a.unsqueeze(2).to_broadcast([P, TT, n])

                def first_of(dst, at, top, n, tmp):
                    link(dve.tensor_tensor(tmp, at, bc(top, n), ALU.is_equal))
                    link(dve.tensor_tensor(tmp, tmp, countdown[n], ALU.mult))
                    link(dve.tensor_reduce(r1[:, 11, :], tmp, AX.X, ALU.max))
                    link(dve.tensor_tensor(dst, tmp, bc(r1[:, 11, :], n), ALU.is_equal))

                link(dve.tensor_scalar(r8[:, 9, 0, :], iot[:, 0:EPG], -1.0, float(EPG), ALU.mult, ALU.add))
                link(dve.tensor_scalar(r4[:, 7, 0, :], iot[:, 0:NG], -1.0, float(NG), ALU.mult, ALU.add))
                countdown = {EPG: r8[:, 9, 0:1, :].to_broadcast([P, TT, EPG]), NG: r4[:, 7, 0:1, :].to_broadcast([P, TT, NG])}
                link(dve.tensor_reduce(r1[:, 0, :], lg[:, :, 0:NG], AX.X, ALU.max))
                link(dve.tensor_tensor(r4[:, 0, :, :], lg[:, :, 0:NG], bc(r1[:, 0, :], NG), ALU.subtract))
                first_of(r4[:, 2, :, :], lg[:, :, 0:NG], r1[:, 0, :], NG, r4[:, 3, :, :])
                for g in range(NG):
                    ge = lg[:, :, NG + EPG * g:NG + EPG * (g + 1)]
                    link(dve.tensor_tensor(r8[:, 0 if g == 0 else 1, :, :], ge, bc(r4[:, 2, :, g], EPG), ALU.mult))
                    if g:
                        link(dve.tensor_tensor(r8[:, 0, :, :], r8[:, 0, :, :], r8[:, 1, :, :], ALU.add))
                link(dve.tensor_reduce(r1[:, 1, :], r8[:, 0, :, :], AX.X, ALU.max))
                first_of(r8[:, 2, :, :], r8[:, 0, :, :], r1[:, 1, :], EPG, r8[:, 3, :, :])
                link(dve.scalar_tensor_tensor(out=r8[:, 4, :, :], in0=r8[:, 2, :, :], scalar=NEG, in1=r8[:, 0, :, :],
                                              op0=ALU.mult, op1=ALU.add))
                link(dve.tensor_reduce(r1[:, 2, :], r8[:, 4, :, :], AX.X, ALU.max))
                first_of(r8[:, 5, :, :], r8[:, 4, :, :], r1[:, 2, :], EPG, r8[:, 3, :, :])
                dve.tensor_tensor(r1[:, 3, :], r1[:, 2, :], r1[:, 1, :], ALU.subtract).then_inc(rt_a, 1)
                link(dve.tensor_tensor(r8[:, 6, :, :], r8[:, 2, :, :], r8[:, 5, :, :], ALU.add))
                for g in range(NG):
                    last = dve.tensor_tensor(member[:, :, EPG * g:EPG * (g + 1)], r8[:, 6, :, :], bc(r4[:, 2, :, g], EPG), ALU.mult)
                last.then_inc(member_ready, 1)
                dve.wait_ge(rt_b, l + 1)
                link(dve.tensor_reduce(r1[:, 5, :], r4[:, 1, :, :], AX.X, ALU.add))
                link(dve.tensor_scalar(r1[:, 6, :], r1[:, 4, :], 1.0, None, ALU.add))
                link(dve.tensor_tensor(r1[:, 7, :], r1[:, 5, :], r1[:, 6, :], ALU.mult))
                link(dve.reciprocal(r1[:, 8, :], r1[:, 7, :]))
                link(dve.tensor_tensor(r8[:, 7, :, :], r8[:, 5, :, :], bc(r1[:, 4, :], EPG), ALU.mult))
                link(dve.tensor_tensor(r8[:, 7, :, :], r8[:, 7, :, :], r8[:, 2, :, :], ALU.add))
                link(dve.tensor_tensor(r8[:, 8, :, :], r8[:, 7, :, :], bc(r1[:, 8, :], EPG), ALU.mult))
                for g in range(NG):
                    last = dve.tensor_tensor(comb[:, :, EPG * g:EPG * (g + 1)], r8[:, 8, :, :], bc(r4[:, 2, :, g], EPG), ALU.mult)
                link(last)
                wait_pe(dve, "rank", l)
                dve.tensor_copy(count, B("rank", l)[:, TT * E:TT * E + E])
                done(dve.scalar_tensor_tensor(out=rk[:, :, :], in0=B("rank", l)[:, 0:TT * E].rearrange("p (t n) -> p t n", t=TT),
                                              scalar=1.0, in1=member[:, :, :], op0=ALU.add, op1=ALU.mult), "rank", l)
                dve.wait_ge(dve_freed, reads[0])
                link(dve.tensor_scalar(rk[:, :, :], rk[:, :, :], -1.0, None, ALU.add))
                for t in range(TT):
                    dve.tensor_tensor(Ps[:, t, :, :], iot[:, :].unsqueeze(1).to_broadcast([P, E, SLOTS]),
                                      rk[:, t, :].unsqueeze(2).to_broadcast([P, E, SLOTS]), ALU.is_equal).then_inc(p_ready, 1)
                for b in range(MORE):
                    dve.tensor_scalar(blk_one[:, b, :], count, float(SLOTS * (b + 1)), None, ALU.is_gt)
                    last = dve.memset(o_first[:, b, :], float(SLOTS * (b + 1)))
                link(last)
                flat = [a.rearrange("p b e -> p (b e)") for a in (blk_one, blk)]
                link(dve.tensor_tensor_scan(flat[1], ones_row, flat[0], 0.0, ALU.mult, ALU.add))
                dve.tensor_copy(flag_i[:, l:l + 1], flat[1][:, MORE * E - 1:MORE * E]).then_inc(flag_ready, 1)
                link(dve.tensor_tensor(o_eq[:, :, :], blk[:, :, :], blk_one[:, :, :], ALU.mult))
                dve.tensor_copy(blk[:, :, :], o_eq[:, :, :])
                link(dve.memset(turn, 0.0))
                choose(l, 1)
                for pr in range(QUADS):
                    if pr == MIDDLE:
                        further_blocks(l)
                    wait_pe(dve, "gather", l, pr, 0)
                    done(dve.tensor_tensor(xe[pr % 2][:, 0:GD, :], B("gather", l, pr, 0)[:, :].rearrange("p (c s) -> p c s", c=GD),
                                           gains[l][:, 1, 0:GD].unsqueeze(2).to_broadcast([P, GD, P]), ALU.mult), "gather", l, pr, 0)
                    a = aT[:, pr % 2, :, :, :]
                    ps = B("guT", l, pr)[:, :].rearrange("p (g c s) -> p g c s", g=2, c=FC)
                    dve.wait_ge(eg_ready, QUADS * l + pr + 1)
                    link(dve.tensor_scalar(a[:, :, 0, :], a[:, :, 0, :], 1.0, None, ALU.add))
                    link(dve.reciprocal(a[:, :, 1, :], a[:, :, 0, :]))
                    link(dve.tensor_tensor(a[:, :, 2, :], a[:, :, 1, :], ps[:, 0, :, :], ALU.mult))
                    done(dve.tensor_tensor(a[:, :, 3, :], a[:, :, 2, :], ps[:, 1, :, :], ALU.mult), "guT", l, pr)
                    wait_pe(dve, "down", l, pr, 1)
                    done(dve.tensor_copy(yS[:, pr % 2, 512:D], B("down", l, pr, 1)[:, :]), "down", l, pr, 1)
                for j in range(4):
                    t, hh = j // 2, j % 2
                    wait_pe(dve, "moe", l, j)
                    m = xs[:, t, hh * 512:(hh + 1) * 512]
                    done(dve.tensor_tensor(m, m, B("moe", l, j)[:, :], ALU.add), "moe", l, j)
                dve.wait_ge(dve_freed, reads[0])
                dve.tensor_copy(nst[:, 6, 0:1], nst[:, 6, 1:2]).then_inc(x_ready, 1)

            dve.wait_ge(ss_ready, 2 * DEPTH + 1)
            newton(0, [(0, TT, D)])
            dve.wait_ge(final_landed, 16)
            for t in range(TT):
                dve.scalar_tensor_tensor(out=xs[:, t, :], in0=xs[:, t, :], scalar=nst[:, 2, t:t + 1], in1=fgain,
                                         op0=ALU.mult, op1=ALU.mult).then_inc(xn_ready, 1)


CHOICE_STEPS = 11
SMALL = 12
CONSTS_N = 11
CONSTS = [0]


def turned_probs(eng, l, j, done, wait_pe, B, pt0, pt1, by):
    wait_pe(eng, "pT", l, j)
    h0 = 4 * (j % 2)
    dst = (pt0[:, h0:h0 + 4, 0:P], pt0[:, h0:h0 + 4, P:T], pt1[:, h0:h0 + 4, :])[j // 2]
    src = B("pT", l, j)[:, :].rearrange("p (h q) -> p h q", h=4)
    if by == "act":
        done(eng.activation(dst, src, ACT.Copy), "pT", l, j)
    else:
        done(eng.tensor_copy(dst, src), "pT", l, j)


def kernel(**inputs):
    import concourse.bacc as bacc
    from concourse.bass_utils import run_bass_kernel_spmd

    nc = bacc.Bacc("TRN2", target_bir_lowering=False, num_devices=1)
    arrays, aps = {}, {}
    for name in INS:
        a = np.ascontiguousarray(inputs[name])
        arrays[f"in_{name}"] = a
        aps[name] = nc.dram_tensor(f"in_{name}", a.shape, mybir.dt.from_np(a.dtype), kind="ExternalInput").ap()
    freqs = (np.float32(10000.0) ** (-np.arange(HALF, dtype=np.float32) / np.float32(HALF))).astype(np.float32)
    arrays["in_freqs"] = freqs
    freqs_d = nc.dram_tensor("in_freqs", freqs.shape, F32, kind="ExternalInput").ap()
    out_d = nc.dram_tensor("out_x", (1, T, D), F32, kind="ExternalOutput").ap()
    build(nc, aps, freqs_d, out_d)
    r = run_bass_kernel_spmd(nc, [arrays], core_ids=[0])
    return r.results[0]["out_x"]
```

```python
from contextlib import ExitStack

import numpy as np

import concourse.bass as bass
from concourse import mybir

F32 = mybir.dt.float32
I32 = mybir.dt.int32
BF16 = mybir.dt.bfloat16
ALU = mybir.AluOpType
ACT = mybir.ActivationFunctionType
AX = mybir.AxisListType

P = 128
D = 1024
T = 256
TT = T // P
DC = D // P
HC = DC // 2
DEPTH = 2
CW = 512
CB = CW // P
H = 8
NOPE, ROPE, VD = 64, 32, 64
QK = NOPE + ROPE
HALF = ROPE // 2
QR, KVR = 256, 128
SBD = 64
LAT = QR + KVR + ROPE
OFF_HC, OFF_BG, OFF_CG = 0, CW, 2 * CW
OFF_LAT = 3 * CW
OFF_SB = OFF_LAT + LAT
OFF_GATE = OFF_SB + 3 * CW
IN_COLS = OFF_GATE + 3 * D
NG, EPG = 4, 8
E = NG * EPG
FE = 256
FC = FE // P
SLOTS = 32
QE = P // SLOTS
QUADS = E // QE
GD = 4
AWAKE_FIRST, AWAKE_LAYER, AWAKE_ROUTE, AWAKE_TILE, AWAKE_LAST = 20, 12, 18, 9, 16
MIDDLE = QUADS // 2
MORE = T // SLOTS - 1
CHOICE_STEPS = 11
SMALL = 10
CONSTS_N = 7
BRANCHES = (0, 2, 1)
EPS = 1e-6
NEG = -1e30
UNIT = 4096
AREA = 17984
SPARES = 2
RING = 7
MAGIC = 1.5 * 2.0 ** 23
TWO_PI = 2.0 * np.pi
C1 = 6.28125
C2 = float(np.float32(np.floor((TWO_PI - C1) * 2 ** 22) / 2 ** 22))
C3 = float(np.float32(TWO_PI - C1 - C2))
PI_LOW = 3.1415925

INS = ["x", "positions", "attn_norm", "w_in", "b_gate", "conv_w", "w_out_conv", "q_norm", "kv_norm",
       "w_uq", "w_ukv", "w_out_mla", "w_out_sb", "w_o", "ffn_norm", "w_router_group",
       "b_router_group", "w_router_expert", "b_router_expert", "w_exp_gate", "w_exp_up",
       "w_exp_down", "final_norm"]


EXPERT_UNITS = ("gu", "dn", "more_gu", "more_dn")


class Plan:

    def __init__(self):
        self.jobs = {}
        self.n = 0
        self.freed = {"dve": 0, "act": 0}
        self.last = [None] * 8
        self.at = 0

    def add(self, key, by, banks=8):
        bank = self.at % banks
        self.at += 1
        self.place(key, by, bank)

    def place(self, key, by, bank, before=None):
        self.n += 1
        self.freed[by] += 1
        self.jobs[key] = (self.n, bank, by, self.freed[by], before if before else self.last[bank])
        self.last[bank] = key


def place_of(h):
    return (h % 2) * (H // 2) + h // 2


def head_at(place):
    return 2 * (place % (H // 2)) + place // (H // 2)


def make_plan():
    p = Plan()
    for l in range(DEPTH):
        for j in range(4):
            p.add(("tr", l, j), "dve" if j % 2 == 0 else "act")
        for name, by in (("qs", "act"), ("ks", "act"), ("vs", "dve"), ("lat", "act")):
            for j in range(2):
                p.add((name, l, j), by)
        for j in range(6):
            p.add(("z", l, j), "act")
        for name, by in (("hc", "act"), ("bg", "act"), ("cg", "dve"), ("latT", "dve")):
            for j in range(2):
                p.add((name, l, j), by)
        for j in range(6):
            p.add(("cum", l, j), "dve")
        for j in range(4):
            p.add(("gate", l, 0, j), "act")
            p.add(("y", l, 0, j), "dve")
        for name in ("q", "kv"):
            for j in range(4):
                p.add((name, l, j), "act")
        for j in range(4):
            p.add(("qT", l, j), "act")
        for j in range(2):
            p.add(("pvs", l, j), "act")
        for j in range(4):
            p.add(("kT", l, j), "dve")
        for j in range(4):
            p.add(("gate", l, 2, j), "act")
            if j == 0:
                for i in range(6):
                    p.add(("s", l, i), "dve")
            p.add(("y", l, 2, j), "dve")
        for j in range(6):
            p.add(("pT", l, j), "dve" if j % 2 == 0 else "act")
        for j in range(4):
            p.add(("gate", l, 1, j), "act")
            if j == 0:
                for i in range(2):
                    p.add(("pvm", l, i), "act")
            else:
                p.add(("y", l, 1, j - 1), "dve")
        p.add(("y", l, 1, 3), "dve")
        for j in range(4):
            p.add(("wo", l, j), "dve")
        for j in range(4):
            p.add(("tr2", l, j), "dve" if j % 2 == 0 else "act")
        for t in range(TT):
            p.add(("routeT", l, t), "dve")
        p.add(("route", l), "dve")
        p.add(("rank", l), "dve")
        before = [p.last[4 + j] for j in range(4)]
        for q in range(QUADS):
            p.add(("gather", l, q, 0), "dve", 4)
            p.add(("gather", l, q, 1), "act", 4)
            p.add(("sT", l, q), "act", 4)
            p.add(("eg", l, q), "act", 4)
            p.add(("egT", l, q), "dve", 4)
            p.add(("eu", l, q), "act", 4)
            p.add(("euT", l, q), "dve", 4)
            p.add(("down", l, q, 0), "act", 4)
            p.add(("down", l, q, 1), "dve", 4)
        for j in range(4):
            p.place(("moe", l, j), "dve", 4 + j, before[j])
    return p


def unit_list():
    units = []
    for l in range(DEPTH):
        for name in ("qs", "ks", "vs", "lat", "hc", "bg", "cg"):
            units.append((name, l, 0))
        for b in BRANCHES:
            units += [("gate", l, 2 * b), ("wy", l, b), ("gate", l, 2 * b + 1)]
            if b == 0:
                units.append(("wu", l, 0))
        units += [("wo", l, 0), ("wo", l, 1)]
        for q in range(QUADS):
            units += [("gu", l, QE * q + i) for i in range(QE)] + [("dn", l, 2 * q), ("dn", l, 2 * q + 1)]
            if q == MIDDLE - 1:
                units += [("more_gu", l, 0), ("more_dn", l, 0)]
    return units


def unit_end(name, l, i):
    if name in ("qs", "ks", "vs", "lat", "hc", "bg", "cg"):
        return (name, l, 1)
    if name == "gate":
        return ("gate", l, i // 2, 2 * (i % 2) + 1)
    if name == "wy":
        return ("y", l, i, 3)
    if name == "wo":
        return ("wo", l, 3)
    if name == "wu":
        return ("kv", l, 3)
    if name in ("more_gu", "more_dn"):
        return ("gather", l, MIDDLE, 0)
    if name == "gu":
        return ("eu", l, i // QE)
    return ("down", l, i // 2, 1)


def slots_of_units(units, jobs):
    taken = []
    free = [(0, None)] * (RING + SPARES)
    for name, l, i in units:
        if name in EXPERT_UNITS:
            for k, j in enumerate((3, 0)):
                free[RING + k] = max(free[RING + k], (jobs[("wo", l, j)][0], ("wo", l, j)), key=lambda f: f[0])
        s = min(range(RING + SPARES if name in EXPERT_UNITS else RING), key=lambda k: free[k][0])
        taken.append((s, free[s][1]))
        end = unit_end(name, l, i)
        free[s] = (jobs[end][0], end)
    return taken


def turned_probs(eng, l, j, done, wait_pe, B, pt0, pt1, by):
    wait_pe(eng, "pT", l, j)
    h0 = 4 * (j % 2)
    dst = (pt0[:, h0:h0 + 4, 0:P], pt0[:, h0:h0 + 4, P:T], pt1[:, h0:h0 + 4, :])[j // 2]
    src = B("pT", l, j)[:, :].rearrange("p (h q) -> p h q", h=4)
    if by == "act":
        done(eng.activation(dst, src, ACT.Copy), "pT", l, j)
    else:
        done(eng.tensor_copy(dst, src), "pT", l, j)


def build(nc, A, freqs_d, out_d):
    plan = make_plan()
    jobs = plan.jobs
    units = unit_list()
    taken = slots_of_units(units, jobs)
    unit_of = {u: n for n, u in enumerate(units)}

    with ExitStack() as ctx:
        def sb(name, shape, dt=F32):
            return ctx.enter_context(nc.sbuf_tensor(name, shape, dt))

        def sem(name):
            return ctx.enter_context(nc.semaphore(name))

        bank = [ctx.enter_context(nc.psum_tensor(f"bank{i}", [P, 512], F32)) for i in range(8)]

        ring = sb("ring", [P, RING, UNIT])
        xs = sb("xs", [P, TT, D])
        hT = sb("hT", [P, DC, T])
        wr = [sb(f"wr{l}", [P, DC, NG + E]) for l in range(DEPTH)]
        rbias = [sb(f"rbias{l}", [P, NG + E]) for l in range(DEPTH)]
        gains = [sb(f"gains{l}", [P, 2, DC]) for l in range(DEPTH)]
        lgain = [sb(f"lgain{l}", [P, 3]) for l in range(DEPTH)]
        nbg = [sb(f"nbg{l}", [P, 24]) for l in range(DEPTH)]
        cw = [sb(f"cw{l}", [P, 3, CB]) for l in range(DEPTH)]
        fgain = hT[:, 0:4, :].rearrange("p c n -> p (c n)")
        ident = sb("ident", [P, P])
        low = sb("low", [P, P])
        ones = sb("ones", [P, P])
        fold = sb("fold", [P, SLOTS])
        hidden = sb("hidden", [P, P])
        before = sb("before", [P, P])
        iot_i = sb("iot_i", [P, SLOTS], I32)
        iot = sb("iot", [P, SLOTS])
        iot1 = sb("iot1", [P, SLOTS])
        countdown = sb("countdown", [P, EPG])
        before_h = sb("before_h", [P, P], BF16)
        ones_h = sb("ones_h", [P, P], BF16)
        member = sb("member", [P, TT, E], BF16)
        epst = sb("epst", [P, 1])
        pos_i = sb("pos_i", [P, TT], I32)
        posf = sb("posf", [P, TT])
        frq = sb("frq", [P, HALF])
        cosn = sb("cosn", [P, TT, HALF])
        sinn = sb("sinn", [P, TT, HALF])
        nst = sb("nst", [P, 6, 8])
        flag_i = sb("flag_i", [P, DEPTH], I32)
        e_i = sb("e_i", [P, 1], I32)
        rope_t = sb("rope_t", [P, 4, H, HALF])

        area = sb("area", [P, AREA])
        at = [0]

        def cut(*shape, back=None):
            if back is not None:
                at[0] = back
            n = int(np.prod(shape))
            a = area[:, at[0]:at[0] + n]
            at[0] += n
            assert at[0] <= AREA, at[0]
            if len(shape) == 2:
                a = a.rearrange("p (a b) -> p a b", b=shape[1])
            elif len(shape) == 3:
                a = a.rearrange("p (a b c) -> p a b c", b=shape[1], c=shape[2])
            elif len(shape) == 4:
                a = a.rearrange("p (a b c d) -> p a b c d", b=shape[1], c=shape[2], d=shape[3])
            return a

        qsT = cut(CB, T)
        ksT = cut(CB, T)
        vs = cut(TT, CW)
        z0 = cut(H, T)
        xn = z0.rearrange("p h n -> p (h n)").rearrange("p (t d) -> p t d", t=TT)
        z1 = cut(H, P)
        l0 = cut(H, T)
        l1 = cut(H, P)
        lat_at = at[0]
        lat = cut(TT, LAT)
        latT = cut(3, T)
        vn = cut(TT, CW)
        ang, ang2 = (vn[:, i, 0:64].rearrange("p (s t n) -> p s t n", s=2, t=TT) for i in range(2))
        sig = cut(2, 512)
        mark = at[0]
        hc = cut(CB, T)
        bg = cut(CB, T)
        yc = cut(CB, T)
        qn = cut(TT, H, QK, back=mark)
        kn = cut(TT, H, QK)
        qT = area[:, 0:H * T].rearrange("p (a b) -> p a b", b=T)
        kT = l0
        omT = cut(CB, T, back=mark)
        osT = cut(CB, T, back=lat_at)
        merged = cut(DC, T, back=mark + 3 * CB * T)
        spare_at = AREA - SPARES * UNIT
        spare = [area[:, AREA - (k + 1) * UNIT:AREA - k * UNIT] for k in range(SPARES)]
        pt0, pt1 = l0, l1

        xn_at = 3 * CB * T
        Ps = cut(TT, E, SLOTS, back=0)
        lgT = area[:, 0:T]
        PW = [cut(TT, QE, SLOTS) for _ in range(2)]
        gus = cut(1, 512)[:, 0, :]
        assert at[0] <= xn_at
        xe = cut(DC, P, back=xn_at + TT * D)
        aT = cut(FC, 2, P)
        yS = cut(1, D)[:, 0, :]
        sS = cut(1, T)[:, 0, :]
        lg = cut(TT, NG + E)
        r4 = cut(4, TT, NG)
        r8 = cut(9, TT, EPG)
        r1 = cut(8, TT)
        comb = cut(TT, E)
        rk = cut(TT, E)
        count = cut(1, E)[:, 0, :]
        blk = cut(MORE, E)
        blk_one = cut(MORE, E)
        o_eq = cut(MORE, E)
        o_first = cut(MORE, E)
        o_sel = cut(1, E)[:, 0, :]
        o_tmp = cut(TT, E)
        o_num = cut(1, 8)[:, 0, :]
        o_rk = cut(1, 4)[:, 0, :]
        o_P = cut(TT, SLOTS)
        o_PW = cut(TT, SLOTS)
        o_x = cut(DC, SLOTS)
        turn = cut(1, 1)[:, 0, :]
        assert at[0] <= spare_at, (at[0], spare_at)
        ones_row = ones[:, 0:1].to_broadcast([P, MORE * E])

        pe_done = sem("pe_done")
        awake = sem("awake")
        dve_freed = sem("dve_freed")
        act_freed = sem("act_freed")
        dve_step = sem("dve_step")
        act_step = sem("act_step")
        freed = {"dve": dve_freed, "act": act_freed}
        landed = [sem(f"unit_landed{i}") for i in range(RING + SPARES)]
        consts_made = sem("consts_made")
        iota_made = sem("iota_made")
        x_landed = [sem(f"x_landed{t}") for t in range(TT)]
        once_landed = sem("once_landed")
        small_landed = [sem(f"small_landed{l}") for l in range(DEPTH)]
        final_landed = sem("final_landed")
        gates_landed = [sem(f"gates_landed{l}") for l in range(DEPTH)]
        gains_landed = [sem(f"gains_landed{l}") for l in range(DEPTH)]
        angles_ready = sem("angles_ready")
        rope_ready = sem("rope_ready")
        const_ready = sem("const_ready")
        ss_ready = sem("ss_ready")
        xn_ready = sem("xn_ready")
        z_abs = sem("z_abs")
        z_sp = sem("z_sp")
        l_ready = sem("l_ready")
        a_ready = sem("a_ready")
        lat_ss = sem("lat_ss")
        lat_ready = sem("lat_ready")
        conv_ready = sem("conv_ready")
        rope_q = sem("rope_q")
        rope_k = sem("rope_k")
        ssub_ready = sem("ssub_ready")
        exp_ready = sem("exp_ready")
        pn_ready = sem("pn_ready")
        sig_ready = sem("sig_ready")
        added = sem("added")
        rt_a = sem("rt_a")
        rt_b = sem("rt_b")
        member_ready = sem("member_ready")
        p_ready = sem("p_ready")
        pw_ready = sem("pw_ready")
        eg_ready = sem("eg_ready")
        out_stored = sem("out_stored")
        flag_ready = sem("flag_ready")
        fold_ready = sem("fold_ready")
        (o_chosen, o_taken, o_landed, o_slots, o_gathered, o_x_ready, o_gu_done, o_gu_read, o_turned, o_exp, o_act,
         o_down, o_y_ready, o_out, o_used, o_step) = (
            [sem(f"{n}{l}") for l in range(DEPTH)] for n in
            ("o_chosen", "o_taken", "o_landed", "o_slots", "o_gathered", "o_x_ready", "o_gu_done", "o_gu_read", "o_turned",
             "o_exp", "o_act", "o_down", "o_y_ready", "o_out", "o_used", "o_step"))

        w_in, w_o = A["w_in"], A["w_o"]
        w_y = {0: A["w_out_conv"], 1: A["w_out_mla"], 2: A["w_out_sb"]}
        col0 = {"qs": OFF_SB, "ks": OFF_SB + CW, "vs": OFF_SB + 2 * CW, "lat": OFF_LAT,
                "hc": OFF_HC, "bg": OFF_BG, "cg": OFF_CG}

        def slot(name, l, i=0):
            return taken[unit_of[(name, l, i)]][0]

        def unit(name, l, i=0):
            s = slot(name, l, i)
            return ring[:, s, :] if s < RING else spare[s - RING]

        def cols_unit(name, l, i=0):
            w = LAT if name == "lat" else 512
            return unit(name, l, i)[:, 0:DC * w].rearrange("p (c n) -> p c n", c=DC)

        def rows_unit(name, l, i):
            return unit(name, l, i).rearrange("p (c n) -> p c n", c=4)

        def gu_unit(l, e):
            return unit("gu", l, e).rearrange("p (g c n) -> p g c n", g=2, c=DC)

        def dn_unit(l, pair):
            return unit("dn", l, pair).rearrange("p (e c n) -> p e c n", e=2, c=FC)

        def wuq(l):
            return unit("wu", l)[:, 0:2 * H * QK].rearrange("p (c n) -> p c n", c=2)

        def wukv(l):
            return unit("wu", l)[:, 2 * H * QK:2 * H * QK + H * (NOPE + VD)]

        def o_gu(l):
            return unit("more_gu", l).rearrange("p (g c n) -> p g c n", g=2, c=DC)

        def o_dn(l):
            return unit("more_dn", l)[:, 0:FC * D].rearrange("p (c n) -> p c n", c=FC)

        def loads_of(name, l, i):
            if name in ("more_gu", "more_dn"):
                return 0
            return 1 if name == "gu" and i >= E - QE else 2

        def wait_unit(eng, name, l, i=0):
            n = unit_of[(name, l, i)]
            seen = sum(loads_of(*units[m]) for m in range(n + 1) if taken[m][0] == taken[n][0])
            eng.wait_ge(landed[taken[n][0]], 16 * seen)

        def wait_pe(eng, *key):
            eng.wait_ge(pe_done, jobs[key][0])

        def wait_read(eng, *key):
            _, _, by, value, _ = jobs[key]
            eng.wait_ge(freed[by], value)

        gates_in_order = [(l, b, j) for l in range(DEPTH) for b in BRANCHES for j in range(4)]

        def wait_merged(eng, l, b, j):
            at = BRANCHES.index(b)
            if at == 0:
                wait_read(eng, "y", l, b, j)
            else:
                eng.wait_ge(added, 4 * ((len(BRANCHES) - 1) * l + at - 1) + j + 1)

        def B(*key):
            return bank[jobs[key][1]]

        block = ctx.enter_context(nc.Block())

        @block.sync
        def _(sp):
            for t in range(TT):
                sp.dma_start(xs[:, t, :], A["x"][0, t * P:(t + 1) * P, :]).then_inc(x_landed[t], 16)
            for n, (name, l, i) in enumerate(units):
                if name == "qs":
                    for g, norm in enumerate(("attn_norm", "ffn_norm")):
                        sp.dma_start(gains[l][:, g, :], A[norm][l].rearrange("(p c) -> p c", c=DC)).then_inc(gains_landed[l], 16)
                if name == "ks":
                    if l == 0:
                        with nc.allow_non_contiguous_dma("small transposed vectors"):
                            sp.dma_start(pos_i[:], A["positions"].rearrange("b (t p) -> p (b t)", p=P)).then_inc(once_landed, 16)
                        sp.dma_start(frq[:], freqs_d.partition_broadcast(P)).then_inc(once_landed, 16)
                    s = small_landed[l]
                    with nc.allow_non_contiguous_dma("small transposed vectors"):
                        sp.dma_start(lgain[l][:, 0:2], A["q_norm"][l].rearrange("(c p) -> p c", p=P)).then_inc(s, 16)
                        sp.dma_start(lgain[l][:, 2:3], A["kv_norm"][l].rearrange("(c p) -> p c", p=P)).then_inc(s, 16)
                        sp.dma_start(nbg[l][:], A["b_gate"][l].rearrange("(c p) -> p c", p=P)).then_inc(s, 16)
                        for k in range(3):
                            sp.dma_start(cw[l][:, k, :], A["conv_w"][l, k].rearrange("(c p) -> p c", p=P)).then_inc(s, 16)
                    sp.dma_start(rbias[l][:, 0:NG], A["b_router_group"][l].partition_broadcast(P)).then_inc(s, 16)
                    sp.dma_start(rbias[l][:, NG:], A["b_router_expert"][l].partition_broadcast(P)).then_inc(s, 16)
                    sp.dma_start(wr[l][:, :, 0:NG], A["w_router_group"][l].rearrange("(p c) n -> p c n", c=DC)).then_inc(s, 16)
                    sp.dma_start(wr[l][:, :, NG:], A["w_router_expert"][l].rearrange("(p c) n -> p c n", c=DC)).then_inc(s, 16)
                if taken[n][1]:
                    wait_pe(sp, *taken[n][1])
                s = landed[taken[n][0]]
                if name == "more_gu":
                    continue
                if name == "more_dn":
                    sp.wait_ge(flag_ready, l + 1)
                    n_more = sp.value_load(flag_i[0:1, l:l + 1], min_val=0, max_val=E * MORE)
                    with sp.If(n_more != 0):
                        with sp.Fori(0, n_more, 1) as i:
                            sp.wait_ge(o_chosen[l], i + 1)
                            sp.sem_inc(o_taken[l], 1)
                            e = sp.value_load(e_i[0:1, 0:1], min_val=0, max_val=E - 1)
                            for g, w in enumerate(("w_exp_gate", "w_exp_up")):
                                sp.dma_start(o_gu(l)[:, g, :, :], A[w][l, bass.ds(e, 1)].rearrange("e (p c) n -> p (e c) n", c=DC)).then_inc(o_landed[l], 16)
                            sp.dma_start(o_dn(l), A["w_exp_down"][l, bass.ds(e, 1)].rearrange("e (p c) n -> p (e c) n", c=FC)).then_inc(o_landed[l], 16)
                    continue
                if name in col0 or name == "gate":
                    c0 = OFF_GATE + 512 * i if name == "gate" else col0[name]
                    dst = cols_unit(name, l, i)
                    src = w_in[l].rearrange("(p c) n -> p c n", c=DC)[:, :, c0:c0 + dst.shape[2]]
                    for hh in range(2):
                        sp.dma_start(dst[:, 4 * hh:4 * hh + 4, :], src[:, 4 * hh:4 * hh + 4, :]).then_inc(s, 16)
                elif name in ("wy", "wo"):
                    src = w_o[l, CW * i:CW * (i + 1), :] if name == "wo" else w_y[i][l]
                    src = src.rearrange("(c p) n -> p c n", p=P)
                    dst = rows_unit(name, l, i)
                    for hh in range(2):
                        sp.dma_start(dst[:, 2 * hh:2 * hh + 2, :], src[:, 2 * hh:2 * hh + 2, :]).then_inc(s, 16)
                elif name == "wu":
                    sp.dma_start(wuq(l), A["w_uq"][l].rearrange("(c p) n -> p c n", p=P)).then_inc(s, 16)
                    sp.dma_start(wukv(l), A["w_ukv"][l]).then_inc(s, 16)
                elif name == "gu" and i < E - QE:
                    dst = gu_unit(l, i)
                    for g, w in enumerate(("w_exp_gate", "w_exp_up")):
                        sp.dma_start(dst[:, g, :, :], A[w][l, i].rearrange("(p c) n -> p c n", c=DC)).then_inc(s, 16)
                elif name == "gu":
                    sp.dma_start(gu_unit(l, i)[:, 0, :, :],
                                 A["w_exp_gate"][l, i].rearrange("(p c) n -> p c n", c=DC)).then_inc(gates_landed[l], 16)
                    if i == E - 1:
                        for e in range(E - QE, E):
                            sp.dma_start(gu_unit(l, e)[:, 1, :, :],
                                         A["w_exp_up"][l, e].rearrange("(p c) n -> p c n", c=DC)).then_inc(landed[slot("gu", l, e)], 16)
                else:
                    dst = dn_unit(l, i)
                    for j in range(2):
                        sp.dma_start(dst[:, j, :, :], A["w_exp_down"][l, 2 * i + j].rearrange("(p c) n -> p c n", c=FC)).then_inc(s, 16)
            wait_pe(sp, "route", DEPTH - 1)
            sp.dma_start(fgain, A["final_norm"].partition_broadcast(P)).then_inc(final_landed, 16)
            for t in range(TT):
                sp.wait_ge(xn_ready, 2 * DEPTH * TT + t + 1)
                sp.dma_start(out_d[0, t * P:(t + 1) * P, :], xs[:, t, :]).then_inc(out_stored, 16)
            sp.wait_ge(out_stored, 16 * TT)

        @block.gpsimd
        def _(pool):
            n = [0]

            def step(ins):
                n[0] += 1
                ins.then_inc(consts_made, 1)
                pool.wait_ge(consts_made, n[0])

            def fill(t, op, mult, stepv, value):
                step(nc.gpsimd.affine_select(out=t[:], in_=t[:], compare_op=op, fill=value, base=0,
                                             pattern=[[stepv, P]], channel_multiplier=mult))

            step(nc.gpsimd.memset(ident[:], 0.0))
            fill(ident, ALU.not_equal, 1, -1, 1.0)
            for t, v in ((low, 1.0), (before, 1.0), (ones, 1.0)):
                step(nc.gpsimd.memset(t[:], v))
            fill(low, ALU.is_ge, 1, -1, 0.0)
            fill(before, ALU.is_gt, -1, 1, 0.0)
            nc.gpsimd.iota(iot_i[:], [[1, SLOTS]], base=0, channel_multiplier=0).then_inc(iota_made, 1)
            assert n[0] == CONSTS_N
            for l in range(DEPTH):
                for q in range(QUADS):
                    pool.wait_ge(p_ready, 4 * l + (2 if q == 0 else 4))
                    if q >= 2:
                        wait_pe(pool, "sT", l, q - 2)
                    for t in range(TT):
                        nc.gpsimd.tensor_tensor(PW[q % 2][:, t, :, :], Ps[:, t, QE * q:QE * q + QE, :],
                                                comb[:, t, QE * q:QE * q + QE].unsqueeze(2).to_broadcast([P, QE, SLOTS]),
                                                ALU.mult).then_inc(pw_ready, 1)

        @block.tensor
        def _(pe):
            def begin(*key):
                before = jobs[key][4]
                if before:
                    wait_read(pe, *before)
                return B(*key)

            wakes = []

            def keep_awake(target, n):
                for _ in range(n):
                    mm = pe.matmul(target[:, 0:P], ident[:], ident[:], start=True, stop=True)
                mm.then_inc(awake, 1)
                wakes.append(n)
                pe.wait_ge(awake, len(wakes))

            def blocks(name, l, unit, i, key, j):
                ps = begin(*key)
                w = cols_unit(unit, l, i)
                for b in range(2):
                    c0 = (2 * j + b) * P % 512
                    for c in range(DC):
                        mm = pe.matmul(ps[:, b * T:(b + 1) * T], w[:, c, c0:c0 + P], hT[:, c, :],
                                       start=c == 0, stop=c == DC - 1)
                mm.then_inc(pe_done, 1)

            def natural(name, l, t):
                ps = begin(name, l, t)
                w = cols_unit(name, l)
                for c in range(DC):
                    mm = pe.matmul(ps[:, 0:w.shape[2]], hT[:, c, t * P:(t + 1) * P], w[:, c, :],
                                   start=c == 0, stop=c == DC - 1)
                mm.then_inc(pe_done, 1)

            def turn_x(name, l, n):
                for j in range(2 * TT):
                    t, half = j // 2, j % 2
                    ps = begin(name, l, j)
                    if name == "tr2" and j == 2:
                        keep_awake(ps, AWAKE_TILE)
                    if half == 0:
                        pe.wait_ge(xn_ready, TT * n + t + 1)
                    for i in range(HC):
                        c = HC * half + i
                        mm = pe.transpose(ps[:, i * P:(i + 1) * P], xn[:, t, c * P:(c + 1) * P], ident[:])
                    mm.then_inc(pe_done, 1)

            def turn_heads(name, l, src):
                for j in range(4):
                    ps = begin(name, l, j)
                    for i in range(2):
                        for t in range(TT):
                            mm = pe.transpose(ps[0:QK, (TT * i + t) * P:(TT * i + t + 1) * P],
                                              src[:, t, 2 * j + i, :], ident[:])
                    mm.then_inc(pe_done, 1)

            def gate(l, b, j):
                if j % 2 == 0:
                    wait_unit(pe, "gate", l, 2 * b + j // 2)
                blocks("gate", l, "gate", 2 * b + j // 2, ("gate", l, b, j), j)

            def branch(l, b, j, src):
                if j == 0:
                    wait_unit(pe, "wy", l, b)
                ps = begin("y", l, b, j)
                w = rows_unit("wy", l, b)
                for bb in range(2):
                    m = 2 * j + bb
                    for c in range(CB):
                        mm = pe.matmul(ps[:, bb * T:(bb + 1) * T], w[:, c, m * P:(m + 1) * P], src[:, c, :],
                                       start=c == 0, stop=c == CB - 1)
                mm.then_inc(pe_done, 1)

            def expert_products(name, l, quad, g, chunks):
                ps = begin(name, l, quad) if chunks[0] == 0 else B(name, l, quad)
                for c in chunks:
                    if g == 0 and c == GD:
                        wait_read(pe, "gather", l, quad, 1)
                    for e in range(QE):
                        mine = slice(e * SLOTS, (e + 1) * SLOTS)
                        mm = pe.matmul(ps[mine, 0:FE], xe[:, c, mine], gu_unit(l, QE * quad + e)[:, g, c, :],
                                       start=c == 0, stop=c == DC - 1, skip_group_check=True)
                return mm

            def turn_expert(name, source, l, quad, g):
                wait_read(pe, source, l, quad)
                ps = begin(name, l, quad)
                for c in range(FC):
                    mm = pe.transpose(ps[:, c * P:(c + 1) * P], gus[:, g * FE + c:(g + 1) * FE:FC], ident[:])
                mm.then_inc(pe_done, 1)

            def further_blocks(l):
                pe.wait_ge(flag_ready, l + 1)
                n_more = pe.value_load(flag_i[0:1, l:l + 1], min_val=0, max_val=E * MORE)
                with pe.If(n_more != 0):
                    for j in range(2):
                        wait_read(pe, "down", l, MIDDLE - 1, j)
                    with pe.Fori(0, n_more, 1) as i:
                        pe.wait_ge(o_slots[l], i + 1)
                        for c in range(DC):
                            for t in range(TT):
                                pe.matmul(bank[0][:, c * SLOTS:(c + 1) * SLOTS], xn[:, t, c * P:(c + 1) * P],
                                          o_P[:, t, :], start=t == 0, stop=t == TT - 1)
                        for t in range(TT):
                            mm = pe.transpose(bank[1][0:SLOTS, t * P:(t + 1) * P], o_PW[:, t, :], ident[:])
                        mm.then_inc(o_gathered[l], 1)
                        pe.wait_ge(o_landed[l], 48 * i + 48)
                        pe.wait_ge(o_x_ready[l], i + 1)
                        for cc in range(2):
                            for g in range(2):
                                for j in range(QE):
                                    c = 2 * j + cc
                                    mm = pe.matmul(bank[2][j * SLOTS:(j + 1) * SLOTS, g * FE:(g + 1) * FE], o_x[:, c, :],
                                                   o_gu(l)[:, g, c, :], start=cc == 0 and g == 0, stop=cc == 1,
                                                   skip_group_check=True)
                        mm.then_inc(o_gu_done[l], 1)
                        pe.wait_ge(o_gu_read[l], i + 1)
                        for g in range(2):
                            for c in range(FC):
                                mm = pe.matmul(bank[3][:, (FC * g + c) * SLOTS:(FC * g + c + 1) * SLOTS],
                                               gus[:, g * FE + c:(g + 1) * FE:FC], fold[:], start=True, stop=True)
                        mm.then_inc(o_turned[l], 1)
                        pe.wait_ge(o_act[l], i + 1)
                        for hh in range(2):
                            for c in range(FC):
                                mm = pe.matmul(bank[hh][0:SLOTS, :], aT[:, c, 1, 0:SLOTS],
                                               o_dn(l)[:, c, hh * 512:(hh + 1) * 512], start=c == 0, stop=c == FC - 1)
                        mm.then_inc(o_down[l], 1)
                        pe.wait_ge(o_y_ready[l], i + 1)
                        for t in range(TT):
                            for hh in range(2):
                                mm = pe.matmul(bank[4 + 2 * t + hh][:, :], sS[0:SLOTS, t * P:(t + 1) * P],
                                               yS[0:SLOTS, hh * 512:(hh + 1) * 512], start=False, stop=False,
                                               skip_group_check=True)
                        mm.then_inc(o_out[l], 1)

            pe.wait_ge(consts_made, 2)
            keep_awake(bank[7], AWAKE_FIRST)
            for l in range(DEPTH):
                turn_x("tr", l, 2 * l)
                wait_read(pe, "tr", l, 2)
                wait_read(pe, "tr", l, 3)
                for name in ("qs", "ks"):
                    wait_unit(pe, name, l)
                    for j in range(2):
                        blocks(name, l, name, 0, (name, l, j), j)
                wait_unit(pe, "vs", l)
                for t in range(TT):
                    natural("vs", l, t)
                wait_unit(pe, "lat", l)
                for t in range(TT):
                    natural("lat", l, t)
                wait_read(pe, "qs", l, 1)
                wait_read(pe, "ks", l, 1)
                for j in range(6):
                    ps = begin("z", l, j)
                    per = 2 if j < 4 else 4
                    h0 = 2 * j if j < 4 else 4 * (j - 4)
                    q0, k0 = (0, 0) if j < 4 else (P, P)
                    nq = T - q0
                    for i in range(per):
                        h = head_at(h0 + i)
                        r0 = SBD * (h % 2)
                        mm = pe.matmul(ps[:, i * nq:(i + 1) * nq], ksT[r0:r0 + SBD, h // 2, k0:k0 + P],
                                       qsT[r0:r0 + SBD, h // 2, q0:T], start=True, stop=True)
                    mm.then_inc(pe_done, 1)
                for name in ("hc", "bg", "cg"):
                    wait_unit(pe, name, l)
                    for j in range(2):
                        blocks(name, l, name, 0, (name, l, j), j)
                pe.wait_ge(lat_ready, l + 1)
                for j in range(2):
                    ps = begin("latT", l, j)
                    for i, c in enumerate((0, 1) if j == 0 else (2,)):
                        for t in range(TT):
                            mm = pe.transpose(ps[:, (TT * i + t) * P:(TT * i + t + 1) * P],
                                              lat[:, t, c * P:(c + 1) * P], ident[:])
                    mm.then_inc(pe_done, 1)
                pe.wait_ge(l_ready, l + 1)
                if l == 0:
                    pe.wait_ge(consts_made, CONSTS_N)
                for j in range(6):
                    ps = begin("cum", l, j)
                    if j < 4:
                        pe.matmul(ps[:, :], low[:], l0[:, 2 * j:2 * j + 2, :], start=True, stop=False)
                        mm = pe.matmul(ps[:, :].rearrange("p (h q) -> p h q", h=2)[:, :, P:T], ones[:],
                                       l1[:, 2 * j:2 * j + 2, :], start=False, stop=True)
                    else:
                        mm = pe.matmul(ps[:, :], low[:], l1[:, 4 * (j - 4):4 * (j - 3), :], start=True, stop=True)
                    mm.then_inc(pe_done, 1)
                for j in range(4):
                    gate(l, 0, j)
                    if j == 0:
                        pe.wait_ge(conv_ready, l + 1)
                    branch(l, 0, j, yc)
                wait_unit(pe, "wu", l)
                for j in range(4):
                    ps = begin("q", l, j)
                    t, hh = j // 2, j % 2
                    for c in range(2):
                        mm = pe.matmul(ps[:, 0:4 * QK], latT[:, c, t * P:(t + 1) * P],
                                       wuq(l)[:, c, hh * 4 * QK:(hh + 1) * 4 * QK], start=c == 0, stop=c == 1)
                    mm.then_inc(pe_done, 1)
                for j in range(4):
                    ps = begin("kv", l, j)
                    t, hh = j // 2, j % 2
                    pe.matmul(ps[:, :], latT[:, 2, t * P:(t + 1) * P], wukv(l)[:, hh * 512:(hh + 1) * 512],
                              start=True, stop=True).then_inc(pe_done, 1)
                pe.wait_ge(rope_q, TT * l + TT)
                turn_heads("qT", l, qn)
                pe.wait_ge(rope_k, l + 1)
                for j in range(2):
                    ps = begin("pvs", l, j)
                    for i in range(4):
                        h = 4 * j + i
                        if i % 2 == 0:
                            pe.wait_ge(a_ready, 2 * l + 2)
                        o = ps[SBD * (h % 2):SBD * (h % 2) + SBD, (i // 2) * T:(i // 2 + 1) * T]
                        pe.matmul(o, vs[:, 0, h * SBD:(h + 1) * SBD], l0[:, place_of(h), :], start=True, stop=False)
                        mm = pe.matmul(o[:, P:T], vs[:, 1, h * SBD:(h + 1) * SBD], l1[:, place_of(h), :], start=False, stop=True)
                    mm.then_inc(pe_done, 1)
                turn_heads("kT", l, kn)
                gate(l, 2, 0)
                wait_read(pe, "qT", l, 3)
                wait_read(pe, "kT", l, 3)
                for j in range(6):
                    ps = begin("s", l, j)
                    per = 4 if j < 2 else 2
                    h0 = 4 * j if j < 2 else 2 * (j - 2)
                    t, nk = (0, P) if j < 2 else (1, T)
                    for i in range(per):
                        mm = pe.matmul(ps[:, i * nk:(i + 1) * nk], qT[0:QK, h0 + i, t * P:(t + 1) * P],
                                       kT[0:QK, h0 + i, 0:nk], start=True, stop=True)
                    mm.then_inc(pe_done, 1)
                wait_read(pe, "pvs", l, 1)
                for j in range(4):
                    if j:
                        gate(l, 2, j)
                    branch(l, 2, j, osT)
                pe.wait_ge(pn_ready, l + 1)
                for j in range(6):
                    ps = begin("pT", l, j)
                    for i in range(4):
                        h = 4 * (j % 2) + i
                        src = (z1[:, h, :], z0[:, h, 0:P], z0[:, h, P:T])[j // 2]
                        mm = pe.transpose(ps[:, i * P:(i + 1) * P], src, ident[:])
                    mm.then_inc(pe_done, 1)
                gate(l, 1, 0)
                wait_read(pe, "pT", l, 4)
                wait_read(pe, "pT", l, 5)
                for j in range(2):
                    ps = begin("pvm", l, j)
                    for i in range(4):
                        h = 4 * j + i
                        o = ps[VD * (h % 2):VD * (h % 2) + VD, (i // 2) * T:(i // 2 + 1) * T]
                        pe.matmul(o, vn[:, 0, h * VD:(h + 1) * VD], pt0[:, h, :], start=True, stop=False)
                        mm = pe.matmul(o[:, P:T], vn[:, 1, h * VD:(h + 1) * VD], pt1[:, h, :], start=False, stop=True)
                    mm.then_inc(pe_done, 1)
                gate(l, 1, 1)
                wait_read(pe, "pvm", l, 1)
                for j in range(4):
                    branch(l, 1, j, omT)
                    if j < 2:
                        gate(l, 1, j + 2)
                wait_merged(pe, l, 1, 2)
                wait_unit(pe, "wo", l, 0)
                wait_unit(pe, "wo", l, 1)
                for j in range(4):
                    ps = begin("wo", l, j)
                    t, hh = j // 2, j % 2
                    for c in range(DC):
                        if j == 0 and c == DC - 2:
                            wait_merged(pe, l, 1, 3)
                        w = rows_unit("wo", l, c // 4)
                        mm = pe.matmul(ps[:, :], merged[:, c, t * P:(t + 1) * P], w[:, c % 4, hh * 512:(hh + 1) * 512],
                                       start=c == 0, stop=c == DC - 1)
                    mm.then_inc(pe_done, 1)

                turn_x("tr2", l, 2 * l + 1)
                for t in range(TT):
                    wait_read(pe, "tr2", l, 2 * t)
                    wait_read(pe, "tr2", l, 2 * t + 1)
                    ps = begin("routeT", l, t)
                    for c in range(DC):
                        mm = pe.matmul(ps[0:NG + E, 0:P], wr[l][:, c, :], hT[:, c, t * P:(t + 1) * P],
                                       start=c == 0, stop=c == DC - 1)
                    mm.then_inc(pe_done, 1)
                ps = begin("route", l)
                for t in range(TT):
                    wait_read(pe, "routeT", l, t)
                    mm = pe.transpose(ps[:, t * 64:t * 64 + NG + E], lgT[0:NG + E, t * P:(t + 1) * P], ident[0:NG + E, 0:NG + E])
                mm.then_inc(pe_done, 1)
                ps = begin("rank", l)
                keep_awake(ps, AWAKE_ROUTE)
                if l == 0:
                    pe.wait_ge(fold_ready, 1)
                pe.wait_ge(member_ready, l + 1)
                pe.matmul(ps[:, 0:E], before_h[:], member[:, 0, :], start=True, stop=True)
                pe.matmul(ps[:, E:2 * E], ones_h[:], member[:, 0, :], start=True, stop=False)
                pe.matmul(ps[:, E:2 * E], before_h[:], member[:, 1, :], start=False, stop=True)
                pe.matmul(ps[:, 2 * E:3 * E], ones_h[:], member[:, 0, :], start=True, stop=False)
                pe.matmul(ps[:, 2 * E:3 * E], ones_h[:], member[:, 1, :], start=False, stop=True).then_inc(pe_done, 1)
                for quad in range(QUADS):
                    pe.wait_ge(p_ready, 4 * l + (1 if quad == 0 else 4))
                    if quad == MIDDLE:
                        further_blocks(l)
                    for b in range(2):
                        ps = begin("gather", l, quad, b)
                        for cc in range(GD):
                            c = GD * b + cc
                            for t in range(TT):
                                mm = pe.matmul(ps[:, cc * P:(cc + 1) * P], xn[:, t, c * P:(c + 1) * P],
                                               Ps[:, t, QE * quad:QE * quad + QE, :], start=t == 0, stop=t == TT - 1)
                        mm.then_inc(pe_done, 1)
                    pe.wait_ge(pw_ready, 2 * (QUADS * l + quad) + 2)
                    ps = begin("sT", l, quad)
                    for t in range(TT):
                        mm = pe.transpose(ps[:, t * P:(t + 1) * P], PW[quad % 2][:, t, :, :], ident[:])
                    mm.then_inc(pe_done, 1)
                    wait_read(pe, "gather", l, quad, 0)
                    if quad == QUADS - 1:
                        pe.wait_ge(gates_landed[l], 16 * QE)
                    else:
                        for e in range(QE):
                            wait_unit(pe, "gu", l, QE * quad + e)
                    expert_products("eg", l, quad, 0, range(DC)).then_inc(pe_done, 1)
                    if quad == QUADS - 1:
                        for e in range(QE):
                            wait_unit(pe, "gu", l, QE * quad + e)
                    expert_products("eu", l, quad, 1, range(HC))
                    turn_expert("egT", "eg", l, quad, 0)
                    expert_products("eu", l, quad, 1, range(HC, DC)).then_inc(pe_done, 1)
                    turn_expert("euT", "eu", l, quad, 1)
                    if quad == QUADS - 1:
                        keep_awake(begin("down", l, quad, 0), AWAKE_LAST)
                    wait_read(pe, "euT", l, quad)
                    wait_unit(pe, "dn", l, 2 * quad)
                    wait_unit(pe, "dn", l, 2 * quad + 1)
                    for hh in range(2):
                        ps = begin("down", l, quad, hh)
                        for c in range(FC):
                            for e in range(QE):
                                mm = pe.matmul(ps[e * SLOTS:(e + 1) * SLOTS, :],
                                               aT[:, c, 1, e * SLOTS:(e + 1) * SLOTS],
                                               dn_unit(l, 2 * quad + e // 2)[:, e % 2, c, hh * 512:(hh + 1) * 512],
                                               start=c == 0, stop=c == FC - 1, skip_group_check=True)
                        mm.then_inc(pe_done, 1)
                    wait_read(pe, "down", l, quad, 0)
                    wait_read(pe, "down", l, quad, 1)
                    wait_read(pe, "sT", l, quad)
                    for j in range(4):
                        if quad == 0:
                            begin("moe", l, j)
                        t, hh = j // 2, j % 2
                        mm = pe.matmul(B("moe", l, j)[:, :], sS[:, t * P:(t + 1) * P],
                                       yS[:, hh * 512:(hh + 1) * 512],
                                       start=quad == 0, stop=quad == QUADS - 1, skip_group_check=True)
                        if quad == QUADS - 1:
                            mm.then_inc(pe_done, 1)
                if l < DEPTH - 1:
                    keep_awake(B("down", l, QUADS - 1, 1), AWAKE_LAYER)

        @block.scalar
        def _(act):
            steps = [0]
            reads = [0]

            def link(ins):
                steps[0] += 1
                ins.then_inc(act_step, 1)
                act.wait_ge(act_step, steps[0])

            def done(ins, *key):
                reads[0] += 1
                assert jobs[key][2:4] == ("act", reads[0]), key
                ins.then_inc(act_freed, 1)

            def rms(n, parts, width, signal):
                for src, junk, k in parts:
                    last = act.activation(junk, src, ACT.Square, accum_out=nst[:, n, k:k + 1])
                link(last)
                for a, b, w in width:
                    last = act.activation(nst[:, n + 1, a:b], nst[:, n, a:b], ACT.Ln, scale=1.0 / w, bias=epst[:, 0:1])
                link(last)
                k = width[-1][1]
                act.activation(nst[:, n + 2, 0:k], nst[:, n + 1, 0:k], ACT.Exp, scale=-0.5).then_inc(signal, 1)

            def norm_x(source, l):
                for t in range(TT):
                    first, second = (slice(0, D // 2), slice(D // 2, D))
                    if source:
                        wait_read(act, source, l, 2 * t)
                    else:
                        act.wait_ge(x_landed[t], 16)
                    link(act.activation(xn[:, t, first], xs[:, t, first], ACT.Square, accum_out=nst[:, 0, t:t + 1]))
                    act.activation(nst[:, 1, t:t + 1], nst[:, 0, t:t + 1], ACT.Identity, scale=1.0 / D, bias=epst[:, 0:1])
                    if source:
                        wait_read(act, source, l, 2 * t + 1)
                    link(act.activation(xn[:, t, second], xs[:, t, second], ACT.Square, accum_out=nst[:, 0, 2 + t:3 + t]))
                    link(act.activation(nst[:, 1, 2 + t:3 + t], nst[:, 0, 2 + t:3 + t], ACT.Ln, scale=1.0 / D, bias=nst[:, 1, t:t + 1]))
                    act.activation(nst[:, 2, t:t + 1], nst[:, 1, 2 + t:3 + t], ACT.Exp, scale=-0.5).then_inc(ss_ready, 1)

            def copy_pair(name, l, dst, scale=1.0):
                for j in range(2):
                    wait_pe(act, name, l, j)
                    done(act.activation(dst[:, 2 * j:2 * j + 2, :], B(name, l, j)[:, :], ACT.Copy, scale=scale), name, l, j)

            def turned(name, l, g):
                for t in range(TT):
                    wait_pe(act, name, l, 2 * t + 1)
                    for i in range(HC):
                        c = HC + i
                        ins = act.activation(hT[:, c, t * P:(t + 1) * P], B(name, l, 2 * t + 1)[:, i * P:(i + 1) * P], ACT.Copy,
                                             scale=gains[l][:, g, c:c + 1])
                    done(ins, name, l, 2 * t + 1)

            def gates(l, b, quarters=range(4)):
                for j in quarters:
                    n = gates_in_order.index((l, b, j))
                    wait_pe(act, "gate", l, b, j)
                    if n >= 2:
                        wait_merged(act, *gates_in_order[n - 2])
                    for bb in range(2):
                        c = 8 * b + 2 * j + bb
                        ins = act.activation(sig[:, n % 2, bb * T:(bb + 1) * T], B("gate", l, b, j)[:, bb * T:(bb + 1) * T],
                                             ACT.Exp, scale=-1.0, bias=nbg[l][:, c:c + 1])
                    done(ins, "gate", l, b, j)

            def further_blocks(l):
                act.wait_ge(flag_ready, l + 1)
                n_more = act.value_load(flag_i[0:1, l:l + 1], min_val=0, max_val=E * MORE)
                with act.If(n_more != 0):
                    with act.Fori(0, n_more, 1) as i:
                        act.wait_ge(o_gathered[l], i + 1)
                        act.activation(sS[0:SLOTS, :], bank[1][0:SLOTS, 0:T], ACT.Copy)
                        act.wait_ge(o_gu_done[l], i + 1)
                        act.activation(gus[:, :], bank[2][:, :], ACT.Copy).then_inc(o_gu_read[l], 1)
                        act.wait_ge(o_turned[l], i + 1)
                        act.activation(aT[:, :, 0, 0:SLOTS], bank[3][:, 0:FC * SLOTS].rearrange("p (c s) -> p c s", c=FC),
                                       ACT.Exp, scale=-1.0).then_inc(o_exp[l], 1)
                        act.wait_ge(o_down[l], i + 1)
                        for hh in range(2):
                            ins = act.activation(yS[0:SLOTS, hh * 512:(hh + 1) * 512], bank[hh][0:SLOTS, :], ACT.Copy)
                        ins.then_inc(o_y_ready[l], 1)

            act.preload_act_table_set("natural_log_exp_and_others")
            act.wait_ge(const_ready, 1)
            for l in range(DEPTH):
                norm_x("moe" if l else None, l - 1)
                act.wait_ge(gains_landed[l], 32)
                turned("tr", l, 0)
                if l == 0:
                    act.wait_ge(angles_ready, 2)
                    act.activation(sinn[:], ang[:, 0, :, :], ACT.Sin)
                    act.activation(cosn[:], ang[:, 1, :, :], ACT.Sin).then_inc(rope_ready, 1)
                    act.preload_act_table_set("natural_log_exp_and_others")
                copy_pair("qs", l, qsT, SBD ** -0.5)
                copy_pair("ks", l, ksT)
                for t in range(TT):
                    wait_pe(act, "lat", l, t)
                    done(act.activation(lat[:, t, :], B("lat", l, t)[:, 0:LAT], ACT.Copy), "lat", l, t)
                for j in range(6):
                    wait_pe(act, "z", l, j)
                    dst = z0[:, 2 * j:2 * j + 2, :] if j < 4 else z1[:, 4 * (j - 4):4 * (j - 3), :]
                    done(act.activation(dst, B("z", l, j)[:, :], ACT.Copy), "z", l, j)
                act.wait_ge(act_freed, jobs[("lat", l, 1)][3])
                rms(3, [(lat[:, t, c0:c1], latT.rearrange("p c n -> p (c n)")[:, TT * c0 + t * (c1 - c0):TT * c0 + (t + 1) * (c1 - c0)], 2 * i + t)
                        for i, (c0, c1) in enumerate(((0, QR), (QR, QR + KVR))) for t in range(TT)],
                    [(0, 2, QR), (2, 4, KVR)], lat_ss)
                act.wait_ge(z_abs, l + 1)
                act.activation(l0[:, :, :], l0[:, :, :], ACT.Exp)
                link(act.activation(l1[:, :, :], l1[:, :, :], ACT.Exp))
                act.activation(l0[:, :, :], l0[:, :, :], ACT.Ln, bias=1.0)
                act.activation(l1[:, :, :], l1[:, :, :], ACT.Ln, bias=1.0).then_inc(z_sp, 1)
                copy_pair("hc", l, hc)
                copy_pair("bg", l, bg)
                act.wait_ge(const_ready, 2 + l)
                wait_read(act, "cum", l, 5)
                act.activation(l0[:, :, :], z0[:, :, :], ACT.Exp).then_inc(a_ready, 1)
                act.activation(l1[:, :, :], z1[:, :, :], ACT.Exp).then_inc(a_ready, 1)
                gates(l, 0)
                for j in range(4):
                    t, hh = j // 2, j % 2
                    wait_pe(act, "q", l, j)
                    done(act.activation(qn[:, t, 4 * hh:4 * hh + 4, :], B("q", l, j)[:, 0:4 * QK], ACT.Copy), "q", l, j)
                for j in range(4):
                    t, hh = j // 2, j % 2
                    wait_pe(act, "kv", l, j)
                    ps = B("kv", l, j)[:, :].rearrange("p (h d) -> p h d", h=4)
                    act.activation(kn[:, t, 4 * hh:4 * hh + 4, 0:NOPE], ps[:, :, 0:NOPE], ACT.Copy)
                    dst = vn[:, t, hh * 256:(hh + 1) * 256].rearrange("p (h d) -> p h d", h=4)
                    done(act.activation(dst, ps[:, :, NOPE:], ACT.Copy), "kv", l, j)
                for j in range(4):
                    wait_pe(act, "qT", l, j)
                    done(act.activation(qT[0:QK, 2 * j:2 * j + 2, :], B("qT", l, j)[0:QK, :], ACT.Copy), "qT", l, j)
                copy_pair("pvs", l, osT)
                gates(l, 2, [0])
                act.wait_ge(ssub_ready, l + 1)
                act.activation(z1[:, :, :], z1[:, :, :], ACT.Exp)
                act.activation(z0[:, :, :], z0[:, :, :], ACT.Exp).then_inc(exp_ready, 1)
                gates(l, 2, range(1, 4))
                for j in (1, 3, 5):
                    turned_probs(act, l, j, done, wait_pe, B, pt0, pt1, "act")
                gates(l, 1, [0])
                copy_pair("pvm", l, omT)
                gates(l, 1, range(1, 4))

                norm_x("wo", l)
                turned("tr2", l, 1)
                act.wait_ge(rt_a, l + 1)
                act.activation(r4[:, 1, :, :], r4[:, 0, :, :], ACT.Exp)
                act.activation(r1[:, 3, :], r1[:, 2, :], ACT.Exp).then_inc(rt_b, 1)
                for quad in range(QUADS):
                    if quad == MIDDLE:
                        further_blocks(l)
                    wait_pe(act, "gather", l, quad, 1)
                    for cc in range(GD):
                        c = GD + cc
                        ins = act.activation(xe[:, c, :], B("gather", l, quad, 1)[:, cc * P:(cc + 1) * P], ACT.Copy,
                                             scale=gains[l][:, 1, c:c + 1])
                    done(ins, "gather", l, quad, 1)
                    wait_pe(act, "sT", l, quad)
                    done(act.activation(sS[:, :], B("sT", l, quad)[:, 0:T], ACT.Copy), "sT", l, quad)
                    wait_pe(act, "eg", l, quad)
                    done(act.activation(gus[:, 0:FE], B("eg", l, quad)[:, 0:FE], ACT.Copy), "eg", l, quad)
                    wait_pe(act, "egT", l, quad)
                    act.activation(aT[:, :, 0, :], B("egT", l, quad)[:, 0:FC * P], ACT.Exp,
                                   scale=-1.0).then_inc(eg_ready, 1)
                    wait_pe(act, "eu", l, quad)
                    done(act.activation(gus[:, FE:2 * FE], B("eu", l, quad)[:, 0:FE], ACT.Copy), "eu", l, quad)
                    wait_pe(act, "down", l, quad, 0)
                    done(act.activation(yS[:, 0:512], B("down", l, quad, 0)[:, :], ACT.Copy), "down", l, quad, 0)
            norm_x("moe", DEPTH - 1)

        @block.vector
        def _(dve):
            steps = [0]
            reads = [0]

            def link(ins):
                steps[0] += 1
                ins.then_inc(dve_step, 1)
                dve.wait_ge(dve_step, steps[0])

            def done(ins, *key):
                reads[0] += 1
                assert jobs[key][2:4] == ("dve", reads[0]), key
                ins.then_inc(dve_freed, 1)

            def newton(n, width):
                k = width[-1][1]
                for a, b, w in width:
                    last = dve.tensor_scalar(nst[:, n + 1, a:b], nst[:, n, a:b], 1.0 / w, EPS, ALU.mult, ALU.add)
                link(last)
                for _ in range(2):
                    link(dve.tensor_tensor(nst[:, n + 1, 0:k], nst[:, n + 1, 0:k], nst[:, n + 2, 0:k], ALU.mult))
                link(dve.tensor_scalar(nst[:, n + 1, 0:k], nst[:, n + 1, 0:k], -0.5, 1.5, ALU.mult, ALU.add))
                link(dve.tensor_tensor(nst[:, n + 2, 0:k], nst[:, n + 1, 0:k], nst[:, n + 2, 0:k], ALU.mult))

            def add_tile(source, l, t):
                for half in range(2):
                    wait_pe(dve, source, l, 2 * t + half)
                    m = xs[:, t, half * 512:(half + 1) * 512]
                    done(dve.tensor_tensor(m, m, B(source, l, 2 * t + half)[:, :], ALU.add), source, l, 2 * t + half)

            def estimate(n, t):
                dve.wait_ge(ss_ready, TT * n + t + 1)
                r, mean, correction = nst[:, 2, t:t + 1], nst[:, 2, 2 + t:3 + t], nst[:, 2, 4 + t:5 + t]
                link(dve.tensor_scalar(mean, nst[:, 0, 2 + t:3 + t], 1.0 / D, nst[:, 1, t:t + 1], ALU.mult, ALU.add))
                link(dve.scalar_tensor_tensor(out=correction, in0=mean, scalar=r, in1=r, op0=ALU.mult, op1=ALU.mult))
                link(dve.tensor_scalar(correction, correction, -0.5, 1.5, ALU.mult, ALU.add))
                return r, correction

            def norm_tile(n, t):
                r, correction = estimate(n, t)
                dve.tensor_scalar(xn[:, t, :].rearrange("q (c p) -> q p c", c=DC), xs[:, t, :].rearrange("q (p c) -> q p c", c=DC),
                                  r, correction, ALU.mult, ALU.mult).then_inc(xn_ready, 1)

            def turned(name, l, g, tiles=range(TT)):
                for t in tiles:
                    wait_pe(dve, name, l, 2 * t)
                    done(dve.tensor_tensor(hT[:, 0:HC, t * P:(t + 1) * P], B(name, l, 2 * t)[:, :].rearrange("p (c n) -> p c n", c=HC),
                                           gains[l][:, g, 0:HC].unsqueeze(2).to_broadcast([P, HC, P]), ALU.mult), name, l, 2 * t)

            def rotate(x1, x2, t, n):
                c = cosn[:, t, :].unsqueeze(1).to_broadcast([P, n, HALF])
                s = sinn[:, t, :].unsqueeze(1).to_broadcast([P, n, HALF])
                r = [rope_t[:, i, 0:n, :] for i in range(4)]
                dve.tensor_tensor(r[0], x1, c, ALU.mult)
                dve.tensor_tensor(r[1], x2, s, ALU.mult)
                dve.tensor_tensor(r[2], x2, c, ALU.mult)
                link(dve.tensor_tensor(r[3], x1, s, ALU.mult))
                dve.tensor_tensor(x1, r[0], r[1], ALU.subtract)
                last = dve.tensor_tensor(x2, r[2], r[3], ALU.add)
                return last

            def gated(l, b):
                for j in range(4):
                    s = sig[:, j % 2, :]
                    wait_read(dve, "gate", l, b, j)
                    link(dve.tensor_scalar(s, s, 1.0, None, ALU.add))
                    link(dve.reciprocal(s, s))
                    wait_pe(dve, "y", l, b, j)
                    m = merged[:, 2 * j:2 * j + 2, :]
                    y = B("y", l, b, j)[:, :]
                    sv = s.rearrange("p (a n) -> p a n", a=2)
                    yv = y.rearrange("p (a n) -> p a n", a=2)
                    if b == BRANCHES[0]:
                        done(dve.tensor_tensor(m, sv, yv, ALU.mult), "y", l, b, j)
                    else:
                        done(dve.tensor_tensor(sv, sv, yv, ALU.mult), "y", l, b, j)
                        dve.wait_ge(dve_freed, reads[0])
                        dve.tensor_tensor(m, m, sv, ALU.add).then_inc(added, 1)

            def choose(l, first):
                k = [0]

                def olink(ins):
                    k[0] += 1
                    ins.then_inc(o_step[l], 1)
                    dve.wait_ge(o_step[l], first + k[0] - 1)

                olink(dve.tensor_scalar(turn, turn, 1.0, None, ALU.add))
                olink(dve.tensor_scalar(o_eq[:, :, :], blk[:, :, :], turn[:, 0:1], None, ALU.is_equal))
                dve.tensor_reduce(o_sel, o_eq.rearrange("p b e -> p e b"), AX.X, ALU.add)
                olink(dve.tensor_tensor(blk_one[:, :, :], o_eq[:, :, :], o_first[:, :, :], ALU.mult))
                dve.tensor_reduce(o_num[:, 0:1], blk_one[:, :, :], AX.XY, ALU.add)
                olink(dve.tensor_tensor(o_eq[:, 0, :], o_sel, iot[:], ALU.mult))
                olink(dve.tensor_reduce(o_num[:, 1:2], o_eq[:, 0, :], AX.X, ALU.add))
                dve.tensor_copy(e_i[:], o_num[:, 1:2]).then_inc(o_chosen[l], 1)
                for q, src in enumerate((rk, comb)):
                    olink(dve.tensor_tensor(o_tmp[:, :, :], src[:, :, :], o_sel.unsqueeze(1).to_broadcast([P, TT, E]), ALU.mult))
                    olink(dve.tensor_reduce(o_rk[:, 2 * q:2 * q + 2], o_tmp[:, :, :], AX.X, ALU.add))
                olink(dve.tensor_scalar(o_rk[:, 0:2], o_rk[:, 0:2], o_num[:, 0:1], None, ALU.subtract))
                for t in range(TT):
                    ins = dve.tensor_scalar(o_P[:, t, :], iot1[:], o_rk[:, t:t + 1], None, ALU.is_equal)
                olink(ins)
                for t in range(TT):
                    ins = dve.tensor_scalar(o_PW[:, t, :], o_P[:, t, :], o_rk[:, 2 + t:3 + t], None, ALU.mult)
                ins.then_inc(o_slots[l], 1)
                assert k[0] == CHOICE_STEPS

            def further_blocks(l):
                n_more = dve.value_load(flag_i[0:1, l:l + 1], min_val=0, max_val=E * MORE)
                with dve.If(n_more != 0):
                    with dve.Fori(0, n_more, 1) as i:
                        k = [0]

                        def olink(ins):
                            k[0] += 1
                            ins.then_inc(o_step[l], 1)
                            dve.wait_ge(o_step[l], CHOICE_STEPS + (CHOICE_STEPS + 3) * i + k[0])

                        dve.wait_ge(o_gathered[l], i + 1)
                        dve.tensor_tensor(o_x[:, :, :], bank[0][:, 0:DC * SLOTS].rearrange("p (c s) -> p c s", c=DC),
                                          gains[l][:, 1, :].unsqueeze(2).to_broadcast([P, DC, SLOTS]), ALU.mult).then_inc(o_x_ready[l], 1)
                        dve.wait_ge(o_exp[l], i + 1)
                        a, act_out = (aT[:, :, j, 0:SLOTS] for j in range(2))
                        ps = bank[3][:, 0:2 * FC * SLOTS].rearrange("p (g c s) -> p g c s", g=2, c=FC)
                        olink(dve.tensor_scalar(a, a, 1.0, None, ALU.add))
                        olink(dve.reciprocal(a, a))
                        olink(dve.tensor_tensor(a, a, ps[:, 0, :, :], ALU.mult))
                        dve.tensor_tensor(act_out, a, ps[:, 1, :, :], ALU.mult).then_inc(o_act[l], 1)
                        dve.wait_ge(o_out[l], i + 1)
                        choose(l, CHOICE_STEPS + (CHOICE_STEPS + 3) * i + 3 + 1)

            def constants():
                dve.wait_ge(consts_made, CONSTS_N)
                dve.tensor_copy(before_h[:], before[:])
                dve.tensor_copy(ones_h[:], ones[:])
                dve.tensor_reduce(fold[:], ident[:, :].rearrange("p (j s) -> p s j", j=QE), AX.X, ALU.add).then_inc(fold_ready, 1)
                dve.wait_ge(iota_made, 1)
                link(dve.tensor_copy(iot[:], iot_i[:]))
                dve.tensor_scalar(iot1[:], iot[:], 1.0, None, ALU.add)
                dve.tensor_scalar(countdown[:], iot[:, 0:EPG], -1.0, float(EPG), ALU.mult, ALU.add)

            def rotary_angles():
                dve.wait_ge(once_landed, 32)
                link(dve.tensor_copy(posf[:], pos_i[:]))
                for t in range(TT):
                    last = dve.tensor_scalar(ang[:, 0, t, :], frq[:], posf[:, t:t + 1], None, ALU.mult)
                link(last)
                for i, shift in ((1, 0.25), (0, 0.0)):
                    k, a = ang2[:, i, :, :], ang[:, i, :, :]
                    link(dve.tensor_scalar(k, ang[:, 0, :, :], float(np.float32(1 / TWO_PI)), shift, ALU.mult, ALU.add))
                    link(dve.tensor_scalar(k, k, MAGIC, None, ALU.add))
                    link(dve.tensor_scalar(k, k, -MAGIC, None, ALU.add))
                    link(dve.scalar_tensor_tensor(out=a, in0=k, scalar=-C1, in1=ang[:, 0, :, :], op0=ALU.mult, op1=ALU.add))
                    link(dve.scalar_tensor_tensor(out=a, in0=k, scalar=-C2, in1=a, op0=ALU.mult, op1=ALU.add))
                    link(dve.scalar_tensor_tensor(out=a, in0=k, scalar=-C3, in1=a, op0=ALU.mult, op1=ALU.add))
                    link(dve.tensor_scalar(a, a, float(np.float32(np.pi / 2)) if i else 0.0, PI_LOW, ALU.add, ALU.min))
                    dve.tensor_scalar(a, a, -PI_LOW, None, ALU.max).then_inc(angles_ready, 1)
                    dve.wait_ge(angles_ready, 2 - i)

            dve.memset(epst[:], EPS)
            dve.memset(nst[:], 0.0).then_inc(const_ready, 1)
            dve.wait_ge(const_ready, 1)

            for l in range(DEPTH):
                if l:
                    for t in range(TT):
                        add_tile("moe", l - 1, t)
                for t in range(TT):
                    norm_tile(2 * l, t)
                dve.wait_ge(gains_landed[l], 32)
                turned("tr", l, 0)
                dve.wait_ge(small_landed[l], 16 * SMALL)
                dve.tensor_scalar(nbg[l][:], nbg[l][:], -1.0, None, ALU.mult).then_inc(const_ready, 1)
                if l == 0:
                    rotary_angles()
                    constants()
                for t in range(TT):
                    wait_pe(dve, "vs", l, t)
                    done(dve.tensor_copy(vs[:, t, :], B("vs", l, t)[:, :]), "vs", l, t)
                dve.tensor_scalar(hidden[:], before[:], -NEG, NEG, ALU.mult, ALU.add)
                wait_read(dve, "z", l, 5)
                dve.scalar_tensor_tensor(out=l0[:, :, :], in0=z0[:, :, :], scalar=-1.0, in1=z0[:, :, :], op0=ALU.mult, op1=ALU.min)
                dve.scalar_tensor_tensor(out=l1[:, :, :], in0=z1[:, :, :], scalar=-1.0, in1=z1[:, :, :], op0=ALU.mult, op1=ALU.min).then_inc(z_abs, 1)
                dve.wait_ge(lat_ss, l + 1)
                newton(3, [(0, 2, QR), (2, 4, KVR)])
                for t in range(TT):
                    dve.tensor_scalar(lat[:, t, 0:QR], lat[:, t, 0:QR], nst[:, 5, t:t + 1], None, ALU.mult)
                    last = dve.tensor_scalar(lat[:, t, QR:QR + KVR], lat[:, t, QR:QR + KVR], nst[:, 5, 2 + t:3 + t], None, ALU.mult)
                last.then_inc(lat_ready, 1)
                dve.wait_ge(z_sp, l + 1)
                dve.scalar_tensor_tensor(out=l0[:, :, :], in0=z0[:, :, :], scalar=0.0, in1=l0[:, :, :], op0=ALU.max, op1=ALU.add)
                link(dve.scalar_tensor_tensor(out=l1[:, :, :], in0=z1[:, :, :], scalar=0.0, in1=l1[:, :, :], op0=ALU.max, op1=ALU.add))
                keep = before[:, :].unsqueeze(1).to_broadcast([P, H, P])
                dve.scalar_tensor_tensor(out=l0[:, :, 0:P], in0=l0[:, :, 0:P], scalar=-1.0, in1=keep, op0=ALU.mult, op1=ALU.mult)
                dve.tensor_scalar(l0[:, :, P:T], l0[:, :, P:T], -1.0, None, ALU.mult)
                dve.scalar_tensor_tensor(out=l1[:, :, :], in0=l1[:, :, :], scalar=-1.0, in1=keep, op0=ALU.mult, op1=ALU.mult).then_inc(l_ready, 1)
                hide = hidden[:, :].unsqueeze(1).to_broadcast([P, H, P])
                dve.tensor_tensor(z0[:, :, 0:P], z0[:, :, 0:P], hide, ALU.add)
                link(dve.tensor_tensor(z1[:, :, :], z1[:, :, :], hide, ALU.add))
                for j in range(2):
                    wait_read(dve, "hc", l, j)
                    wait_pe(dve, "cg", l, j)
                    m = hc[:, 2 * j:2 * j + 2, :]
                    ins = dve.tensor_tensor(m, m, B("cg", l, j)[:, :].rearrange("p (a n) -> p a n", a=2), ALU.mult)
                    done(ins, "cg", l, j)
                for j in range(2):
                    wait_pe(dve, "latT", l, j)
                    for i, c in enumerate((0, 1) if j == 0 else (2,)):
                        ins = dve.tensor_scalar(latT[:, c, :], B("latT", l, j)[:, i * T:(i + 1) * T], lgain[l][:, c:c + 1], None, ALU.mult)
                    done(ins, "latT", l, j)
                wait_read(dve, "cg", l, 1)
                for c in range(CB):
                    last = dve.tensor_scalar(yc[:, c, :], hc[:, c, :], cw[l][:, 2, c:c + 1], None, ALU.mult)
                link(last)
                for k in (1, 0):
                    s = 2 - k
                    for c in range(CB):
                        last = dve.scalar_tensor_tensor(out=yc[:, c, s:T], in0=hc[:, c, 0:T - s], scalar=cw[l][:, k, c:c + 1],
                                                        in1=yc[:, c, s:T], op0=ALU.mult, op1=ALU.add)
                    link(last)
                wait_read(dve, "bg", l, 1)
                dve.tensor_tensor(yc[:, :, :], yc[:, :, :], bg[:, :, :], ALU.mult).then_inc(conv_ready, 1)
                if l == 0:
                    dve.wait_ge(rope_ready, 1)
                for t in range(TT):
                    kr0 = lat[:, t, QR + KVR:LAT].rearrange("p (a n) -> p a n", a=2)
                    link(rotate(kr0[:, 0:1, :], kr0[:, 1:2, :], t, 1))
                for j in range(6):
                    wait_pe(dve, "cum", l, j)
                    m = z0[:, 2 * j:2 * j + 2, :] if j < 4 else z1[:, 4 * (j - 4):4 * (j - 3), :]
                    ins = dve.tensor_tensor(m, m, B("cum", l, j)[:, :].rearrange("p (a n) -> p a n", a=2 if j < 4 else 4), ALU.add)
                    done(ins, "cum", l, j)
                gated(l, 0)
                wait_read(dve, "q", l, 3)
                for t in range(TT):
                    last = rotate(qn[:, t, :, NOPE:NOPE + HALF], qn[:, t, :, NOPE + HALF:QK], t, H)
                    last.then_inc(rope_q, 1)
                    dve.wait_ge(rope_q, TT * l + t + 1)
                wait_read(dve, "kv", l, 3)
                for t in range(TT):
                    last = dve.tensor_copy(kn[:, t, :, NOPE:QK], lat[:, t, QR + KVR:LAT].unsqueeze(1).to_broadcast([P, H, ROPE]))
                last.then_inc(rope_k, 1)
                for j in range(4):
                    wait_pe(dve, "kT", l, j)
                    done(dve.tensor_copy(kT[0:QK, 2 * j:2 * j + 2, :], B("kT", l, j)[0:QK, :].rearrange("p (a n) -> p a n", a=2)), "kT", l, j)
                scale = QK ** -0.5
                link(dve.tensor_scalar(hidden[:], low[:], -NEG, NEG, ALU.mult, ALU.add))
                for j in range(6):
                    wait_pe(dve, "s", l, j)
                    per, nk = (4, P) if j < 2 else (2, T)
                    ps = B("s", l, j)[:, :].rearrange("p (h k) -> p h k", h=per)
                    dst = z1[:, 4 * j:4 * j + 4, :] if j < 2 else z0[:, 2 * (j - 2):2 * (j - 1), :]
                    if j >= 2:
                        dve.tensor_scalar(dst[:, :, 0:P], ps[:, :, 0:P], scale, None, ALU.mult)
                    done(dve.scalar_tensor_tensor(out=dst[:, :, nk - P:nk], in0=ps[:, :, nk - P:nk], scalar=scale,
                                                  in1=hidden[:, :].unsqueeze(1).to_broadcast([P, per, P]),
                                                  op0=ALU.mult, op1=ALU.add), "s", l, j)
                dve.wait_ge(dve_freed, reads[0])
                mx = rope_t[:, 0, :, 0:2]
                dve.tensor_reduce(mx[:, :, 0:1], z1[:, :, :], AX.X, ALU.max)
                link(dve.tensor_reduce(mx[:, :, 1:2], z0[:, :, :], AX.X, ALU.max))
                dve.tensor_tensor(z1[:, :, :], z1[:, :, :], mx[:, :, 0:1].to_broadcast([P, H, P]), ALU.subtract)
                dve.tensor_tensor(z0[:, :, :], z0[:, :, :], mx[:, :, 1:2].to_broadcast([P, H, T]), ALU.subtract).then_inc(ssub_ready, 1)
                dve.wait_ge(exp_ready, l + 1)
                dve.tensor_reduce(mx[:, :, 0:1], z1[:, :, :], AX.X, ALU.add)
                link(dve.tensor_reduce(mx[:, :, 1:2], z0[:, :, :], AX.X, ALU.add))
                link(dve.reciprocal(rope_t[:, 1, :, 0:2], mx))
                rc = rope_t[:, 1, :, :]
                dve.tensor_tensor(z1[:, :, :], z1[:, :, :], rc[:, :, 0:1].to_broadcast([P, H, P]), ALU.mult)
                dve.tensor_tensor(z0[:, :, :], z0[:, :, :], rc[:, :, 1:2].to_broadcast([P, H, T]), ALU.mult).then_inc(pn_ready, 1)
                gated(l, 2)
                for j in (0, 2, 4):
                    turned_probs(dve, l, j, done, wait_pe, B, pt0, pt1, "dve")
                gated(l, 1)

                add_tile("wo", l, 0)
                norm_tile(2 * l + 1, 0)
                add_tile("wo", l, 1)
                turned("tr2", l, 1, [0])
                norm_tile(2 * l + 1, 1)
                turned("tr2", l, 1, [1])
                for t in range(TT):
                    wait_pe(dve, "routeT", l, t)
                    done(dve.tensor_copy(lgT[0:NG + E, t * P:(t + 1) * P], B("routeT", l, t)[0:NG + E, 0:P]), "routeT", l, t)
                wait_pe(dve, "route", l)
                done(dve.tensor_tensor(lg[:, :, :], B("route", l)[:, 0:TT * 64].rearrange("p (t n) -> p t n", t=TT)[:, :, 0:NG + E],
                                       rbias[l][:, :].unsqueeze(1).to_broadcast([P, TT, NG + E]), ALU.add), "route", l)
                dve.wait_ge(dve_freed, reads[0])

                def bc(a, n):
                    return a.unsqueeze(2).to_broadcast([P, TT, n])

                def down_from(n):
                    return countdown[:, 0:n].unsqueeze(1).to_broadcast([P, TT, n])

                def first_top(dst, less, n, tmp, top):
                    link(dve.scalar_tensor_tensor(out=tmp, in0=less, scalar=0.0, in1=down_from(n), op0=ALU.is_equal, op1=ALU.mult))
                    link(dve.tensor_reduce(top, tmp, AX.X, ALU.max))
                    link(dve.tensor_tensor(dst, tmp, bc(top, n), ALU.is_equal))

                def by_group(src, dst):
                    return dve.tensor_tensor(dst.rearrange("p t (g e) -> p t g e", g=NG), src.unsqueeze(2).to_broadcast([P, TT, NG, EPG]),
                                             group.unsqueeze(3).to_broadcast([P, TT, NG, EPG]), ALU.mult)

                group_less, group_exp, group, group_tmp = (r4[:, i, :, :] for i in range(4))
                chosen, less, first, tmp, rest, second, both, pair, weight = (r8[:, i, :, :] for i in range(9))
                top_group, top, gap, gap_exp, denom, norm, recip, mark_at = (r1[:, i, :] for i in range(8))
                link(dve.tensor_reduce(top_group, lg[:, :, 0:NG], AX.X, ALU.max))
                link(dve.tensor_tensor(group_less, lg[:, :, 0:NG], bc(top_group, NG), ALU.subtract))
                first_top(group, group_less, NG, group_tmp, mark_at)
                link(dve.tensor_tensor(comb[:, :, :].rearrange("p t (g e) -> p t g e", g=NG),
                                       lg[:, :, NG:].rearrange("p t (g e) -> p t g e", g=NG),
                                       group.unsqueeze(3).to_broadcast([P, TT, NG, EPG]), ALU.mult))
                link(dve.tensor_reduce(chosen, comb[:, :, :].rearrange("p t (g e) -> p t e g", g=NG), AX.X, ALU.add))
                link(dve.tensor_reduce(top, chosen, AX.X, ALU.max))
                link(dve.tensor_tensor(less, chosen, bc(top, EPG), ALU.subtract))
                first_top(first, less, EPG, tmp, mark_at)
                link(dve.scalar_tensor_tensor(out=rest, in0=first, scalar=NEG, in1=less, op0=ALU.mult, op1=ALU.add))
                dve.tensor_reduce(gap, rest, AX.X, ALU.max).then_inc(rt_a, 1)
                dve.wait_ge(rt_a, l + 1)
                link(dve.tensor_tensor(tmp, rest, bc(gap, EPG), ALU.is_equal))
                link(dve.tensor_tensor(tmp, tmp, down_from(EPG), ALU.mult))
                link(dve.tensor_reduce(mark_at, tmp, AX.X, ALU.max))
                link(dve.tensor_tensor(second, tmp, bc(mark_at, EPG), ALU.is_equal))
                link(dve.tensor_tensor(both, first, second, ALU.add))
                by_group(both, member[:, :, :]).then_inc(member_ready, 1)
                wait_pe(dve, "rank", l)
                link(dve.scalar_tensor_tensor(out=rk[:, :, :], in0=B("rank", l)[:, 0:TT * E].rearrange("p (t n) -> p t n", t=TT),
                                              scalar=1.0, in1=member[:, :, :], op0=ALU.add, op1=ALU.mult))

                def slots_of(a, b):
                    for t in range(TT):
                        yield dve.tensor_tensor(Ps[:, t, a:b, :], iot1[:, :].unsqueeze(1).to_broadcast([P, b - a, SLOTS]),
                                                rk[:, t, a:b].unsqueeze(2).to_broadcast([P, b - a, SLOTS]), ALU.is_equal)

                for ins in slots_of(0, QE):
                    last = ins
                last.then_inc(p_ready, 1)
                dve.wait_ge(rt_b, l + 1)
                dve.tensor_reduce(denom, group_exp, AX.X, ALU.add)
                link(dve.tensor_tensor(pair, second, bc(gap_exp, EPG), ALU.mult))
                link(dve.scalar_tensor_tensor(out=norm, in0=gap_exp, scalar=1.0, in1=denom, op0=ALU.add, op1=ALU.mult))
                dve.tensor_tensor(pair, pair, first, ALU.add)
                link(dve.reciprocal(recip, norm))
                link(dve.tensor_tensor(weight, pair, bc(recip, EPG), ALU.mult))
                by_group(weight, comb[:, :, :]).then_inc(p_ready, 1)
                for ins in slots_of(QE, E):
                    ins.then_inc(p_ready, 1)
                done(dve.tensor_copy(count, B("rank", l)[:, TT * E:TT * E + E]), "rank", l)

                def queue_blocks():
                    dve.wait_ge(dve_freed, jobs[("rank", l)][3])
                    for b in range(MORE):
                        dve.tensor_scalar(blk_one[:, b, :], count, float(SLOTS * (b + 1)), None, ALU.is_gt)
                        last = dve.memset(o_first[:, b, :], float(SLOTS * (b + 1)))
                    link(last)
                    flat = [a.rearrange("p b e -> p (b e)") for a in (blk_one, blk)]
                    link(dve.tensor_tensor_scan(flat[1], ones_row, flat[0], 0.0, ALU.mult, ALU.add))
                    dve.tensor_copy(flag_i[:, l:l + 1], flat[1][:, MORE * E - 1:MORE * E]).then_inc(flag_ready, 1)
                    link(dve.tensor_tensor(o_eq[:, :, :], blk[:, :, :], blk_one[:, :, :], ALU.mult))
                    dve.tensor_copy(blk[:, :, :], o_eq[:, :, :])
                    link(dve.memset(turn, 0.0))
                    choose(l, 1)

                for quad in range(QUADS):
                    if quad == MIDDLE:
                        further_blocks(l)
                    wait_pe(dve, "gather", l, quad, 0)
                    done(dve.tensor_tensor(xe[:, 0:GD, :], B("gather", l, quad, 0)[:, :].rearrange("p (c s) -> p c s", c=GD),
                                           gains[l][:, 1, 0:GD].unsqueeze(2).to_broadcast([P, GD, P]), ALU.mult), "gather", l, quad, 0)
                    a, act_out = (aT[:, :, j, :] for j in range(2))
                    gate_p, up_p = (B(name, l, quad)[:, 0:FC * P].rearrange("p (c s) -> p c s", c=FC) for name in ("egT", "euT"))
                    dve.wait_ge(eg_ready, QUADS * l + quad + 1)
                    link(dve.tensor_scalar(a, a, 1.0, None, ALU.add))
                    link(dve.reciprocal(a, a))
                    done(dve.tensor_tensor(a, a, gate_p, ALU.mult), "egT", l, quad)
                    wait_pe(dve, "euT", l, quad)
                    dve.wait_ge(dve_freed, reads[0])
                    done(dve.tensor_tensor(act_out, a, up_p, ALU.mult), "euT", l, quad)
                    if quad == 0:
                        queue_blocks()
                    wait_pe(dve, "down", l, quad, 1)
                    done(dve.tensor_copy(yS[:, 512:D], B("down", l, quad, 1)[:, :]), "down", l, quad, 1)

            for t in range(TT):
                add_tile("moe", DEPTH - 1, t)
            for t in range(TT):
                r, correction = estimate(2 * DEPTH, t)
                link(dve.tensor_tensor(nst[:, 3, t:t + 1], r, correction, ALU.mult))
                if t == 0:
                    dve.wait_ge(final_landed, 16)
                dve.scalar_tensor_tensor(out=xs[:, t, :], in0=xs[:, t, :], scalar=nst[:, 3, t:t + 1], in1=fgain,
                                         op0=ALU.mult, op1=ALU.mult).then_inc(xn_ready, 1)




def kernel(**inputs):
    import concourse.bacc as bacc
    from concourse.bass_utils import run_bass_kernel_spmd

    nc = bacc.Bacc("TRN2", target_bir_lowering=False, num_devices=1)
    arrays, aps = {}, {}
    for name in INS:
        a = np.ascontiguousarray(inputs[name])
        arrays[f"in_{name}"] = a
        aps[name] = nc.dram_tensor(f"in_{name}", a.shape, mybir.dt.from_np(a.dtype), kind="ExternalInput").ap()
    freqs = (np.float32(10000.0) ** (-np.arange(HALF, dtype=np.float32) / np.float32(HALF))).astype(np.float32)
    arrays["in_freqs"] = freqs
    freqs_d = nc.dram_tensor("in_freqs", freqs.shape, F32, kind="ExternalInput").ap()
    out_d = nc.dram_tensor("out_x", (1, T, D), F32, kind="ExternalOutput").ap()
    build(nc, aps, freqs_d, out_d)
    r = run_bass_kernel_spmd(nc, [arrays], core_ids=[0])
    return r.results[0]["out_x"]
```
